# Optimizing a Trainium2 kernel written in Bass

```python
import math
import jax
import jax.numpy as jnp
from jax import lax
import numpy as np

D_MODEL = 1024
BATCH = 1
SEQ = 1024
DEPTH = 1

HEAD_DIM = 64
NSA_HEADS = 8
NSA_KV_GROUPS = 2
CMP_BLOCK = 32
CMP_STRIDE = 16
CMP_HIDDEN = 256
SLC_BLOCK = 64
SLC_TOPK = 16
WINDOW = 512
FOX_HEADS = 4
DIFF_HEADS = 4
DIFF_QK_DIM = HEAD_DIM // 2
N_GROUPS = 4
EXPERTS_PER_GROUP = 8
N_EXPERTS = N_GROUPS * EXPERTS_PER_GROUP
TOPK_IN_GROUP = 2
D_EXPERT = 256
Q_BLOCK = 128
SLC_Q_BLOCK = 64
RMS_EPS = 1e-6
NEG_INF = -1e30
FORCE_SCORE = 1e4

NSA_Q = NSA_HEADS * HEAD_DIM
NSA_KV = NSA_KV_GROUPS * HEAD_DIM
NSA_GATE = NSA_HEADS * 3
FOX_W = FOX_HEADS * HEAD_DIM
DIFF_W = DIFF_HEADS * HEAD_DIM
MIX_WIDTH = NSA_Q + FOX_W + DIFF_W
IN_WIDTHS = (NSA_Q, NSA_KV, NSA_KV, NSA_KV, NSA_KV, NSA_KV, NSA_KV, NSA_GATE,
             FOX_W, FOX_W, FOX_W, FOX_HEADS, DIFF_W, DIFF_W, DIFF_W)
D_IN = sum(IN_WIDTHS)

kernel_name = "hybrid_nsa_fox_diff_hmoe"

def _rmsnorm(x, g):
    xf = x.astype(jnp.float32)
    y = xf * lax.rsqrt(jnp.mean(xf * xf, axis=-1, keepdims=True) + RMS_EPS)
    return (y * g.astype(jnp.float32)).astype(x.dtype)

def _masked_softmax(logits, mask):
    logits = jnp.where(mask, logits.astype(jnp.float32), NEG_INF)
    return jnp.where(mask, jax.nn.softmax(logits, axis=-1), 0.0)

def _alibi_slopes(n):
    return jnp.asarray(2.0 ** (-8.0 * np.arange(1, n + 1) / n), dtype=jnp.float32)

def _lambda_init(layer):
    return 0.8 - 0.6 * math.exp(-0.3 * layer)

def _nsa_mixer(q, kc, vc, ks, vs, kw, vw, gate_logits,
               cmp_k_pe, cmp_k_w1, cmp_k_w2, cmp_v_pe, cmp_v_w1, cmp_v_w2):
    B, T, _ = q.shape
    G, HG, HD = NSA_KV_GROUPS, NSA_HEADS // NSA_KV_GROUPS, HEAD_DIM
    scale = HD ** -0.5
    slopes = _alibi_slopes(NSA_HEADS).reshape(G, HG)[:, :, None, None]
    qh = q.reshape(B, T, G, HG, HD).transpose(0, 2, 3, 1, 4)

    def kvh(a):
        return a.reshape(B, T, G, HD).transpose(0, 2, 1, 3)

    kc, vc, ks, vs, kw, vw = (kvh(a) for a in (kc, vc, ks, vs, kw, vw))
    pos = jnp.arange(T)

    n_cmp = (T - CMP_BLOCK) // CMP_STRIDE + 1
    tok = np.arange(n_cmp)[:, None] * CMP_STRIDE + np.arange(CMP_BLOCK)[None, :]

    def compress(a, pe, w1, w2):
        blk = (a[:, :, tok, :] + pe).reshape(B, G, n_cmp, CMP_BLOCK * HD)
        return jax.nn.gelu(blk @ w1) @ w2

    k_cmp = compress(kc, cmp_k_pe, cmp_k_w1, cmp_k_w2)
    v_cmp = compress(vc, cmp_v_pe, cmp_v_w1, cmp_v_w2)
    cmp_end = jnp.arange(n_cmp) * CMP_STRIDE + CMP_BLOCK - 1
    dist_c = (pos[:, None] - cmp_end[None, :]).astype(jnp.float32)
    s_cmp = jnp.einsum('bghtd,bgcd->bghtc', qh, k_cmp) * scale - slopes * dist_c
    p_cmp = _masked_softmax(s_cmp, dist_c >= 0)
    o_cmp = jnp.einsum('bghtc,bgcd->bghtd', p_cmp.astype(v_cmp.dtype), v_cmp)

    n_sel = T // SLC_BLOCK
    top_n = min(SLC_TOPK, n_sel)
    c_start = np.arange(n_cmp) * CMP_STRIDE
    s_start = np.arange(n_sel) * SLC_BLOCK
    overlap = np.clip(np.minimum(c_start[:, None] + CMP_BLOCK, s_start[None, :] + SLC_BLOCK)
                      - np.maximum(c_start[:, None], s_start[None, :]), 0, None) / CMP_BLOCK
    overlap = jnp.asarray(overlap, dtype=jnp.float32)
    imp = jnp.einsum('bghtc,cj->bgtj', p_cmp, overlap)
    cur = pos // SLC_BLOCK
    j = jnp.arange(n_sel)
    valid = j[None, :] <= cur[:, None]
    forced = (j[None, :] == 0) | (j[None, :] == cur[:, None]) | (j[None, :] == cur[:, None] - 1)
    imp = jnp.where(valid, jnp.where(forced, FORCE_SCORE, imp), NEG_INF)
    _, sel_idx = lax.top_k(imp, top_n)

    ks_b = ks.reshape(B, G, n_sel, SLC_BLOCK, HD)
    vs_b = vs.reshape(B, G, n_sel, SLC_BLOCK, HD)
    nq = T // SLC_Q_BLOCK
    q_chunks = qh.reshape(B, G, HG, nq, SLC_Q_BLOCK, HD).transpose(3, 0, 1, 2, 4, 5)
    idx_chunks = sel_idx.reshape(B, G, nq, SLC_Q_BLOCK, top_n).transpose(2, 0, 1, 3, 4)
    pos_chunks = pos.reshape(nq, SLC_Q_BLOCK)
    b_ix = jnp.arange(B)[:, None, None, None]
    g_ix = jnp.arange(G)[None, :, None, None]
    n_keys = top_n * SLC_BLOCK

    def slc_block(args):
        qc, ic, pc = args
        k_sel = ks_b[b_ix, g_ix, ic].reshape(B, G, SLC_Q_BLOCK, n_keys, HD)
        v_sel = vs_b[b_ix, g_ix, ic].reshape(B, G, SLC_Q_BLOCK, n_keys, HD)
        kpos = (ic[..., None] * SLC_BLOCK + jnp.arange(SLC_BLOCK)).reshape(B, G, SLC_Q_BLOCK, n_keys)
        dist = (pc[:, None] - kpos).astype(jnp.float32)[:, :, None]
        s = jnp.einsum('bghqd,bgqkd->bghqk', qc, k_sel) * scale - slopes * dist
        p = _masked_softmax(s, dist >= 0)
        return jnp.einsum('bghqk,bgqkd->bghqd', p.astype(v_sel.dtype), v_sel)

    o_slc = lax.map(slc_block, (q_chunks, idx_chunks, pos_chunks))
    o_slc = o_slc.transpose(1, 2, 3, 0, 4, 5).reshape(B, G, HG, T, HD)

    nb = T // Q_BLOCK
    span = WINDOW + Q_BLOCK
    kw_p = jnp.pad(kw, ((0, 0), (0, 0), (WINDOW, 0), (0, 0)))
    vw_p = jnp.pad(vw, ((0, 0), (0, 0), (WINDOW, 0), (0, 0)))
    q_blocks = qh.reshape(B, G, HG, nb, Q_BLOCK, HD).transpose(3, 0, 1, 2, 4, 5)

    def win_block(args):
        qb, i = args
        start = i * Q_BLOCK
        kb = lax.dynamic_slice_in_dim(kw_p, start, span, axis=2)
        vb = lax.dynamic_slice_in_dim(vw_p, start, span, axis=2)
        qpos = start + jnp.arange(Q_BLOCK)
        kpos = start - WINDOW + jnp.arange(span)
        dist = (qpos[:, None] - kpos[None, :]).astype(jnp.float32)
        mask = (dist >= 0) & (dist < WINDOW) & (kpos[None, :] >= 0)
        s = jnp.einsum('bghqd,bgkd->bghqk', qb, kb) * scale - slopes * dist
        p = _masked_softmax(s, mask)
        return jnp.einsum('bghqk,bgkd->bghqd', p.astype(vb.dtype), vb)

    o_win = lax.map(win_block, (q_blocks, jnp.arange(nb)))
    o_win = o_win.transpose(1, 2, 3, 0, 4, 5).reshape(B, G, HG, T, HD)

    gates = jax.nn.sigmoid(gate_logits).reshape(B, T, G, HG, 3).transpose(0, 2, 3, 1, 4)
    o = gates[..., 0:1] * o_cmp + gates[..., 1:2] * o_slc + gates[..., 2:3] * o_win
    return o.transpose(0, 3, 1, 2, 4).reshape(B, T, NSA_Q)

def _fox_mixer(q, k, v, f_logit):
    B, T, _ = q.shape
    H, HD = FOX_HEADS, HEAD_DIM
    scale = HD ** -0.5
    qh = q.reshape(B, T, H, HD).transpose(0, 2, 1, 3)
    kh = k.reshape(B, T, H, HD).transpose(0, 2, 1, 3)
    vh = v.reshape(B, T, H, HD).transpose(0, 2, 1, 3)
    log_f = jax.nn.log_sigmoid(f_logit.astype(jnp.float32)).transpose(0, 2, 1)
    cum = jnp.cumsum(log_f, axis=-1)
    nb = T // Q_BLOCK
    q_blocks = qh.reshape(B, H, nb, Q_BLOCK, HD).transpose(2, 0, 1, 3, 4)
    c_blocks = cum.reshape(B, H, nb, Q_BLOCK).transpose(2, 0, 1, 3)
    pos_blocks = jnp.arange(T).reshape(nb, Q_BLOCK)
    kpos = jnp.arange(T)

    def blk(args):
        qb, cb, pb = args
        s = jnp.einsum('bhqd,bhkd->bhqk', qb, kh) * scale + (cb[..., None] - cum[:, :, None, :])
        p = _masked_softmax(s, pb[:, None] >= kpos[None, :])
        return jnp.einsum('bhqk,bhkd->bhqd', p.astype(vh.dtype), vh)

    o = lax.map(blk, (q_blocks, c_blocks, pos_blocks))
    return o.transpose(1, 0, 3, 2, 4).reshape(B, T, FOX_W)

def _diff_mixer(q, k, v, lam, subln, lambda_init):
    B, T, _ = q.shape
    H, d, HD = DIFF_HEADS, DIFF_QK_DIM, HEAD_DIM
    scale = d ** -0.5
    qh = q.reshape(B, T, H, 2, d).transpose(0, 2, 3, 1, 4)
    kh = k.reshape(B, T, H, 2, d).transpose(0, 2, 3, 1, 4)
    vh = v.reshape(B, T, H, HD).transpose(0, 2, 1, 3)
    lam_f = lam.astype(jnp.float32)
    lam_full = jnp.exp(jnp.sum(lam_f[0] * lam_f[1])) - jnp.exp(jnp.sum(lam_f[2] * lam_f[3])) + lambda_init
    slopes = _alibi_slopes(H)[:, None, None, None]
    nb = T // Q_BLOCK
    q_blocks = qh.reshape(B, H, 2, nb, Q_BLOCK, d).transpose(3, 0, 1, 2, 4, 5)
    pos_blocks = jnp.arange(T).reshape(nb, Q_BLOCK)
    kpos = jnp.arange(T)

    def blk(args):
        qb, pb = args
        dist = (pb[:, None] - kpos[None, :]).astype(jnp.float32)
        s = jnp.einsum('bhiqd,bhikd->bhiqk', qb, kh) * scale - slopes * dist
        p = _masked_softmax(s, dist >= 0)
        attn = p[:, :, 0] - lam_full * p[:, :, 1]
        return jnp.einsum('bhqk,bhkd->bhqd', attn.astype(vh.dtype), vh)

    o = lax.map(blk, (q_blocks, pos_blocks))
    o = o.transpose(1, 0, 3, 2, 4).reshape(B, T, H, HD)
    o = _rmsnorm(o, subln) * (1.0 - lambda_init)
    return o.reshape(B, T, DIFF_W)

def _hier_moe(h, w_grp, b_grp, w_exp, b_exp, w_e_gate, w_e_up, w_e_down):
    B, T, D = h.shape
    hf = h.reshape(B * T, D)
    n = hf.shape[0]
    rows = jnp.arange(n)
    grp_logits = (hf @ w_grp).astype(jnp.float32) + b_grp.astype(jnp.float32)
    grp_prob = jax.nn.softmax(grp_logits, axis=-1)
    grp = jnp.argmax(grp_logits, axis=-1)
    grp_gate = grp_prob[rows, grp][:, None]
    exp_logits = ((hf @ w_exp).astype(jnp.float32) + b_exp.astype(jnp.float32)).reshape(n, N_GROUPS, EXPERTS_PER_GROUP)
    in_grp = exp_logits[rows, grp]
    top_val, top_idx = lax.top_k(in_grp, TOPK_IN_GROUP)
    w_top = jax.nn.softmax(top_val, axis=-1) * grp_gate
    eid = grp[:, None] * EXPERTS_PER_GROUP + top_idx
    gate = jnp.sum(jax.nn.one_hot(eid, N_EXPERTS, dtype=jnp.float32) * w_top[..., None], axis=1)
    gate = gate.astype(hf.dtype)
    out = jnp.zeros_like(hf)
    for e in range(N_EXPERTS):
        a = hf @ w_e_gate[e]
        u = hf @ w_e_up[e]
        out = out + (jax.nn.silu(a) * u * gate[:, e:e + 1]) @ w_e_down[e]
    return out.reshape(B, T, D)

def setup_inputs(seed: int = 0) -> dict:
    key = jax.random.key(seed)
    ks = jax.random.split(key, 24)
    L, D = DEPTH, D_MODEL

    def nrm(k, shape, fan_in):
        return jax.random.normal(k, shape, jnp.float32) * fan_in ** -0.5

    def small(k, shape, s):
        return s * jax.random.normal(k, shape, jnp.float32)

    return {
        'x': jax.random.normal(ks[0], (BATCH, SEQ, D), jnp.float32),
        'norm_attn': 1.0 + small(ks[1], (L, D), 0.02),
        'w_in': nrm(ks[2], (L, D, D_IN), D),
        'b_gate': small(ks[3], (L, NSA_GATE), 0.02),
        'b_fgt': 2.0 + 2.0 * jax.random.uniform(ks[4], (L, FOX_HEADS), jnp.float32),
        'cmp_k_pe': small(ks[5], (L, CMP_BLOCK, HEAD_DIM), 0.1),
        'cmp_k_w1': nrm(ks[6], (L, CMP_BLOCK * HEAD_DIM, CMP_HIDDEN), CMP_BLOCK * HEAD_DIM),
        'cmp_k_w2': nrm(ks[7], (L, CMP_HIDDEN, HEAD_DIM), CMP_HIDDEN),
        'cmp_v_pe': small(ks[8], (L, CMP_BLOCK, HEAD_DIM), 0.1),
        'cmp_v_w1': nrm(ks[9], (L, CMP_BLOCK * HEAD_DIM, CMP_HIDDEN), CMP_BLOCK * HEAD_DIM),
        'cmp_v_w2': nrm(ks[10], (L, CMP_HIDDEN, HEAD_DIM), CMP_HIDDEN),
        'diff_lambda': small(ks[11], (L, 4, DIFF_QK_DIM), 0.1),
        'diff_subln': 1.0 + small(ks[12], (L, HEAD_DIM), 0.02),
        'w_out': nrm(ks[13], (L, MIX_WIDTH, D), MIX_WIDTH),
        'norm_ffn': 1.0 + small(ks[14], (L, D), 0.02),
        'w_grp': nrm(ks[15], (L, D, N_GROUPS), D),
        'b_grp': small(ks[16], (L, N_GROUPS), 0.01),
        'w_exp': nrm(ks[17], (L, D, N_EXPERTS), D),
        'b_exp': small(ks[18], (L, N_EXPERTS), 0.01),
        'w_e_gate': nrm(ks[19], (L, N_EXPERTS, D, D_EXPERT), D),
        'w_e_up': nrm(ks[20], (L, N_EXPERTS, D, D_EXPERT), D),
        'w_e_down': nrm(ks[21], (L, N_EXPERTS, D_EXPERT, D), D_EXPERT),
        'norm_final': 1.0 + small(ks[22], (D,), 0.02),
    }

def reference(x, norm_attn, w_in, b_gate, b_fgt, cmp_k_pe, cmp_k_w1, cmp_k_w2,
              cmp_v_pe, cmp_v_w1, cmp_v_w2, diff_lambda, diff_subln, w_out,
              norm_ffn, w_grp, b_grp, w_exp, b_exp, w_e_gate, w_e_up, w_e_down,
              norm_final):
    splits = [int(s) for s in np.cumsum(IN_WIDTHS)[:-1]]
    for l in range(DEPTH):
        h = _rmsnorm(x, norm_attn[l])
        proj = h @ w_in[l]
        (nsa_q, kc, vc, ks_, vs_, kw, vw, nsa_g,
         fq, fk, fv, ff, dq, dk, dv) = jnp.split(proj, splits, axis=-1)
        o_a = _nsa_mixer(nsa_q, kc, vc, ks_, vs_, kw, vw, nsa_g + b_gate[l],
                         cmp_k_pe[l], cmp_k_w1[l], cmp_k_w2[l],
                         cmp_v_pe[l], cmp_v_w1[l], cmp_v_w2[l])
        o_b = _fox_mixer(fq, fk, fv, ff + b_fgt[l])
        o_c = _diff_mixer(dq, dk, dv, diff_lambda[l], diff_subln[l], _lambda_init(l))
        x = x + jnp.concatenate([o_a, o_b, o_c], axis=-1) @ w_out[l]
        x = x + _hier_moe(_rmsnorm(x, norm_ffn[l]), w_grp[l], b_grp[l], w_exp[l], b_exp[l],
                          w_e_gate[l], w_e_up[l], w_e_down[l])
    return _rmsnorm(x, norm_final)


_drawn_inputs = setup_inputs


def setup_inputs(seed=0):
    import zlib

    import numpy as np

    out = dict(_drawn_inputs(seed))
    spreads = {}
    factors = {'b_gate': 26.283,
     'cmp_k_pe': 25.965,
     'diff_subln': 3.643,
     'b_grp': 19.354,
     'b_exp': 11.136,
     'norm_final': 7.982,
     'b_fgt': 3.186,
     'cmp_v_pe': 3.623,
     'norm_ffn': 3.685}
    for name, (base, spread) in spreads.items():
        noise = np.random.default_rng([zlib.crc32(name.encode()), seed]).standard_normal(out[name].shape)
        drawn = base * np.exp(spread * noise) if base else spread * noise
        out[name] = jnp.asarray(drawn.astype(out[name].dtype))
    for name, factor in factors.items():
        out[name] = (out[name] * factor).astype(out[name].dtype)
    return out
```

```python
import numpy as np
import concourse.bass as bass
from concourse import mybir
from contextlib import ExitStack

SEQ, D = 1024, 1024
P = 128
NT = SEQ // P
KC = D // P
HD = 64
VW = HD + 1
NSA_H, FOX_H, DIFF_H = 8, 4, 4
NCMP = 63
EPS = 1e-6
NEG = -1e30
LAM_INIT = 0.8 - 0.6
NE, DE = 32, 256
CAP = 128
MAX_OVF = 2 * SEQ // CAP - 1
NTILES = NE + MAX_OVF
NROWS = NTILES * CAP
ROUT = 36
NGL = 28
WN = (384, 412)
G_QN, G_QF, G_KS, G_KW, G_KF, G_QD, G_KD, G_KC = 0, 4, 6, 7, 8, 10, 12, 14

_CW = [("ident", P), ("scale", 16), ("eps", 1), ("dist", SEQ), ("distw", 640), ("distc", 512), ("tri", P), ("tris", P),
       ("fi4", 4), ("fi32", 32), ("tok", 8), ("thr", 224), ("ecap", 32), ("jj", 16),
       ("e31", 32), ("cvalid", 8)]
COL, _o = {}, 0
for _n, _w in _CW:
    COL[_n] = (_o, _o + _w)
    _o += _w
CONSTS = _o
SMALL = COL["eps"][1]


def steps_of(kind):
    full = [(t, 0, t + 1) for t in reversed(range(NT))]
    win = [(t, max(0, t - 4), min(t, 4) + 1) for t in reversed(range(NT))]
    out = []
    if kind == "nsa":
        out += [("C", 0, 0, 1), ("C", 4, 0, 1)]
    out += [("X", *s) for s in full]
    out += [("Y", *s) for s in (win if kind == "nsa" else full)]
    return out


class Count:

    def __init__(self, start=0):
        self.base, self.i, self.per, self.k = start, 0, 0, 0

    def loop(self, i, per):
        self.i, self.per, self.k = i, per, 0

    def done(self, trips):
        assert self.k == self.per, (self.k, self.per)
        self.base += trips * self.per
        self.i, self.per, self.k = 0, 0, 0

    def at(self, k):
        return self.base + k if isinstance(self.i, int) else self.i * self.per + (self.base + k)

    def next(self):
        self.k += 1
        return self.at(self.k)


def program(nc, a, out):
    f32, f32r = mybir.dt.float32, mybir.dt.float32r
    u32, i32 = mybir.dt.uint32, mybir.dt.int32
    ALU, ACT, AX = mybir.AluOpType, mybir.ActivationFunctionType, mybir.AxisListType
    ts = bass.ts
    ctx = ExitStack()
    with ctx:
        BASE = 16512

        def at(name, shape, dt, off):
            return nc.alloc_sbuf_tensor_at(name, shape, dt, offset=BASE + off)

        place = [0]

        def small(name, shape, dt=f32):
            n = 4
            for s in shape[1:]:
                n *= s
            t = at(name, shape, dt, place[0])
            place[0] += (n + 31) // 32 * 32
            return t

        cst = small("cst", [P, CONSTS])

        def C(n, lo=0, hi=None):
            s, e = COL[n]
            return cst[:, s + lo:(e if hi is None else s + hi)]

        ident = C("ident")
        ones = small("ones", [P, P])
        gbias = small("gbias", [P, NGL])
        rbias = small("rbias", [P, ROUT])
        subln = small("subln", [P, HD])
        lam4 = small("lam4", [P, 4, 32])
        GL = small("GL", [P, NT, NGL])
        G24 = small("G24", [P, 24, NT])
        cum = small("cum", [P, NT, 4])
        ssq = small("ssq", [P, 40])
        rstd, nv, nz = (small(n, [P, 40]) for n in ("rstd", "nv", "nz"))
        mx = small("mx", [P, 3, 4])
        r4 = small("r4", [P, 4])
        nlam = small("nlam", [P, 4])
        LG = small("LG", [P, NT, ROUT])
        w12 = small("w12", [P, 2, NT])
        slot = small("slot", [P, 2, NT], u32)
        ids = small("ids", [P, NTILES + 1], u32)
        idc = small("idc", [P, 2], u32)
        info = small("info", [1, 16], i32)
        KB = 1024
        assert place[0] <= 21 * KB, place[0]
        ZB, ZC, ZD, ZE = 21 * KB, 85 * KB, 110 * KB, 174 * KB
        END = 229344 - BASE

        hTh = at("hTh", [P, KC, SEQ], f32r, ZB)
        hTl = at("hTl", [P, KC, SEQ], f32r, ZB + 32 * KB)
        V = at("V", [P, 12, NT, VW], f32, ZC)
        wn = at("wn", [P, KC * WN[1]], f32, ZD)
        wnh = at("wnh", [P, KC * WN[1]], f32r, ZD + 13 * KB)
        wnl = at("wnl", [P, KC * WN[1]], f32r, ZD + 26 * KB)
        wst = at("wst", [P, 2, SEQ], f32, ZD + 39 * KB)
        wth = at("wth", [P, 2, SEQ], f32r, ZD + 47 * KB)
        wtl = at("wtl", [P, 2, SEQ], f32r, ZD + 55 * KB)
        thi = at("thi", [P, 2, SEQ], f32r, ZE)
        tlo = at("tlo", [P, 2, SEQ], f32r, ZE + 8 * KB)
        xt = at("xt", [P, NT, D], f32, ZE)
        gbc = at("gbc", [P, D], f32, ZD + 55 * KB)
        xn = at("xn", [P, 2, D], f32, ZD + 47 * KB)
        junk = at("junk", [P, D], f32, ZD + 59 * KB)

        w1 = at("w1", [P, 2, 16, 256], f32, ZD)
        w2k = at("w2k", [P, 2, P], f32, ZD + 32 * KB)
        w2v = at("w2v", [P, 2, HD], f32, ZD + 33 * KB)
        pe = at("pe", [P, 2, 16], f32, ZD + 34 * KB)
        blk = at("blk", [P, 16, P], f32, ZD + 35 * KB)
        zh = at("zh", [P, SEQ], f32, ZD + 43 * KB)
        zl = at("zl", [P, SEQ], f32, ZD + 47 * KB)
        ga = at("ga", [P, 256], f32, ZD + 51 * KB)
        gb = at("gb", [P, 256], f32, ZD + 52 * KB)
        gc = at("gc", [P, 256], f32, ZD + 53 * KB)
        hT2 = at("hT2", [P, 2, P], f32, ZD + 54 * KB)
        dg = at("dg", [P, 512], f32, ZD + 55 * KB)
        tmpd = at("tmpd", [P, 8, 64], f32, ZD + 57 * KB)
        lf = at("lf", [P, NT, 4], f32, ZD + 59 * KB)
        lfb = at("lfb", [P, NT, 4], f32, ZD + 60 * KB)
        qs = [at(f"qs{u}", [P, SEQ], f32r, ZB + 12 * KB * u) for u in range(2)]
        k1 = [at(f"k1{u}", [P, SEQ], f32r, ZB + 12 * KB * u + 4 * KB) for u in range(2)]
        k2 = [at(f"k2{u}", [P, SEQ], f32r, ZB + 12 * KB * u + 8 * KB) for u in range(2)]
        sp = at("sp", [P, 3, SEQ], f32, ZB + 24 * KB)
        pt = at("pt", [P, 2, SEQ], f32, ZB + 36 * KB)
        tabX = at("tabX", [P, SEQ], f32, ZB + 44 * KB)
        tabY = at("tabY", [P, SEQ], f32, ZB + 48 * KB)
        tabC = at("tabC", [P, 512], f32, ZB + 52 * KB)
        oh = at("oh", [P, 2, NT, HD], f32, ZB + 54 * KB)
        tmp = at("tmp", [P, NT, HD], f32, ZB + 58 * KB)
        kc1 = at("kc1", [P, P], f32r, ZB + 60 * KB)
        kc2 = at("kc2", [P, P], f32r, ZB + 61 * KB)
        vcm = at("vcm", [HD, 2, VW], f32, ZB + 62 * KB)
        FX = at("FX", [P, FOX_H, SEQ], f32, ZE)
        od = at("od", [P, NT, DIFF_H, HD], f32, ZE + 16 * KB)
        ot = at("ot", [P, 2, 6 * P], f32, ZE + 24 * KB)
        zrow = at("zrow", [P, D // 4], f32, ZE + 32 * KB)
        woh = at("woh", [P, KC, D], f32r, ZD)
        wol = at("wol", [P, KC, D], f32r, ZD + 32 * KB)
        wraw = at("wraw", [P, KC, D], f32, ZD + 32 * KB)
        oth = at("oth", [P, 2, KC, P], f32r, ZC)
        otl = at("otl", [P, 2, KC, P], f32r, ZC + 8 * KB)
        x2 = at("x2", [P, NT, D], f32, ZB)
        xr = at("xr", [P, 2, D], f32, ZB + 32 * KB)
        h2 = at("h2", [P, 2, D], f32, ZB + 40 * KB)
        h2T = at("h2T", [P, KC, P], f32, ZB + 48 * KB)
        wr = at("wr", [P, KC, ROUT], f32, ZB + 52 * KB)
        gf = at("gf", [P, D], f32, ZB + 54 * KB)
        junk2 = at("junk2", [P, D], f32, ZB + 58 * KB)
        _io = [0]

        def ri(name, shape, dt=f32):
            n = 4
            for s in shape[1:]:
                n *= s
            t = at(name, shape, dt, ZC + _io[0])
            _io[0] += (n + 31) // 32 * 32
            return t

        ra, rb, rc, rd = (ri(n, [P, NT, NE]) for n in ("ra", "rb", "rc", "rd"))
        oh1, oh2, memb = (ri(n, [P, NT, NE]) for n in ("oh1", "oh2", "memb"))
        el = ri("el", [P, NT, NE])
        s8 = ri("s8", [P, 8, NT])
        g4a, g4b = ri("g4a", [P, NT, 4]), ri("g4b", [P, NT, 4])
        mb = ri("mb", [P, NT + 1, NE])
        cntb = ri("cntb", [P, NE])
        cmp7 = ri("cmp7", [P, NE, 7])
        vt = ri("vt", [P, 2, NE])
        eb = ri("eb", [P, NE])
        cj = ri("cj", [P, 16, NE])
        ej = ri("ej", [P, 17])
        ltile = ri("ltile", [P, P])
        lzero = ri("lzero", [NTILES, P])
        slf = ri("slf", [P, 2, NT])
        assert _io[0] <= 25 * KB, _io[0]
        XG = at("XG", [P, 2, D], f32, ZD + 48 * KB)
        YO = at("YO", [P, 2, D], f32, ZD + 56 * KB)
        XT = at("XT", [P, 2, KC, P], f32, ZB + 56 * KB)
        ge = at("ge", [P, DE], f32, ZC)
        gd = at("gd", [P, DE], f32, ZC + KB)
        act2 = at("act2", [P, 2, DE], f32, ZC + 2 * KB)
        aT = at("aT", [P, 2, 2, P], f32, ZC + 4 * KB)
        WOFF = [ZE, ZD, ZD + 24 * KB, ZB + 32 * KB]
        wgu = [at(f"wgu{q}", [P, KC, 2 * DE], f32, o) for q, o in enumerate(WOFF)]
        wdn = [at(f"wdn{q}", [P, 2, D], f32, o + 16 * KB) for q, o in enumerate(WOFF)]
        y1 = at("y1", [P, NT, D], f32, ZD)
        y2 = at("y2", [P, NT, D], f32, ZD + 32 * KB)
        gfin = at("gfin", [P, D], f32, ZC + 12 * KB)
        junk3 = at("junk3", [P, D], f32, ZC + 16 * KB)

        PS = ctx.enter_context(nc.psum_tensor("PS", [P, 8, 512], f32))

        T_d = nc.dram_tensor("T_d", [2, 16, P, SEQ], f32).ap()
        T_r = T_d.rearrange("a g p t -> a (g p) t")
        O_d = nc.dram_tensor("O_d", [SEQ, 6 * P], f32).ap()
        O_v = O_d.rearrange("(t p) c -> p t c", p=P)
        h2_d = nc.dram_tensor("h2_d", [SEQ, D], f32).ap()
        list_d = nc.dram_tensor("list_d", [NROWS, 1], f32).ap()
        list_v = list_d.rearrange("(n p) o -> n (p o)", p=P)
        Y_d = nc.dram_tensor("Y_d", [NROWS, D], f32).ap()

        def sem(n):
            return ctx.enter_context(nc.semaphore(n))

        const_in, tab_in, gbc_in, waited = map(sem, ("const_in", "tab_in", "gbc_in", "waited"))
        rs_l, rs_0, rs_mid, rs_done, dq_done = map(sem, ("rs_l", "rs_0", "rs_mid", "rs_done", "dq_done"))
        x_in = [sem(f"x_in{t}") for t in range(NT)]
        ss_done, xn_done, a_tr, a_hi, a_free = map(sem, ("ss_done", "xn_done", "a_tr", "a_hi", "a_free"))
        wn_in, wn_hi, wn_split, c_mm, c_free = map(sem, ("wn_in", "wn_hi", "wn_split", "c_mm", "c_free"))
        w_in = [sem(f"w_in{p}") for p in range(2)]
        t_st = [sem(f"t_st{p}") for p in range(2)]
        b_whi, b_split, b_tr, b_hi, b_free = map(sem, ("b_whi", "b_split", "b_tr", "b_hi", "b_free"))
        dve_did, act_did, pe_did, blk_zero, w1_in, z_in = map(
            sem, ("dve_did", "act_did", "pe_did", "blk_zero", "w1_in", "z_in"))
        st_in = [sem("st_inX"), sem("st_inY")]
        s_ready, mx_ready, sub_ready, t_ready, p_ready, pv_done, o_free, tab_ready, oh_ready, oh_st, link = map(
            sem, ("s_ready", "mx_ready", "sub_ready", "t_ready", "p_ready", "pv_done", "o_free", "tab_ready",
                  "oh_ready", "oh_st", "link"))
        wo_in, wo_hi, wo_lo = sem("wo_in"), sem("wo_hi"), sem("wo_lo")
        o_in = [sem(f"o_in{p}") for p in range(2)]
        r_in = [sem(f"r_in{p}") for p in range(2)]
        g_tr, g_hi, g_lo, g_mm, x2_done, h_ss, h_xn, h_tr, h_ev, h_mm, h_lg, hw_in = map(
            sem, ("g_tr", "g_hi", "g_lo", "g_mm", "x2_done", "h_ss", "h_xn", "h_tr", "h_ev", "h_mm",
                  "h_lg", "hw_in"))
        h_st = [sem(f"h_st{p}") for p in range(2)]
        yz_st, ftab_ready, o_norm = map(sem, ("yz_st", "ftab_ready", "o_norm"))
        l0_st, sc_st, l_in = sem("l0_st"), sem("sc_st"), sem("l_in")
        we_in = [sem(f"we_in{q}") for q in range(4)]
        xg_in = [sem(f"xg_in{p}") for p in range(2)]
        ids_ok, idx_c, m_tr, m_x0, m_x1, m_gu, m_e, m_act, m_ta, m_aT, m_dn, m_y0, m_y1 = map(
            sem, ("ids_ok", "idx_c", "m_tr", "m_x0", "m_x1", "m_gu", "m_e", "m_act", "m_ta", "m_aT",
                  "m_dn", "m_y0", "m_y1"))
        y_st = [sem(f"y_st{p}") for p in range(2)]
        v_pe, v_act, v_dve, v_pool, v_w, v_x, v_y = map(
            sem, ("v_pe", "v_act", "v_dve", "v_pool", "v_w", "v_x", "v_y"))
        k_in = [sem(f"k_in{t}") for t in range(NT)]
        k_acc, k_ss, k_out, gfin_in = map(sem, ("k_acc", "k_ss", "k_out", "gfin_in"))
        k_st = sem("k_st")

        SEGS = [("nsa", 0, 4), ("nsa", 1, 4), ("fox", 0, 2), ("diff", 0, 4)]
        NSTEP = {"nsa": 18, "fox": 16, "diff": 16}
        FOX0 = 8 * NSTEP["nsa"]
        DIFF0 = FOX0 + 2 * NSTEP["fox"]
        ALL_STEPS = DIFF0 + 4 * NSTEP["diff"]

        RS_D, RS_H, RS_K = 2, 3, 11
        K_BATCH = ((0, 4), (4, 3), (7, 1))

        class Events:

            def __init__(self, s, names):
                self.s, self.names, self.n = s, names, 0

            def of(self, name):
                return self.names.index(name) + 1

            def did(self, name, ins, eng=None):
                assert self.names[self.n] == name, (self.names[self.n], name)
                self.n += 1
                ins.then_inc(self.s, 1)
                if eng is not None:
                    eng.wait_ge(self.s, self.n)

        gelu_d = ["z0", "b0", "z1", "b1", "q", "u", "d1", "r", "h"]
        DV = Events(dve_did, ["gl", "nz", "az", "u", "dm", "rd", "er", "g1", "g24", "le", "mn", "lf"] + [f"lb{t}" for t in range(NT)] + ["lamp0",
                              "lamp1", "nlam", "cum"]
                    + [n + "k" for n in gelu_d] + ["kc2k"] + [n + "v" for n in gelu_d]
                    + [f"dg{n}" for n in range(8)]
                    + ["gm", "ge1", "ge2", "gx", "g1h", "gs", "gsum", "gpen", "el", "m1", "q1", "q1i", "i1",
                       "o1", "rb", "m2", "q2", "q2i", "i2", "o2", "memb"] + [f"mb{t}" for t in range(NT + 1)] + ["md",
                       "cntb", "cmp", "v"] + [f"s{k}{c}" for k in (1, 2, 4, 8, 16) for c in "ab"]
                    + ["exc", "eb", "ra", "ge", "geb", "rae", "rs", "p1", "sl1", "r1", "sl2", "r2", "slot",
                       "den0", "den", "w1", "w2", "cj", "ej", "ejc", "nov", "info", "ids"])
        AC = Events(act_did, ["eg", "ef", "ln", "lam"] + [n + k for k in "kv" for n in ("sq", "ex", "hT", "c1")]
                    + [f"fx{n}" for n in range(8)] + ["rge", "re2"])
        PEV = Events(pe_did, ["cum"] + [n + k for k in "kv" for n in ("h", "tr", "o")]
                     + [f"fx{n}" for n in range(8)] + ["rank", "idt"])

        def flat(b, n=2):
            return PS[:, b:b + n, :].rearrange("p b c -> p (b c)")

        def apart(eng):
            eng.sem_inc(waited, 1)

        block = ctx.enter_context(nc.Block())

        @block.sync
        def _(sp_):
            sp_.dma_start(xt[:, 0, :], a["x"][0:P, :]).then_inc(x_in[0], 16)
            sp_.dma_start(cst[:, 0:SMALL], a["consts"][:, 0:SMALL]).then_inc(const_in, 16)
            for t in range(1, NT):
                sp_.dma_start(xt[:, t, :], a["x"][t * P:(t + 1) * P, :]).then_inc(x_in[t], 16)
            sp_.dma_start(gbc[:], a["g_attn"]).then_inc(gbc_in, 16)
            sp_.dma_start(wn[:, 0:KC * WN[0]], a["wn0"]).then_inc(wn_in, 16)
            sp_.dma_start(wst[:, 0, :], a["wt"][0]).then_inc(w_in[0], 16)
            sp_.dma_start(wst[:, 1, :], a["wt"][1]).then_inc(w_in[1], 16)
            sp_.dma_start(cst[:, SMALL:CONSTS], a["consts"][:, SMALL:CONSTS]).then_inc(tab_in, 16)
            sp_.dma_start(gbias[:], a["gbias"]).then_inc(tab_in, 16)
            sp_.dma_start(rbias[:], a["rbias"]).then_inc(tab_in, 16)
            sp_.dma_start(subln[:], a["subln"]).then_inc(tab_in, 16)
            sp_.dma_start(lam4[:], a["lam"].rearrange("p (a b) -> p a b", a=4)).then_inc(tab_in, 16)
            sp_.wait_ge(wn_split, 1)
            sp_.dma_start(wn[:, 0:KC * WN[1]], a["wn1"]).then_inc(wn_in, 16)

            def store_t(g, p):
                sp_.wait_ge(b_free, 4 + 2 * g + 2)
                sp_.dma_start(T_d[0, g], thi[:, p, :].bitcast(f32)).then_inc(t_st[p], 16)
                sp_.dma_start(T_d[1, g], tlo[:, p, :].bitcast(f32)).then_inc(t_st[p], 16)

            with sp_.Fori(0, 7) as j:
                for p in range(2):
                    sp_.wait_ge(b_split, 2 * j + (p + 1))
                    sp_.dma_start(wst[:, p, :], a["wt"][2 * j + (p + 2)]).then_inc(w_in[p], 16)
                    store_t(2 * j + p, p)
            for p in range(2):
                store_t(14 + p, p)
            for p in range(2):
                sp_.wait_ge(t_st[p], 32 * 8 + 1)
            sp_.wait_ge(c_free, 4 + 16)
            sp_.dma_start(w2k[:, :, 0:HD], a["w2k"].rearrange("p (c n) -> p c n", c=2)).then_inc(w1_in, 16)
            sp_.dma_start(w2k[:, :, HD:P], a["w2k"].rearrange("p (c n) -> p c n", c=2)).then_inc(w1_in, 16)
            sp_.dma_start(w2v[:], a["w2v"].rearrange("p (c n) -> p c n", c=2)).then_inc(w1_in, 16)
            sp_.dma_start(pe[:], a["pe"].rearrange("p (v c) -> p v c", v=2)).then_inc(w1_in, 16)
            for kv in range(2):
                sp_.dma_start(w1[:, kv], a["w1"][kv].rearrange("p (c n) -> p c n", c=16)).then_inc(w1_in, 16)
            for kv in range(2):
                for g in range(2):
                    n = 2 * kv + g
                    if n:
                        sp_.wait_ge(dve_did, DV.of(("b1k", "b0v")[0] if n == 2 else ("b0k" if n == 1 else "b0v")))
                    for r, z in enumerate((zh, zl)):
                        src = T_d[r, G_KC + kv, g * HD:(g + 1) * HD, :]
                        sp_.dma_start(z[0:HD, :], src).then_inc(z_in, 16)
                        sp_.dma_start(z[HD:P, 0:SEQ - 1], src[:, 1:SEQ]).then_inc(z_in, 16)

            def unit_rows(kind, g, i, u):
                if kind == "nsa":
                    return 64 * i + 256 * g, (G_KS, G_KW)[u] * P + 64 * g
                if kind == "fox":
                    return P * i + (G_QF * P + 64 * u), P * i + (G_KF * P + 64 * u)
                return HD * i + (G_QD * P + 32 * u), HD * i + (G_KD * P + 32 * u)

            def load_unit(kind, g, i, u):
                q0, k0 = unit_rows(kind, g, i, u)
                w = 32 if kind == "diff" else HD
                for b, part in enumerate((0, 1, 0, 1) if kind == "diff" else (0, 1)):
                    sp_.dma_start(qs[u][w * b:w * b + w, :].bitcast(f32), T_r[part, bass.ds(q0, w), :])\
                       .then_inc(st_in[u], 16)
                if kind == "diff":
                    for b, part in enumerate((0, 0, 1, 1)):
                        sp_.dma_start(k1[u][w * b:w * b + w, :].bitcast(f32), T_r[part, bass.ds(k0, w), :])\
                           .then_inc(st_in[u], 16)
                else:
                    for part, dst in ((0, k1), (1, k2)):
                        for b in range(2):
                            sp_.dma_start(dst[u][w * b:w * b + w, :].bitcast(f32),
                                          T_r[part, bass.ds(k0, w), :]).then_inc(st_in[u], 16)

            load_unit("nsa", 0, 0, 0)
            load_unit("nsa", 0, 0, 1)
            sp_.wait_ge(blk_zero, 3)
            for c in range(4):
                sp_.dma_start(Y_d[NE * CAP:, c * (D // 4):(c + 1) * (D // 4)].rearrange("(n p) d -> p n d", p=P),
                              zrow[:].unsqueeze(1).broadcast_to([P, MAX_OVF, D // 4])).then_inc(yz_st, 16)
            sdone, ohd = Count(), Count()

            def pair_io(kind, g, i, nxt):
                xs = 10 if kind == "nsa" else 8
                for k in range(NSTEP[kind]):
                    v = sdone.next()
                    if nxt and k == xs - 1:
                        sp_.wait_ge(s_ready, v)
                        load_unit(*nxt, 0)
                    if nxt and k == NSTEP[kind] - 1:
                        sp_.wait_ge(s_ready, v)
                        load_unit(*nxt, 1)
                for u in range({"nsa": 1, "fox": 2, "diff": 0}[kind]):
                    col = {"nsa": HD * i + 256 * g, "fox": P * i + (512 + HD * u)}[kind]
                    sp_.wait_ge(oh_ready, ohd.next())
                    sp_.dma_start(O_v[:, :, bass.ds(col, HD)], oh[:, u]).then_inc(oh_st, 16)

            for n, (kind, g, trips) in enumerate(SEGS):
                with sp_.Fori(0, trips - 1) as i:
                    sdone.loop(i, NSTEP[kind])
                    ohd.loop(i, {"nsa": 1, "fox": 2, "diff": 0}[kind])
                    pair_io(kind, g, i, (kind, g, i + 1))
                sdone.done(trips - 1)
                ohd.done(trips - 1)
                nxt = (SEGS[n + 1][0], SEGS[n + 1][1], 0) if n + 1 < len(SEGS) else None
                pair_io(kind, g, trips - 1, nxt)
                sdone.base, sdone.k = sdone.base + sdone.k, 0
                ohd.base, ohd.k = ohd.base + ohd.k, 0
                if kind == "fox":
                    sp_.wait_ge(oh_st, 16 * 12 + 1)
                    for p in range(2):
                        sp_.dma_start(ot[:, p, :], O_d[p * P:(p + 1) * P, :]).then_inc(o_in[p], 16)
                if n == 0:
                    for c in range(4):
                        sp_.dma_start(wraw[:, 2 * c:2 * c + 2, :],
                                      a["wo"][c].rearrange("p (k n) -> p k n", k=2)).then_inc(wo_in, 16)

            def load_expert(e, q):
                sp_.dma_start(wgu[q][:], a["wgu"][e].rearrange("p (k n) -> p k n", k=KC)).then_inc(we_in[q], 16)
                sp_.dma_start(wdn[q][:], a["wdn"][e].rearrange("p (k n) -> p k n", k=2)).then_inc(we_in[q], 16)

            sp_.wait_ge(pv_done, ALL_STEPS)
            for p in range(2):
                sp_.dma_start(xr[:, p, :], a["x"][p * P:(p + 1) * P, :]).then_inc(r_in[p], 16)
            sp_.wait_ge(dq_done, 4)
            sp_.dma_start(wr[:], a["wr"].rearrange("p (k n) -> p k n", k=KC)).then_inc(hw_in, 16)
            sp_.dma_start(gf[:], a["g_ffn"]).then_inc(hw_in, 16)
            sp_.dma_start(wgu[0][:], a["wgu"][0].rearrange("p (k n) -> p k n", k=KC)).then_inc(we_in[0], 16)

            def h2_store(t, p):
                sp_.wait_ge(h_xn, t + 1)
                sp_.dma_start(h2_d[ts(t, P), :], h2[:, p, :]).then_inc(h_st[p], 16)

            with sp_.Fori(0, 3) as j:
                for p in range(2):
                    sp_.wait_ge(g_tr, 4 * j + (2 * p + 2))
                    sp_.dma_start(ot[:, p, :], O_d[ts(2 * j + (p + 2), P), :]).then_inc(o_in[p], 16)
                    sp_.wait_ge(x2_done, 4 * j + (2 * p + 2))
                    sp_.dma_start(xr[:, p, :], a["x"][ts(2 * j + (p + 2), P), :]).then_inc(r_in[p], 16)
                    h2_store(2 * j + p, p)
            for p in range(2):
                h2_store(6 + p, p)
            sp_.wait_ge(g_mm, 16)
            sp_.dma_start(wdn[0][:], a["wdn"][0].rearrange("p (k n) -> p k n", k=2)).then_inc(we_in[0], 16)
            load_expert(1, 1)
            load_expert(2, 2)
            sp_.wait_ge(h_lg, 8)
            load_expert(3, 3)
            sp_.wait_ge(sc_st, 16 * 16)
            sp_.dma_start(ltile[0:NTILES, :], list_v).then_inc(l_in, 16)
            sp_.wait_ge(dve_did, DV.of("ids"))
            sp_.dma_start(gfin[:], a["g_fin"]).then_inc(gfin_in, 16)
            with sp_.Fori(0, 7) as i:
                for q in range(4):
                    sp_.wait_ge(m_dn, 4 * i + (q + 1))
                    load_expert(4 * i + (q + 4), q)
            sp_.wait_ge(m_dn, NE - 3)
            n_ovf = sp_.value_load(info[0:1, 0:1], min_val=0, max_val=MAX_OVF)
            with sp_.Fori(0, MAX_OVF) as j:
                with sp_.If(j < n_ovf):
                    eid = sp_.value_load(info[0:1, bass.ds(j + 1, 1)], min_val=0, max_val=NE - 1)
                    sp_.wait_ge(v_y, 16 * j + 1)
                    sp_.dma_start(wgu[0][:], a["wgu"][eid].rearrange("p (k n) -> p k n", k=KC)).then_inc(v_w, 16)
                    sp_.dma_start(wdn[0][:], a["wdn"][eid].rearrange("p (k n) -> p k n", k=2)).then_inc(v_w, 16)
            for t in range(NT):
                sp_.wait_ge(k_out, t + 1)
                sp_.dma_start(out[t * P:(t + 1) * P, :], y1[:, t, :]).then_inc(k_st, 16)
            sp_.wait_ge(k_st, 16 * NT)
            for p in range(2):
                sp_.wait_ge(y_st[p], 16 * 16 + 1)
            sp_.wait_ge(l0_st, 16)

        @block.gpsimd
        def _(pool):
            pool.sem_inc(m_tr, 2)
            nc.gpsimd.memset(ones[:], 1.0).then_inc(blk_zero, 1)
            nc.gpsimd.memset(zrow[:], 0.0).then_inc(blk_zero, 1)
            nc.gpsimd.memset(V[:, :, :, HD:VW], 1.0).then_inc(blk_zero, 1)

            def newton(col, w, n, count):
                y, v, z = (b[:, col:col + w] for b in (rstd, nv, nz))

                def did(ins, k):
                    ins.then_inc(rs_mid, 1)
                    pool.wait_ge(rs_mid, 4 * count + k)
                    apart(pool)

                did(nc.gpsimd.tensor_scalar(out=v, in0=ssq[:, col:col + w], scalar1=1.0 / n, scalar2=EPS,
                                            op0=ALU.mult, op1=ALU.add), 1)
                pool.wait_ge(rs_0, count + 1)
                apart(pool)
                did(nc.gpsimd.tensor_tensor(out=z, in0=y, in1=y, op=ALU.mult), 2)
                did(nc.gpsimd.tensor_tensor(out=z, in0=z, in1=v, op=ALU.mult), 3)
                did(nc.gpsimd.tensor_scalar(out=z, in0=z, scalar1=-0.5, scalar2=1.5, op0=ALU.mult,
                                            op1=ALU.add), 4)
                nc.gpsimd.tensor_tensor(out=y, in0=y, in1=z, op=ALU.mult).then_inc(rs_done, 1)

            for b in range(2):
                pool.wait_ge(ss_done, 4 * b + 4)
                newton(4 * b, 4, D, b)
            pool.wait_ge(c_free, 4 + 16)
            pool.wait_ge(b_free, 4 + 32)
            nc.gpsimd.memset(blk[:], 0.0).then_inc(blk_zero, 1)
            nc.gpsimd.memset(vcm[:], 1.0).then_inc(blk_zero, 1)
            pool.wait_ge(tab_in, 16 * 5)
            sub = Count()
            for tab, src in ((tabC, C("distc")), (tabX, C("dist")), (tabY[:, 0:640], C("distw"))):
                nc.gpsimd.tensor_scalar(out=tab[:], in0=src, scalar1=0.5, scalar2=None, op0=ALU.mult)\
                  .then_inc(tab_ready, 1)

            def halve(trips):
                with pool.Fori(0, trips) as i:
                    sub.loop(i, 18)
                    for k in range(18):
                        v = sub.next()
                        for at_, tab in ((1, tabC[:]), (9, tabX[:]), (17, tabY[:, 0:640])):
                            if k == at_:
                                pool.wait_ge(mx_ready, v)
                                apart(pool)
                                nc.gpsimd.tensor_scalar(out=tab, in0=tab, scalar1=0.5, scalar2=None,
                                                        op0=ALU.mult).then_inc(tab_ready, 1)
                sub.done(trips)

            def wo_low(c):
                pool.wait_ge(wo_hi, c + 1)
                nc.gpsimd.tensor_tensor(out=wol[:, 2 * c:2 * c + 2, :], in0=wraw[:, 2 * c:2 * c + 2, :],
                                        in1=woh[:, 2 * c:2 * c + 2, :].bitcast(f32), op=ALU.subtract)\
                  .then_inc(wo_lo, 1)

            halve(7)
            with pool.Fori(0, 2) as i:
                for s, (u, t, _, nk) in enumerate(steps_of("fox")):
                    tab, L = (tabX, tabY)[s % 2], nk * P
                    pool.wait_ge(ftab_ready, 16 * i + (s + 1))
                    apart(pool)
                    nc.gpsimd.affine_select(out=tab[:, L - P:L], in_=tab[:, L - P:L],
                                            compare_op=ALU.is_ge, fill=NEG, base=0, pattern=[[-1, P]],
                                            channel_multiplier=1).then_inc(tab_ready, 1)
            pool.wait_ge(mx_ready, DIFF0)
            nc.gpsimd.tensor_scalar(out=tabX[:], in0=C("dist"), scalar1=0.25, scalar2=None, op0=ALU.mult)\
              .then_inc(tab_ready, 1)
            for c in range(4):
                wo_low(c)

            with pool.Fori(0, 3) as i:
                pool.wait_ge(mx_ready, 16 * i + (DIFF0 + 16))
                apart(pool)
                nc.gpsimd.tensor_scalar(out=tabX[:], in0=tabX[:], scalar1=0.25, scalar2=None, op0=ALU.mult)\
                  .then_inc(tab_ready, 1)
            pool.wait_ge(dq_done, 4)
            newton(8, 32, HD, RS_D)
            for t in range(NT):
                pool.wait_ge(h_ss, t + 1)
                newton(2 + t, 1, D, RS_H + t)
            pool.wait_ge(g_mm, 16)
            pool.wait_ge(g_tr, 16)
            nc.gpsimd.memset(ltile[:], 0.0)
            nc.gpsimd.memset(lzero[:], 0.0).then_inc(idx_c, 1)
            pool.wait_ge(idx_c, 1)
            pool.dma_start(list_v, lzero[:]).then_inc(l0_st, 16)
            pool.wait_ge(l0_st, 16)
            pool.wait_ge(dve_did, DV.of("slot"))
            for k in range(2):
                for t in range(NT):
                    pool.indirect_dma_start(
                        out=list_d, out_offset=bass.IndirectOffsetOnAxis(ap=slot[:, k, t:t + 1], axis=0),
                        in_=C("tok", t, t + 1), in_offset=None).then_inc(sc_st, 16)
            pool.wait_ge(dve_did, DV.of("ids"))
            for p in range(2):
                pool.wait_ge(h_st[p], 16 * NT // 2)

            def gather(n, p, into, got):
                nc.gpsimd.tensor_copy(out=idc[:, p:p + 1], in_=ids[:, bass.ds(n, 1)]).then_inc(idx_c, 1)

            with pool.Fori(0, NE // 2) as j:
                for p in range(2):
                    n = 2 * j + p
                    pool.wait_ge(m_tr, n + 1)
                    gather(n, p, None, None)
                    pool.wait_ge(idx_c, n + 2)
                    apart(pool)
                    pool.indirect_dma_start(
                        out=XG[:, p, :], out_offset=None, in_=h2_d,
                        in_offset=bass.IndirectOffsetOnAxis(ap=idc[:, p:p + 1], axis=0)).then_inc(xg_in[p], 16)
            pool.wait_ge(m_tr, 2 + NE - 1)
            n_ovf = pool.value_load(info[0:1, 0:1], min_val=0, max_val=MAX_OVF)
            with pool.Fori(0, MAX_OVF) as j:
                with pool.If(j < n_ovf):
                    pool.wait_ge(v_y, 16 * j + 1)
                    nc.gpsimd.tensor_copy(out=idc[:, 0:1], in_=ids[:, bass.ds(j + NE, 1)]).then_inc(v_pool, 1)
                    pool.wait_ge(v_pool, j + 1)
                    apart(pool)
                    pool.indirect_dma_start(
                        out=XG[:, 0, :], out_offset=None, in_=h2_d,
                        in_offset=bass.IndirectOffsetOnAxis(ap=idc[:, 0:1], axis=0)).then_inc(v_x, 16)
            for p in range(2):
                pool.wait_ge(y_st[p], 16 * 16 + 1)
            pool.wait_ge(yz_st, 16 * 4)
            pool.wait_ge(v_y, 16 * n_ovf + 1)
            apart(pool)
            for t in range(NT):
                for k, dst in enumerate((y1, y2)):
                    pool.indirect_dma_start(
                        out=dst[:, t, :], out_offset=None, in_=Y_d,
                        in_offset=bass.IndirectOffsetOnAxis(ap=slot[:, k, t:t + 1], axis=0))\
                        .then_inc(k_in[t], 16)
            for b, (t, w) in enumerate(K_BATCH):
                pool.wait_ge(k_ss, t + w)
                newton(t, w, D, RS_K + b)

        @block.scalar
        def _(act):
            def copy(o, i, **kw):
                return nc.scalar.activation(o, i, ACT.Identity, **kw)

            def inv_sqrt(col, w, n, count):
                y = rstd[:, col:col + w]
                nc.scalar.activation(y, ssq[:, col:col + w], ACT.Ln, scale=1.0 / n, bias=C("eps")).then_inc(rs_l, 1)
                act.wait_ge(rs_l, count + 1)
                nc.scalar.activation(y, y, ACT.Exp, scale=-0.5).then_inc(rs_0, 1)

            act.sem_inc(c_free, 4)
            act.wait_ge(const_in, 16)
            act.sem_inc(p_ready, 2)
            act.sem_inc(v_y, 1)
            for p in range(2):
                act.sem_inc(t_st[p], 1)
                act.sem_inc(y_st[p], 1)
            for b in range(2):
                for t in range(4 * b, 4 * b + 4):
                    act.wait_ge(x_in[t], 16)
                    if t:
                        act.wait_ge(ss_done, t)
                    nc.scalar.activation(junk[:], xt[:, t, :], ACT.Square, accum_out=ssq[:, t:t + 1])\
                      .then_inc(ss_done, 1)
                act.wait_ge(ss_done, 4 * b + 4)
                inv_sqrt(4 * b, 4, D, b)
            with act.Fori(0, 4) as j:
                for p in range(2):
                    for c in range(2):
                        act.wait_ge(a_tr, 4 * j + (2 * p + c + 1))
                        apart(act)
                        copy(hTh[:, 4 * c:4 * c + 4, ts(2 * j + p, P)],
                             PS[:, 2 * p + c, :].rearrange("p (k t) -> p k t", k=4)).then_inc(a_hi, 1)

            def split_hi(n):
                act.wait_ge(wn_in, 16 * (n + 1))
                copy(wnh[:, 0:KC * WN[n]], wn[:, 0:KC * WN[n]]).then_inc(wn_hi, 1)

            def project_copy(h):
                for t in range(NT):
                    act.wait_ge(c_mm, NT * h + t + 1)
                    b = 4 + t % 4
                    ins = copy(V[:, 6 * h:6 * h + 6, t, 0:HD],
                               PS[:, b, 0:384].rearrange("p (h d) -> p h d", h=6))
                    if h:
                        ins = copy(GL[:, t, :], PS[:, b, 384:412])
                    ins.then_inc(c_free, 1)

            split_hi(0)
            project_copy(0)
            split_hi(1)

            def w_hi(g, p, k):
                act.wait_ge(w_in[p], k)
                copy(wth[:, p, :], wst[:, p, :]).then_inc(b_whi, 1)

            def t_hi(g, p, j):
                act.wait_ge(t_st[p], 32 * j + 1)
                for h in range(2):
                    act.wait_ge(b_tr, 2 * g + (h + 1))
                    apart(act)
                    nc.scalar.activation(thi[:, p, h * 512:(h + 1) * 512], PS[:, 2 * p + h, :], ACT.Identity,
                                         scale=cst[:, bass.ds(g + COL["scale"][0], 1)]).then_inc(b_hi, 1)

            w_hi(0, 0, 16)
            with act.Fori(0, 7) as j:
                for p in range(2):
                    w_hi(2 * j + (p + 1), 1 - p, 16 * j + 16 * (p + 1))
                    t_hi(2 * j + p, p, j)
            w_hi(15, 1, 16 * 8)
            t_hi(14, 0, 7)
            t_hi(15, 1, 7)
            project_copy(1)
            act.wait_ge(dve_did, DV.of("gl"))
            AC.did("eg", nc.scalar.activation(G24[:].rearrange("p c t -> p t c"), GL[:, :, 0:24], ACT.Exp,
                                              scale=-1.0))
            act.wait_ge(dve_did, DV.of("az"))
            AC.did("ef", nc.scalar.activation(tmpd[:, :, 4:8], tmpd[:, :, 0:4], ACT.Exp, scale=-1.0))
            act.wait_ge(dve_did, DV.of("u"))
            AC.did("ln", nc.scalar.activation(tmpd[:, :, 16:20], tmpd[:, :, 8:12], ACT.Ln))
            act.wait_ge(dve_did, DV.of("lamp1"))
            AC.did("lam", nc.scalar.activation(nlam[:, 2:4], nlam[:, 0:2], ACT.Exp))
            for kv, n in enumerate("kv"):
                act.wait_ge(pe_did, PEV.of("h" + n))
                AC.did("sq" + n, nc.scalar.activation(ga[:], PS[:, 4, 0:256], ACT.Square))
                act.wait_ge(dve_did, DV.of("u" + n))
                AC.did("ex" + n, nc.scalar.activation(gc[:], gb[:], ACT.Exp, scale=-1.5957691216057308))
                act.wait_ge(pe_did, PEV.of("tr" + n))
                AC.did("hT" + n, copy(hT2[:].rearrange("p c m -> p (c m)"), PS[:, 5, 0:256]))
                act.wait_ge(pe_did, PEV.of("o" + n))
                if kv == 0:
                    AC.did("c1k", copy(kc1[:], PS[:, 6, 0:P]))
                else:
                    act.wait_ge(blk_zero, 5)
                    AC.did("c1v", copy(vcm[:, :, 0:HD], PS[0:HD, 6, 0:P].rearrange("p (g d) -> p g d", g=2)))
            for n in range(8):
                act.wait_ge(pe_did, PEV.of(f"fx{n}"))
                AC.did(f"fx{n}", copy(FX[:, n // 2, (n % 2) * 512:(n % 2) * 512 + 512], PS[:, n % 2, :],
                                      scale=-1.0))
            tr = Count()

            def exps(s, u, t, k0, nk):
                if u == "C":
                    act.wait_ge(t_ready, tr.next())
                    nc.scalar.activation(pt[0:HD, s % 2, 0:512], PS[0:HD, 4 + s % 2, :], ACT.Exp)\
                      .then_inc(p_ready, 1)
                    return
                for c in range(0, nk, 4):
                    w = min(4, nk - c) * P
                    v = tr.next()
                    act.wait_ge(t_ready, v)
                    nc.scalar.activation(
                        pt[:, s % 2, c * P:c * P + w], PS[:, 4 + (tr.k - 1) % 2, 0:w], ACT.Exp)\
                        .then_inc(p_ready, 1)

            def fox_table(s, i):
                u, t, _, nk = steps_of("fox")[s]
                copy((tabX, tabY)[s % 2][:, 0:nk * P],
                     FX[:, bass.ds(2 * i + "XY".index(u), 1), 0:nk * P].rearrange("p o k -> p (o k)"),
                     bias=cum[:, t, bass.ds(2 * i + "XY".index(u), 1)]).then_inc(ftab_ready, 1)

            def wo_high(c):
                act.wait_ge(wo_in, 16 * 4)
                copy(woh[:, 2 * c:2 * c + 2, :], wraw[:, 2 * c:2 * c + 2, :]).then_inc(wo_hi, 1)

            for n, (kind, g, trips) in enumerate(SEGS):
                with act.Fori(0, trips) as i:
                    if kind == "fox":
                        act.wait_ge(mx_ready, 16 * i + FOX0)
                        apart(act)
                        for s in range(2):
                            fox_table(s, i)
                    tr.loop(i, 26 if kind == "nsa" else 24)
                    for s, step in enumerate(steps_of(kind)):
                        if kind == "fox" and s + 2 < NSTEP[kind]:
                            act.wait_ge(mx_ready, 16 * i + (FOX0 + s + 1))
                            apart(act)
                            fox_table(s + 2, i)
                        exps(s, *step)
                tr.done(trips)
                if n in (1, 2):
                    wo_high(2 * n - 2)
                    wo_high(2 * n - 1)
            act.wait_ge(dq_done, 4)
            inv_sqrt(8, 32, HD, RS_D)

            def o_high(t, p):
                for c in range(2):
                    act.wait_ge(g_tr, 2 * t + (c + 1))
                    copy(oth[:, p, 4 * c:4 * c + 4, :].rearrange("p k t -> p (k t)"), PS[:, c, :]).then_inc(g_hi, 1)

            def sumsq(t):
                act.wait_ge(x2_done, 2 * t + 2)
                nc.scalar.activation(junk2[:], x2[:, t, :], ACT.Square, accum_out=ssq[:, 2 + t:3 + t])\
                  .then_inc(h_ss, 1)
                act.wait_ge(h_ss, t + 1)
                inv_sqrt(2 + t, 1, D, RS_H + t)

            def hT_copy(t):
                for c in range(2):
                    act.wait_ge(h_tr, 2 * t + c + 1)
                    copy(h2T[:, 4 * c:4 * c + 4, :].rearrange("p k t -> p (k t)"), PS[:, 4 + c, :]).then_inc(h_ev, 1)

            o_high(0, 0)
            for t in range(NT):
                if t + 1 < NT:
                    o_high(t + 1, (t + 1) % 2)
                if t:
                    hT_copy(t - 1)
                sumsq(t)
            hT_copy(NT - 1)
            act.wait_ge(dve_did, DV.of("gs"))
            AC.did("rge", nc.scalar.activation(rb[:, :, 0:4], ra[:, :, 0:4], ACT.Exp))
            act.wait_ge(dve_did, DV.of("md"))
            AC.did("re2", nc.scalar.activation(s8[:, 7, :], s8[:, 7, :], ACT.Exp))

            def m_x(n, p):
                act.wait_ge(m_tr, n + 3)
                copy(XT[:, p, 0:4, :].rearrange("p k t -> p (k t)"), PS[:, 0, :]).then_inc(m_x0, 1)

            def m_exp(n, p):
                act.wait_ge(m_gu, n + 1)
                act.wait_ge(m_act, n)
                nc.scalar.activation(ge[:], PS[:, 2 + p, 0:DE], ACT.Exp, scale=-1.0).then_inc(m_e, 1)

            def m_at(n, p):
                act.wait_ge(m_ta, n + 1)
                copy(aT[:, p].rearrange("p c t -> p (c t)"), PS[:, 4, 0:DE]).then_inc(m_aT, 1)

            def m_out(n, p, k):
                act.wait_ge(m_dn, n + 1)
                act.wait_ge(y_st[p], 16 * k + 1)
                copy(YO[:, p, 0:512], PS[:, 5, :]).then_inc(m_y0, 1)
                act.wait_ge(m_y0, n + 2)
                act.wait_ge(m_y1, n + 2)
                act.dma_start(Y_d[ts(n, P), :], YO[:, p, :]).then_inc(y_st[p], 16)

            def m_slot(n, p, k, before=True, after=True):
                m_exp(n, p)
                if before:
                    m_at(n - 1, 1 - p)
                if after:
                    m_x(n + 1, 1 - p)
                if before:
                    m_out(n - 1, 1 - p, k)

            m_x(0, 0)
            m_slot(0, 0, 0, before=False)
            with act.Fori(0, 7) as i:
                for q in range(1, 5):
                    m_slot(4 * i + q, q % 2, 2 * i + (q - 1) // 2)
            for q in range(1, 4):
                m_slot(28 + q, q % 2, 14 + (q - 1) // 2, after=q < 3)
            m_at(31, 1)
            m_out(31, 1, 15)
            act.wait_ge(m_dn, NE)
            act.wait_ge(yz_st, 16 * 4)
            act.wait_ge(y_st[0], 16 * NE // 2 + 1)
            n_ovf = act.value_load(info[0:1, 0:1], min_val=0, max_val=MAX_OVF)
            with act.Fori(0, MAX_OVF) as j:
                with act.If(j < n_ovf):
                    act.wait_ge(v_pe, 4 * j + 1)
                    copy(XT[:, 0, 0:4, :].rearrange("p k t -> p (k t)"), PS[:, 0, :]).then_inc(v_act, 1)
                    act.wait_ge(v_pe, 4 * j + 2)
                    nc.scalar.activation(ge[:], PS[:, 2, 0:DE], ACT.Exp, scale=-1.0).then_inc(v_act, 1)
                    act.wait_ge(v_pe, 4 * j + 3)
                    copy(aT[:, 0].rearrange("p c t -> p (c t)"), PS[:, 4, 0:DE]).then_inc(v_act, 1)
                    act.wait_ge(v_pe, 4 * j + 4)
                    copy(YO[:, 0, 0:512], PS[:, 5, :]).then_inc(v_act, 1)
                    act.wait_ge(v_act, 4 * j + 4)
                    act.wait_ge(v_dve, 6 * j + 6)
                    act.dma_start(Y_d[ts(j + NE, P), :], YO[:, 0, :]).then_inc(v_y, 16)
            for b, (t0, w) in enumerate(K_BATCH):
                for t in range(t0, t0 + w):
                    act.wait_ge(k_acc, t + 1)
                    if t:
                        act.wait_ge(k_ss, t)
                    nc.scalar.activation(junk3[:], x2[:, t, :], ACT.Square, accum_out=ssq[:, t:t + 1])\
                      .then_inc(k_ss, 1)
                act.wait_ge(k_ss, t0 + w)
                inv_sqrt(t0, w, D, RS_K + b)

        @block.vector
        def _(dve):
            V_ = nc.vector
            lk = Count()

            def chain(ins):
                v = lk.next()
                ins.then_inc(link, 1)
                dve.wait_ge(link, v)

            dve.sem_inc(a_free, 4)
            dve.sem_inc(b_free, 4)
            dve.sem_inc(o_free, 2)
            dve.sem_inc(oh_st, 1)
            dve.sem_inc(m_y0, 1)
            dve.sem_inc(m_y1, 1)
            dve.wait_ge(gbc_in, 16)
            for t in range(NT + 1):
                if t < NT:
                    dve.wait_ge(rs_done, t // 4 + 1)
                    if t >= 2:
                        dve.wait_ge(a_tr, 2 * t - 2)
                    V_.scalar_tensor_tensor(out=xn[:, t % 2, :], in0=xt[:, t, :], scalar=rstd[:, t:t + 1],
                                            in1=gbc[:], op0=ALU.mult, op1=ALU.mult).then_inc(xn_done, 1)
                if t:
                    for c in range(2):
                        dve.wait_ge(a_hi, 2 * t - 1 + c)
                        o = (slice(None), slice(4 * c, 4 * c + 4), slice((t - 1) * P, t * P))
                        V_.tensor_tensor(out=hTl[o], in0=PS[:, 2 * ((t - 1) % 2) + c, :].rearrange(
                            "p (k t) -> p k t", k=4), in1=hTh[o].bitcast(f32), op=ALU.subtract).then_inc(a_free, 1)

            def split_lo(n):
                dve.wait_ge(wn_hi, n + 1)
                V_.tensor_tensor(out=wnl[:, 0:KC * WN[n]], in0=wn[:, 0:KC * WN[n]],
                                 in1=wnh[:, 0:KC * WN[n]].bitcast(f32), op=ALU.subtract).then_inc(wn_split, 1)

            split_lo(0)
            split_lo(1)

            def w_lo(g, p):
                dve.wait_ge(b_whi, g + 1)
                V_.tensor_tensor(out=wtl[:, p, :], in0=wst[:, p, :], in1=wth[:, p, :].bitcast(f32),
                                 op=ALU.subtract).then_inc(b_split, 1)

            def t_lo(g, p):
                for h in range(2):
                    dve.wait_ge(b_hi, 2 * g + (h + 1))
                    V_.scalar_tensor_tensor(out=tlo[:, p, h * 512:(h + 1) * 512], in0=PS[:, 2 * p + h, :],
                                            scalar=cst[:, bass.ds(g + COL["scale"][0], 1)],
                                            in1=thi[:, p, h * 512:(h + 1) * 512].bitcast(f32),
                                            op0=ALU.mult, op1=ALU.subtract).then_inc(b_free, 1)

            w_lo(0, 0)
            with dve.Fori(0, 7) as j:
                for p in range(2):
                    w_lo(2 * j + (p + 1), 1 - p)
                    t_lo(2 * j + p, p)
            w_lo(15, 1)
            t_lo(14, 0)
            t_lo(15, 1)
            dve.wait_ge(c_free, 4 + 16)
            dve.wait_ge(tab_in, 16 * 5)
            D_ = lambda n, ins: DV.did(n, ins, dve)
            D_("gl", V_.tensor_tensor(out=GL[:], in0=GL[:], in1=gbias[:].unsqueeze(1).broadcast_to([P, NT, NGL]),
                                      op=ALU.add))
            z = GL[:, :, 24:28]
            td = lambda k: tmpd[:, :, 4 * k:4 * k + 4]
            D_("nz", V_.tensor_scalar(out=td(0), in0=z, scalar1=-1.0, scalar2=None, op0=ALU.mult))
            D_("az", V_.tensor_tensor(out=td(0), in0=td(0), in1=z, op=ALU.max))
            dve.wait_ge(act_did, AC.of("ef"))
            D_("u", V_.tensor_scalar(out=td(2), in0=td(1), scalar1=1.0, scalar2=None, op0=ALU.add))
            D_("dm", V_.tensor_scalar(out=td(3), in0=td(2), scalar1=-1.0, scalar2=1e-30, op0=ALU.add, op1=ALU.max))
            D_("rd", V_.reciprocal(out=td(3), in_=td(3)))
            D_("er", V_.tensor_tensor(out=td(3), in0=td(3), in1=td(1), op=ALU.mult))
            D_("g1", V_.tensor_scalar(out=G24[:], in0=G24[:], scalar1=1.0, scalar2=None, op0=ALU.add))
            D_("g24", V_.reciprocal(out=G24[:], in_=G24[:]))
            dve.wait_ge(act_did, AC.of("ln"))
            D_("le", V_.tensor_tensor(out=td(3), in0=td(3), in1=td(4), op=ALU.mult))
            D_("mn", V_.tensor_scalar(out=td(0), in0=z, scalar1=0.0, scalar2=None, op0=ALU.min))
            D_("lf", V_.tensor_tensor(out=lf[:], in0=td(0), in1=td(3), op=ALU.subtract))
            D_("lb0", V_.tensor_scalar(out=lfb[:, 0], in0=lf[:, 0], scalar1=0.0, scalar2=None, op0=ALU.mult))
            for t in range(1, NT):
                D_(f"lb{t}", V_.tensor_tensor(out=lfb[:, t], in0=lfb[:, t - 1], in1=lf[:, t - 1], op=ALU.add))
            for k in range(2):
                D_(f"lamp{k}", V_.tensor_tensor_reduce(out=ga[:, 0:32], in0=lam4[:, 2 * k, :],
                                                       in1=lam4[:, 2 * k + 1, :], scale=1.0, scalar=0.0,
                                                       op0=ALU.mult, op1=ALU.add, accum_out=nlam[:, k:k + 1]))
            dve.wait_ge(act_did, AC.of("lam"))
            D_("nlam", V_.scalar_tensor_tensor(out=nlam[:, 0:1], in0=nlam[:, 3:4], scalar=LAM_INIT,
                                               in1=nlam[:, 2:3], op0=ALU.subtract, op1=ALU.subtract))
            dve.wait_ge(pe_did, PEV.of("cum"))
            D_("cum", V_.tensor_copy(out=cum[:].rearrange("p t f -> p (t f)"), in_=PS[:, 7, 0:32]))
            dve.wait_ge(w1_in, 16 * 6)
            dve.wait_ge(blk_zero, 5)
            for kv, n in enumerate("kv"):
                if kv:
                    dve.wait_ge(pe_did, PEV.of("hk"))
                for g in range(2):
                    dve.wait_ge(z_in, 64 * (2 * kv + g + 1))
                    D_(f"z{g}" + n, V_.tensor_tensor(out=zh[:, 0:SEQ - 1], in0=zh[:, 0:SEQ - 1],
                                                     in1=zl[:, 0:SEQ - 1], op=ALU.add))
                    zv = zh[:].rearrange("p (m s two) -> p s two m", s=8, two=2)
                    for b in range(2):
                        ins = V_.tensor_tensor(
                            out=blk[:, 8 * b:8 * b + 8, g * HD:g * HD + NCMP], in0=zv[:, :, 0, b:b + NCMP],
                            in1=pe[:, kv, 8 * b:8 * b + 8].unsqueeze(2).broadcast_to([P, 8, NCMP]), op=ALU.add)
                    D_(f"b{g}" + n, ins)
                dve.wait_ge(act_did, AC.of("sq" + n))
                D_("q" + n, V_.tensor_scalar(out=gb[:], in0=ga[:], scalar1=0.044715, scalar2=1.0, op0=ALU.mult,
                                             op1=ALU.add))
                D_("u" + n, V_.tensor_tensor(out=gb[:], in0=gb[:], in1=PS[:, 4, 0:256], op=ALU.mult))
                dve.wait_ge(act_did, AC.of("ex" + n))
                D_("d1" + n, V_.tensor_scalar(out=gc[:], in0=gc[:], scalar1=1.0, scalar2=None, op0=ALU.add))
                D_("r" + n, V_.reciprocal(out=gc[:], in_=gc[:]))
                D_("h" + n, V_.tensor_tensor(out=ga[:], in0=gc[:], in1=PS[:, 4, 0:256], op=ALU.mult))
                if kv == 0:
                    dve.wait_ge(act_did, AC.of("c1k"))
                    D_("kc2k", V_.tensor_tensor(out=kc2[:], in0=PS[:, 6, 0:P], in1=kc1[:].bitcast(f32),
                                                op=ALU.subtract))
            for n in range(8):
                f, h = n // 2, n % 2
                if n:
                    dve.wait_ge(pe_did, PEV.of(f"fx{n - 1}"))
                D_(f"dg{n}", V_.tensor_tensor(
                    out=dg[:].rearrange("p (t c) -> p t c", t=4), in0=ident.unsqueeze(1).broadcast_to([P, 4, P]),
                    in1=cum[:, 4 * h:4 * h + 4, f].unsqueeze(2).broadcast_to([P, 4, P]), op=ALU.mult))

            sr, hr, tb, pv, ob = Count(), Count(), Count(), Count(), Count()

            def softmax_step(kind, s, u, t, k0, nk):
                first = s == 0 or steps_of(kind)[s - 1][0] != u
                if kind == "fox" or (kind == "diff" and s == 0) or (kind == "nsa" and first):
                    dve.wait_ge(tab_ready, tb.next())
                dve.wait_ge(s_ready, sr.next())
                apart(dve)
                b, bank = s % 3, 2 * (s % 2)
                if u == "C":
                    sv = sp[:, b, 0:256].rearrange("p (t c) -> p t c", t=4)
                    chain(V_.tensor_tensor(out=sp[:, b, 0:256], in0=PS[:, bank, 0:256],
                                           in1=tabC[:, HD * t:HD * t + 256], op=ALU.add))
                    V_.tensor_reduce(out=mx[:, b, :], in_=sv, axis=AX.X, op=ALU.max).then_inc(mx_ready, 1)
                    return
                L = nk * P
                if kind == "fox":
                    tab = (tabX, tabY)[s % 2][:, 0:L]
                elif kind == "nsa" and u == "Y":
                    off = P * (4 - min(t, 4))
                    tab = tabY[:, off:off + L]
                else:
                    tab = tabX[:, (NT - 1 - t) * P:(NT - 1 - t) * P + L]
                V_.tensor_tensor_reduce(out=sp[:, b, 0:L], in0=flat(bank)[:, 0:L], in1=tab, scale=1.0,
                                        scalar=-3e38, op0=ALU.add, op1=ALU.max,
                                        accum_out=mx[:, b, 0:1]).then_inc(mx_ready, 1)

            def subtract(s, u, t, k0, nk):
                dve.wait_ge(mx_ready, hr.next())
                if u == "C":
                    apart(dve)
                    sv = sp[:, s % 3, 0:256].rearrange("p (t c) -> p t c", t=4)
                    V_.tensor_tensor(out=sv, in0=sv, in1=mx[:, s % 3, :].unsqueeze(2).broadcast_to([P, 4, HD]),
                                     op=ALU.subtract).then_inc(sub_ready, 1)
                    return
                L = nk * P
                V_.tensor_scalar(out=sp[:, s % 3, 0:L], in0=sp[:, s % 3, 0:L], scalar1=mx[:, s % 3, 0:1],
                                 scalar2=None, op0=ALU.subtract).then_inc(sub_ready, 1)

            def out_batch(kind, i, g, b, last):
                unit = ("CXY" if kind == "nsa" else "XY")[b // 2]
                if unit == "C":
                    t4 = 4 * (b % 2)
                else:
                    t4 = 4 - 4 * (b % 2)
                bank = 6 + b % 2
                dve.wait_ge(pv_done, pv.at(last))
                o = PS[:, bank, 0:4 * VW].rearrange("p (j c) -> p j c", c=VW)
                chain(V_.reciprocal(out=r4[:].unsqueeze(2), in_=o[:, :, HD:VW]))
                if kind == "nsa":
                    br = "CXY".index(unit)
                    gate = G24[:].rearrange("p c t -> p (c t)")[:, bass.ds(24 * i + (96 * g + 8 * br + t4), 4)]
                    chain(V_.tensor_tensor(out=r4[:], in0=r4[:], in1=gate, op=ALU.mult))
                    if unit == "C" and t4 == 0:
                        chain(V_.tensor_tensor(out=r4[:], in0=r4[:], in1=C("cvalid", 0, 4), op=ALU.mult))
                rb_ = r4[:].unsqueeze(2).broadcast_to([P, 4, HD])
                if kind == "nsa":
                    dst = oh[:, 0, t4:t4 + 4, :]
                    into = dst if unit == "C" else tmp[:, t4:t4 + 4, :]
                else:
                    u = "XY".index(unit)
                    into = oh[:, u, t4:t4 + 4, :] if kind == "fox" else (tmp[:, t4:t4 + 4, :] if u else
                                                                         oh[:, 1, t4:t4 + 4, :])
                V_.tensor_tensor(out=into, in0=o[:, :, 0:HD], in1=rb_, op=ALU.mult).then_inc(o_free, 1)
                dve.wait_ge(o_free, 2 + ob.next())
                if kind == "nsa" and unit != "C":
                    chain(V_.tensor_tensor(out=dst, in0=dst, in1=into, op=ALU.add))
                if (kind == "nsa" and unit == "Y" or kind == "fox") and t4 == 0:
                    dve.sem_inc(oh_ready, 1)

            def diff_end(i):
                chain(V_.scalar_tensor_tensor(out=tmp[:], in0=tmp[:], scalar=nlam[:, 0:1], in1=oh[:, 1],
                                              op0=ALU.mult, op1=ALU.add))
                V_.scalar_tensor_tensor(out=od[:, :, bass.ds(i, 1), :].rearrange("p t o d -> p t (o d)"), in0=tmp[:],
                                        scalar=1.0 - LAM_INIT, in1=subln[:].unsqueeze(1).broadcast_to([P, NT, HD]),
                                        op0=ALU.mult, op1=ALU.mult)
                chain(V_.tensor_tensor(out=oh[:, 1], in0=tmp[:], in1=tmp[:], op=ALU.mult))
                V_.tensor_reduce(out=ssq[:, bass.ds(8 * i + 8, 8)], in_=oh[:, 1], axis=AX.X, op=ALU.add)\
                  .then_inc(dq_done, 1)
                dve.wait_ge(dq_done, i + 1)

            stored = 0
            for kind, g, trips in SEGS:
                st = steps_of(kind)
                nb = 6 if kind == "nsa" else 4
                ends = ([0, 1] if kind == "nsa" else []) + [len(st) - 13, len(st) - 9, len(st) - 5, len(st) - 1]
                heads = {"nsa": 1, "fox": 2, "diff": 0}[kind]
                with dve.Fori(0, trips) as i:
                    lk.loop(i, {"nsa": 19, "fox": 4, "diff": 6}[kind])
                    for c, per in ((sr, len(st)), (hr, len(st)), (pv, len(st)), (ob, nb), (tb, {"nsa": 3, "fox": 16, "diff": 1}[kind])):
                        c.loop(i, per)
                    b = 0
                    for s in range(len(st) + 5):
                        if s < len(st):
                            softmax_step(kind, s, *st[s])
                        if 1 <= s <= len(st):
                            subtract(s - 1, *st[s - 1])
                        while b < nb and ends[b] + 4 <= s:
                            if b == 0:
                                dve.wait_ge(oh_st, 16 * heads * i + (16 * stored + 1))
                            out_batch(kind, i, g, b, ends[b] + 1)
                            b += 1
                    if kind == "diff":
                        diff_end(i)
                pv.k = len(st)
                for c in (lk, sr, hr, pv, ob, tb):
                    c.done(trips)
                stored += trips * heads

            dve.wait_ge(rs_done, RS_D + 1)
            for t in range(NT):
                V_.tensor_tensor(out=od[:, t], in0=od[:, t], in1=rstd[:, 8 + t:40:8].unsqueeze(2)
                                 .broadcast_to([P, 4, HD]), op=ALU.mult).then_inc(o_norm, 1)

            def o_lo(t, p):
                for c in range(2):
                    dve.wait_ge(g_hi, 2 * t + c + 1)
                    V_.tensor_tensor(out=otl[:, p, 4 * c:4 * c + 4, :].rearrange("p k t -> p (k t)"),
                                     in0=PS[:, c, :],
                                     in1=oth[:, p, 4 * c:4 * c + 4, :].rearrange("p k t -> p (k t)").bitcast(f32),
                                     op=ALU.subtract).then_inc(g_lo, 1)

            o_lo(0, 0)
            for t in range(NT):
                if t + 1 < NT:
                    o_lo(t + 1, (t + 1) % 2)
                dve.wait_ge(r_in[t % 2], 16 * (t // 2 + 1))
                for h in range(2):
                    dve.wait_ge(g_mm, 2 * t + h + 1)
                    V_.tensor_tensor(out=x2[:, t, h * 512:h * 512 + 512], in0=PS[:, 2 + h, :],
                                     in1=xr[:, t % 2, h * 512:h * 512 + 512], op=ALU.add).then_inc(x2_done, 1)
                if t:
                    dve.wait_ge(h_mm, t)
                    V_.tensor_tensor(out=LG[:, t - 1, :], in0=PS[:, 6, 0:ROUT], in1=rbias[:], op=ALU.add)\
                      .then_inc(h_lg, 1)
                dve.wait_ge(rs_done, RS_H + t + 1)
                if t >= 2:
                    dve.wait_ge(h_st[t % 2], 16 * (t // 2))
                dve.wait_ge(hw_in, 32)
                V_.scalar_tensor_tensor(out=h2[:, t % 2, :], in0=x2[:, t, :], scalar=rstd[:, 2 + t:3 + t],
                                        in1=gf[:], op0=ALU.mult, op1=ALU.mult).then_inc(h_xn, 1)
            dve.wait_ge(h_mm, NT)
            V_.tensor_tensor(out=LG[:, NT - 1, :], in0=PS[:, 6, 0:ROUT], in1=rbias[:], op=ALU.add).then_inc(h_lg, 1)
            dve.wait_ge(h_lg, NT)

            bc = lambda x, w: x.unsqueeze(2).broadcast_to([P, NT, w])
            tt = lambda n, o, i0, i1, op: D_(n, V_.tensor_tensor(out=o, in0=i0, in1=i1, op=op))
            red = lambda n, o, i0, op: D_(n, V_.tensor_reduce(out=o, in_=i0, axis=AX.X, op=op))
            gl, ex = LG[:, :, 0:4], LG[:, :, 4:ROUT]
            fi4 = C("fi4").unsqueeze(1).broadcast_to([P, NT, 4])
            fi32 = C("fi32").unsqueeze(1).broadcast_to([P, NT, NE])
            red("gm", s8[:, 0, :], gl, ALU.max)
            tt("ge1", g4a[:], gl, bc(s8[:, 0, :], 4), ALU.is_equal)
            tt("ge2", g4a[:], g4a[:], fi4, ALU.mult)
            red("gx", s8[:, 1, :], g4a[:], ALU.max)
            tt("g1h", g4b[:], g4a[:], bc(s8[:, 1, :], 4), ALU.is_equal)
            tt("gs", ra[:, :, 0:4], gl, bc(s8[:, 0, :], 4), ALU.subtract)
            dve.wait_ge(act_did, AC.of("rge"))
            red("gsum", s8[:, 2, :], rb[:, :, 0:4], ALU.add)
            D_("gpen", V_.tensor_scalar(out=g4a[:], in0=g4b[:], scalar1=-1.0, scalar2=1e30, op0=ALU.add,
                                        op1=ALU.mult))
            r48 = lambda x: x.rearrange("p t (g e) -> p t g e", g=4)
            tt("el", r48(el[:]), r48(ex), g4a[:].unsqueeze(3).broadcast_to([P, NT, 4, 8]), ALU.add)
            red("m1", s8[:, 3, :], el[:], ALU.max)
            tt("q1", ra[:], el[:], bc(s8[:, 3, :], NE), ALU.is_equal)
            tt("q1i", ra[:], ra[:], fi32, ALU.mult)
            red("i1", s8[:, 4, :], ra[:], ALU.max)
            tt("o1", oh1[:], ra[:], bc(s8[:, 4, :], NE), ALU.is_equal)
            D_("rb", V_.scalar_tensor_tensor(out=rb[:], in0=oh1[:], scalar=-1e35, in1=el[:], op0=ALU.mult,
                                             op1=ALU.add))
            red("m2", s8[:, 5, :], rb[:], ALU.max)
            tt("q2", rc[:], rb[:], bc(s8[:, 5, :], NE), ALU.is_equal)
            tt("q2i", rc[:], rc[:], fi32, ALU.mult)
            red("i2", s8[:, 6, :], rc[:], ALU.max)
            tt("o2", oh2[:], rc[:], bc(s8[:, 6, :], NE), ALU.is_equal)
            tt("memb", memb[:], oh1[:], oh2[:], ALU.add)
            D_("mb0", V_.tensor_scalar(out=mb[:, 0, :], in0=memb[:, 0, :], scalar1=0.0, scalar2=None, op0=ALU.mult))
            for t in range(1, NT + 1):
                tt(f"mb{t}", mb[:, t, :], mb[:, t - 1, :], memb[:, t - 1, :], ALU.add)
            tt("md", s8[:, 7, :], s8[:, 5, :], s8[:, 3, :], ALU.subtract)
            dve.wait_ge(pe_did, PEV.of("rank"))
            D_("cntb", V_.tensor_copy(out=cntb[:], in_=PS[:, 1, 0:NE]))
            tt("cmp", cmp7[:], cntb[:].unsqueeze(2).broadcast_to([P, NE, 7]),
               C("thr").rearrange("p (e j) -> p e j", j=7), ALU.is_gt)
            red("v", vt[:, 0, :], cmp7[:], ALU.add)
            src = 0
            for k in (1, 2, 4, 8, 16):
                D_(f"s{k}a", V_.tensor_copy(out=vt[:, 1 - src, :], in_=vt[:, src, :]))
                tt(f"s{k}b", vt[:, 1 - src, k:NE], vt[:, 1 - src, k:NE], vt[:, src, 0:NE - k], ALU.add)
                src = 1 - src
            inc = vt[:, src, :]
            red("exc", eb[:], cmp7[:], ALU.add)
            tt("eb", eb[:], inc, eb[:], ALU.subtract)
            D_("ra", V_.tensor_copy(out=ra[:], in_=PS[:, 0, 0:NT * NE].rearrange("p (t e) -> p t e", e=NE)))
            D_("ge", V_.tensor_scalar(out=rb[:], in0=ra[:], scalar1=float(CAP), scalar2=None, op0=ALU.is_ge))
            D_("geb", V_.scalar_tensor_tensor(out=rc[:, 0, :], in0=eb[:], scalar=float(CAP), in1=C("e31"),
                                              op0=ALU.mult, op1=ALU.add))
            tt("rae", rb[:], rb[:], rc[:, 0, :].unsqueeze(1).broadcast_to([P, NT, NE]), ALU.mult)
            tt("rs", ra[:], ra[:], C("ecap").unsqueeze(1).broadcast_to([P, NT, NE]), ALU.add)
            tt("p1", ra[:], ra[:], rb[:], ALU.add)
            tt("sl1", rb[:], ra[:], oh1[:], ALU.mult)
            red("r1", slf[:, 0, :], rb[:], ALU.add)
            tt("sl2", rb[:], ra[:], oh2[:], ALU.mult)
            red("r2", slf[:, 1, :], rb[:], ALU.add)
            D_("slot", V_.tensor_copy(out=slot[:], in_=slf[:]))
            dve.wait_ge(act_did, AC.of("re2"))
            D_("den0", V_.tensor_scalar(out=s8[:, 0, :], in0=s8[:, 7, :], scalar1=1.0, scalar2=None, op0=ALU.add))
            tt("den", s8[:, 0, :], s8[:, 0, :], s8[:, 2, :], ALU.mult)
            D_("w1", V_.reciprocal(out=w12[:, 0, :], in_=s8[:, 0, :]))
            tt("w2", w12[:, 1, :], w12[:, 0, :], s8[:, 7, :], ALU.mult)
            tt("cj", cj[:], inc.unsqueeze(1).broadcast_to([P, 16, NE]),
               C("jj").unsqueeze(2).broadcast_to([P, 16, NE]), ALU.is_le)
            red("ej", ej[:, 1:17], cj[:], ALU.add)
            D_("ejc", V_.tensor_scalar(out=ej[:, 1:17], in0=ej[:, 1:17], scalar1=float(NE - 1), scalar2=None,
                                       op0=ALU.min))
            D_("nov", V_.tensor_copy(out=ej[:, 0:1], in_=inc[:, NE - 1:NE]))
            D_("info", V_.tensor_copy(out=info[0:1, 0:16], in_=ej[0:1, 0:16]))
            dve.wait_ge(pe_did, PEV.of("idt"))
            D_("ids", V_.tensor_copy(out=ids[:, 0:NTILES], in_=PS[:, 2, 0:NTILES]))

            def m_x(n, p):
                dve.wait_ge(m_tr, n + 3)
                V_.tensor_copy(out=XT[:, p, 4:8, :].rearrange("p k t -> p (k t)"), in_=PS[:, 1, :]).then_inc(m_x1, 1)

            def m_gate(n, p):
                dve.wait_ge(m_e, n + 1)
                chain(V_.tensor_scalar(out=gd[:], in0=ge[:], scalar1=1.0, scalar2=None, op0=ALU.add))
                chain(V_.reciprocal(out=gd[:], in_=gd[:]))
                chain(V_.tensor_tensor(out=gd[:], in0=gd[:], in1=PS[:, 2 + p, 0:DE], op=ALU.mult))
                V_.tensor_tensor(out=act2[:, p, :], in0=gd[:], in1=PS[:, 2 + p, DE:2 * DE], op=ALU.mult)\
                  .then_inc(m_act, 1)

            def m_out(n, p, k):
                dve.wait_ge(m_dn, n + 1)
                dve.wait_ge(y_st[p], 16 * k + 1)
                V_.tensor_copy(out=YO[:, p, 512:D], in_=PS[:, 6, :]).then_inc(m_y1, 1)

            def m_slot(n, p, k, before=True, after=True):
                m_gate(n, p)
                if after:
                    m_x(n + 1, 1 - p)
                if before:
                    m_out(n - 1, 1 - p, k)

            m_x(0, 0)
            m_slot(0, 0, 0, before=False)
            lk.base, lk.k = lk.base + lk.k, 0
            with dve.Fori(0, 7) as i:
                lk.loop(i, 12)
                for q in range(1, 5):
                    m_slot(4 * i + q, q % 2, 2 * i + (q - 1) // 2)
            lk.done(7)
            for q in range(1, 4):
                m_slot(28 + q, q % 2, 14 + (q - 1) // 2, after=q < 3)
            m_out(31, 1, 15)
            dve.wait_ge(m_dn, NE)
            dve.wait_ge(y_st[0], 16 * NE // 2 + 1)
            n_ovf = dve.value_load(info[0:1, 0:1], min_val=0, max_val=MAX_OVF)
            with dve.Fori(0, MAX_OVF) as j:
                with dve.If(j < n_ovf):
                    dve.wait_ge(v_pe, 4 * j + 1)
                    V_.tensor_copy(out=XT[:, 0, 4:8, :].rearrange("p k t -> p (k t)"), in_=PS[:, 1, :]).then_inc(v_dve, 1)
                    dve.wait_ge(v_act, 4 * j + 2)
                    V_.tensor_scalar(out=gd[:], in0=ge[:], scalar1=1.0, scalar2=None, op0=ALU.add).then_inc(v_dve, 1)
                    dve.wait_ge(v_dve, 6 * j + 2)
                    V_.reciprocal(out=gd[:], in_=gd[:]).then_inc(v_dve, 1)
                    dve.wait_ge(v_dve, 6 * j + 3)
                    V_.tensor_tensor(out=gd[:], in0=gd[:], in1=PS[:, 2, 0:DE], op=ALU.mult).then_inc(v_dve, 1)
                    dve.wait_ge(v_dve, 6 * j + 4)
                    V_.tensor_tensor(out=act2[:, 0, :], in0=gd[:], in1=PS[:, 2, DE:2 * DE], op=ALU.mult)\
                      .then_inc(v_dve, 1)
                    dve.wait_ge(v_pe, 4 * j + 4)
                    V_.tensor_copy(out=YO[:, 0, 512:D], in_=PS[:, 6, :]).then_inc(v_dve, 1)
            dve.wait_ge(gfin_in, 16)
            dve.wait_ge(k_in[0], 32)
            def k_final(b):
                t0, w = K_BATCH[b]
                dve.wait_ge(rs_done, RS_K + b + 1)
                for t in range(t0, t0 + w):
                    V_.scalar_tensor_tensor(out=y1[:, t, :], in0=x2[:, t, :], scalar=rstd[:, t:t + 1],
                                            in1=gfin[:], op0=ALU.mult, op1=ALU.mult).then_inc(k_out, 1)

            for t in range(NT):
                dve.wait_ge(k_in[t], 32)
                for k, y in enumerate((y1, y2)):
                    V_.scalar_tensor_tensor(out=x2[:, t, :], in0=y[:, t, :], scalar=w12[:, k, t:t + 1],
                                            in1=x2[:, t, :], op0=ALU.mult, op1=ALU.add).then_inc((link, k_acc)[k], 1)
                    if k == 0:
                        dve.wait_ge(link, lk.next())
                if t == 5:
                    k_final(0)
            k_final(1)
            k_final(2)

        @block.tensor
        def _(pe_):
            mm, tp = nc.tensor.matmul, nc.tensor.transpose
            pe_.wait_ge(const_in, 16)
            with pe_.Fori(0, 4) as j:
                for p in range(2):
                    pe_.wait_ge(xn_done, 2 * j + (p + 1))
                    for c in range(2):
                        pe_.wait_ge(a_free, 4 * j + (2 * p + c + 1))
                        for q in range(4):
                            k = 4 * c + q
                            ins = tp(PS[:, 2 * p + c, q * P:(q + 1) * P], xn[:, p, k * P:(k + 1) * P], ident)
                        ins.then_inc(a_tr, 1)
            pe_.wait_ge(a_free, 4 + 16)

            def project(h):
                pe_.wait_ge(wn_split, h + 1)
                n = WN[h]
                wv = [w[:, 0:KC * n].rearrange("p (k n) -> p k n", k=KC) for w in (wnh, wnl)]
                for t in range(NT):
                    pe_.wait_ge(c_free, NT * h + t + 1)
                    o = PS[:, 4 + t % 4, 0:n]
                    for k in range(KC):
                        for x, w in ((hTh, 0), (hTh, 1), (hTl, 0)):
                            ins = mm(o, x[:, k, t * P:(t + 1) * P], wv[w][:, k, :],
                                     start=(k == 0 and x is hTh and w == 0), stop=(k == KC - 1 and x is hTl))
                    ins.then_inc(c_mm, 1)

            project(0)
            with pe_.Fori(0, 8) as j:
                for p in range(2):
                    pe_.wait_ge(b_split, 2 * j + (p + 1))
                    for h in range(2):
                        pe_.wait_ge(b_free, 4 * j + (2 * p + h + 1))
                        for k in range(KC):
                            for w, x in ((wth, hTh), (wth, hTl), (wtl, hTh)):
                                ins = mm(PS[:, 2 * p + h, :], w[:, p, k * P:(k + 1) * P],
                                         x[:, k, h * 512:(h + 1) * 512],
                                         start=(k == 0 and w is wth and x is hTh), stop=(k == KC - 1 and w is wtl))
                        ins.then_inc(b_tr, 1)
            project(1)

            def prefix(o, tri, src, before, w):
                mm(o[:, 0:NT * w], C(tri), src, start=True, stop=False)
                return mm(o[:, 0:NT * w], ones[:], before, start=False, stop=True)

            pe_.wait_ge(tab_in, 16 * 5)
            pe_.wait_ge(dve_did, DV.of(f"lb{NT - 1}"))
            pe_.wait_ge(blk_zero, 5)
            PEV.did("cum", prefix(PS[:, 7, :], "tri", lf[:].rearrange("p t f -> p (t f)"),
                                  lfb[:, 0:NT].rearrange("p t f -> p (t f)"), 4))
            pe_.wait_ge(w1_in, 16 * 6)
            for kv, n in enumerate("kv"):
                pe_.wait_ge(dve_did, DV.of("b1" + n))
                for c in range(16):
                    ins = mm(PS[:, 4, 0:256], blk[:, c, :], w1[:, kv, c, :], start=(c == 0), stop=(c == 15))
                PEV.did("h" + n, ins)
                pe_.wait_ge(dve_did, DV.of("h" + n))
                for c in range(2):
                    ins = tp(PS[:, 5, c * P:(c + 1) * P], ga[:, c * P:(c + 1) * P], ident)
                PEV.did("tr" + n, ins)
                pe_.wait_ge(act_did, AC.of("hT" + n))
                if kv == 0:
                    for c in range(2):
                        ins = mm(PS[:, 6, 0:P], w2k[:, c, :], hT2[:, c, :], start=(c == 0), stop=(c == 1))
                else:
                    pe_.wait_ge(dve_did, DV.of("kc2k"))
                    for g in range(2):
                        for c in range(2):
                            ins = mm(PS[0:HD, 6, g * HD:(g + 1) * HD], hT2[:, c, g * HD:(g + 1) * HD],
                                     w2v[:, c, :], start=(c == 0), stop=(c == 1))
                PEV.did("o" + n, ins)
            pe_.wait_ge(b_free, 4 + 32)
            for n in range(8):
                pe_.wait_ge(dve_did, DV.of(f"dg{n}"))
                if n >= 2:
                    pe_.wait_ge(act_did, AC.of(f"fx{n - 2}"))
                PEV.did(f"fx{n}", mm(PS[:, n % 2, :], ones[:], dg[:], start=True, stop=True))
            pe_.wait_ge(act_did, AC.of("fx7"))
            su, cf, ch, ob = Count(), Count(), Count(), Count()
            units = 0
            for kind, g, trips in SEGS:
                st = steps_of(kind)
                chunks = [1 if s[0] == "C" else (s[3] + 3) // 4 for s in st]
                per_in = 128 if kind == "diff" else 96
                with pe_.Fori(0, trips) as i:
                    for c, per in ((su, len(st)), (cf, sum(chunks)), (ch, sum(chunks)),
                                   (ob, 6 if kind == "nsa" else 4)):
                        c.loop(i, per)

                    def scores(s):
                        u, t, k0, nk = st[s]
                        if s == 0 or st[s - 1][0] != u and u != "X" or (u == "X" and s == 0):
                            un = 1 if u == "Y" else 0
                            pe_.wait_ge(st_in[un], per_in * i + (units + per_in))
                        if s == 2:
                            pe_.wait_ge(mx_ready, su.at(1))
                        if u == "C":
                            for q in range(4):
                                for n, kk in enumerate((kc1, kc2)):
                                    ins = mm(PS[:, 2 * (s % 2), q * HD:(q + 1) * HD],
                                             qs[0][:, (t + q) * P:(t + q + 1) * P],
                                             kk[:, g * HD:(g + 1) * HD], start=(n == 0), stop=(n == 1))
                            ins.then_inc(s_ready, 1)
                            return
                        un = "XY".index(u)
                        ks = (k1[un],) if kind == "diff" else (k1[un], k2[un])
                        for c in range(0, nk, 4):
                            w = min(4, nk - c) * P
                            for n, kk in enumerate(ks):
                                ins = mm(PS[:, 2 * (s % 2) + c // 4, 0:w], qs[un][:, t * P:(t + 1) * P],
                                         kk[:, (k0 + c) * P:(k0 + c) * P + w],
                                         start=(n == 0), stop=(n == len(ks) - 1))
                        ins.then_inc(s_ready, 1)

                    def transposes(s):
                        u, t, k0, nk = st[s]
                        pe_.wait_ge(sub_ready, su.next())
                        for c in range(0, nk, 4):
                            pe_.wait_ge(p_ready, cf.next())
                            if u == "C":
                                apart(pe_)
                            bank = 4 + (cf.k - 1) % 2
                            if u == "C":
                                for q in range(4):
                                    ins = tp(PS[0:HD, bank, q * P:(q + 1) * P],
                                             sp[:, s % 3, q * HD:(q + 1) * HD], ident)
                            else:
                                for q in range(min(4, nk - c)):
                                    ins = tp(PS[:, bank, q * P:(q + 1) * P],
                                             sp[:, s % 3, (c + q) * P:(c + q + 1) * P], ident)
                            ins.then_inc(t_ready, 1)

                    def values(s):
                        u, t, k0, nk = st[s]
                        pe_.wait_ge(p_ready, ch.at(2 + sum(chunks[:s + 1])))
                        if u == "C" or t % 4 == 3:
                            pe_.wait_ge(o_free, ob.next())
                        bank = 6 + (ob.k - 1) % 2
                        if u == "C":
                            for q in range(4):
                                ins = mm(PS[:, bank, q * VW:(q + 1) * VW], pt[0:HD, s % 2, q * P:(q + 1) * P],
                                         vcm[:, g, :], start=True, stop=True)
                            ins.then_inc(pv_done, 1)
                            return
                        if kind == "nsa":
                            vh = V[:, g if u == "X" else 2 + g]
                        elif kind == "fox":
                            vh = V[:, bass.ds(2 * i + (4 + "XY".index(u)), 1)].rearrange("p o t d -> p (o t) d")
                        else:
                            vh = V[:, bass.ds(i + 8, 1)].rearrange("p o t d -> p (o t) d")
                        for q in range(nk):
                            ins = mm(PS[:, bank, (t % 4) * VW:(t % 4 + 1) * VW],
                                     pt[:, s % 2, q * P:(q + 1) * P], vh[:, k0 + q, :],
                                     start=(q == 0), stop=(q == nk - 1))
                        ins.then_inc(pv_done, 1)

                    for s in range(len(st) + 3):
                        if s < len(st):
                            scores(s)
                        if 2 <= s < len(st) + 2:
                            transposes(s - 2)
                        if s >= 3:
                            values(s - 3)
                ch.k = sum(chunks)
                for c in (su, cf, ch, ob):
                    c.done(trips)
                units += trips * per_in
            pe_.wait_ge(o_free, 2 + ob.base)

            def o_transposes(t):
                pe_.wait_ge(o_in[t % 2], 16 * (t // 2 + 1))
                pe_.wait_ge(o_norm, t + 1)
                for c in range(2):
                    for q in range(4):
                        k = 4 * c + q
                        src = ot[:, t % 2, k * P:(k + 1) * P] if k < 6 else \
                            od[:, t, 2 * k - 12:2 * k - 10, :].rearrange("p h d -> p (h d)")
                        ins = tp(PS[:, c, q * P:(q + 1) * P], src, ident)
                    ins.then_inc(g_tr, 1)

            def router(t):
                pe_.wait_ge(hw_in, 32)
                pe_.wait_ge(h_xn, t + 1)
                for c in range(2):
                    for q in range(4):
                        k = 4 * c + q
                        ins = tp(PS[:, 4 + c, q * P:(q + 1) * P], h2[:, t % 2, k * P:(k + 1) * P], ident)
                    ins.then_inc(h_tr, 1)
                pe_.wait_ge(h_ev, 2 * t + 2)
                if t:
                    pe_.wait_ge(h_lg, t)
                for k in range(KC):
                    ins = mm(PS[:, 6, 0:ROUT], h2T[:, k, :], wr[:, k, :], start=(k == 0), stop=(k == KC - 1))
                ins.then_inc(h_mm, 1)

            o_transposes(0)
            pe_.wait_ge(wo_lo, 4)
            for t in range(NT):
                pe_.wait_ge(g_lo, 2 * t + 2)
                for h in range(2):
                    if t:
                        pe_.wait_ge(x2_done, 2 * (t - 1) + h + 1)
                    for k in range(KC):
                        for x, w in ((oth, woh), (oth, wol), (otl, woh)):
                            ins = mm(PS[:, 2 + h, :], x[:, t % 2, k, :], w[:, k, h * 512:(h + 1) * 512],
                                     start=(k == 0 and x is oth and w is woh), stop=(k == KC - 1 and x is otl))
                    ins.then_inc(g_mm, 1)
                if t + 1 < NT:
                    o_transposes(t + 1)
                if t:
                    router(t - 1)
            router(NT - 1)
            pe_.wait_ge(dve_did, DV.of(f"mb{NT}"))
            prefix(PS[:, 0, :], "tris", memb[:].rearrange("p t e -> p (t e)"),
                   mb[:, 0:NT].rearrange("p t e -> p (t e)"), NE)
            PEV.did("rank", mm(PS[:, 1, 0:NE], ones[:], mb[:, NT, :], start=True, stop=True))
            pe_.wait_ge(x2_done, 16)
            pe_.wait_ge(l_in, 16)
            PEV.did("idt", tp(PS[:, 2, 0:P], ltile[:], ident))
            pe_.wait_ge(dve_did, DV.of("ids"))

            def m_transposes(n, p, k):
                pe_.wait_ge(xg_in[p], k)
                for c in range(2):
                    for q in range(4):
                        kk = 4 * c + q
                        ins = tp(PS[:, c, q * P:(q + 1) * P], XG[:, p, kk * P:(kk + 1) * P], ident)
                ins.then_inc(m_tr, 1)

            def m_up(n, p, q, k):
                pe_.wait_ge(m_x0, n + 1)
                pe_.wait_ge(m_x1, n + 1)
                pe_.wait_ge(we_in[q], k)
                for c in range(KC):
                    ins = mm(PS[:, 2 + p, :], XT[:, p, c, :], wgu[q][:, c, :], start=(c == 0), stop=(c == KC - 1))
                ins.then_inc(m_gu, 1)

            def m_act_t(n, p):
                pe_.wait_ge(m_act, n + 1)
                for c in range(2):
                    ins = tp(PS[:, 4, c * P:(c + 1) * P], act2[:, p, c * P:(c + 1) * P], ident)
                ins.then_inc(m_ta, 1)

            def m_down(n, p, q):
                pe_.wait_ge(m_aT, n + 1)
                pe_.wait_ge(m_y0, n + 1)
                pe_.wait_ge(m_y1, n + 1)
                for h in range(2):
                    for c in range(2):
                        ins = mm(PS[:, 5 + h, :], aT[:, p, c, :], wdn[q][:, c, h * 512:(h + 1) * 512],
                                 start=(c == 0), stop=(c == 1))
                ins.then_inc(m_dn, 1)

            def m_slot(n, q, kw_, kx, before=True, after=True):
                p = q % 2
                m_up(n, p, q % 4, kw_)
                if before:
                    m_act_t(n - 1, 1 - p)
                if after:
                    m_transposes(n + 1, 1 - p, kx)
                if before:
                    m_down(n - 1, 1 - p, (q - 1) % 4)

            m_transposes(0, 0, 16)
            m_slot(0, 0, 32, 16, before=False)
            with pe_.Fori(0, 7) as i:
                for q in range(1, 5):
                    m_slot(4 * i + q, q, 32 * i + 32 * (1 + q // 4), 32 * i + 16 * ((q + 1) // 2 + 1))
            for q in range(1, 4):
                m_slot(28 + q, q, 32 * 8, 32 * 7 + 16 * ((q + 1) // 2 + 1), after=q < 3)
            m_act_t(31, 1)
            m_down(31, 1, 3)
            pe_.wait_ge(m_y0, NE + 1)
            pe_.wait_ge(m_y1, NE + 1)
            n_ovf = pe_.value_load(info[0:1, 0:1], min_val=0, max_val=MAX_OVF)
            with pe_.Fori(0, MAX_OVF) as j:
                with pe_.If(j < n_ovf):
                    pe_.wait_ge(v_x, 16 * j + 16)
                    for c in range(2):
                        for q in range(4):
                            kk = 4 * c + q
                            ins = tp(PS[:, c, q * P:(q + 1) * P], XG[:, 0, kk * P:(kk + 1) * P], ident)
                    ins.then_inc(v_pe, 1)
                    pe_.wait_ge(v_act, 4 * j + 1)
                    pe_.wait_ge(v_dve, 6 * j + 1)
                    pe_.wait_ge(v_w, 32 * j + 32)
                    for c in range(KC):
                        ins = mm(PS[:, 2, :], XT[:, 0, c, :], wgu[0][:, c, :], start=(c == 0), stop=(c == KC - 1))
                    ins.then_inc(v_pe, 1)
                    pe_.wait_ge(v_dve, 6 * j + 5)
                    for c in range(2):
                        ins = tp(PS[:, 4, c * P:(c + 1) * P], act2[:, 0, c * P:(c + 1) * P], ident)
                    ins.then_inc(v_pe, 1)
                    pe_.wait_ge(v_act, 4 * j + 3)
                    for h in range(2):
                        for c in range(2):
                            ins = mm(PS[:, 5 + h, :], aT[:, 0, c, :], wdn[0][:, c, h * 512:(h + 1) * 512],
                                     start=(c == 0), stop=(c == 1))
                    ins.then_inc(v_pe, 1)


_WIDTHS = (512, 128, 128, 128, 128, 128, 128, 24, 256, 256, 256, 4, 256, 256, 256)
_NAMES = ("q", "kc", "vc", "ks", "vs", "kw", "vw", "gate", "fq", "fk", "fv", "ff", "dq", "dk", "dv")


def constants():
    c = np.zeros((P, CONSTS), np.float32)
    p = np.arange(P)[:, None]

    def put(name, v):
        s, e = COL[name]
        c[:, s:e] = np.broadcast_to(np.asarray(v, np.float32).reshape(-1, e - s) if np.ndim(v) else v, (P, e - s))

    put("ident", np.eye(P))
    d = p - np.arange(SEQ)[None] + (SEQ - P)
    put("dist", np.where(d >= 0, -d, NEG))
    d = p - np.arange(640)[None] + 512
    put("distw", np.where((d >= 0) & (d < 512), -d, NEG))
    d = (p[:, :, None] + P * np.arange(NT)[None, :, None]) - (16 * np.arange(64)[None, None] + 31)
    put("distc", np.where(d >= 0, -d, NEG).reshape(P, 512))
    m = np.arange(P)[None]
    put("tri", p <= m)
    put("tris", p < m)
    sc = np.ones(16)
    sc[:6] = HD ** -0.5
    sc[G_QD:G_QD + 2] = 32 ** -0.5
    put("scale", sc)
    put("fi4", 4 - np.arange(4))
    put("fi32", NE - np.arange(NE))
    put("tok", p + P * np.arange(8)[None])
    put("thr", np.tile(CAP * np.arange(1, 8), NE))
    put("ecap", CAP * np.arange(NE))
    put("jj", np.arange(16))
    put("e31", CAP * (NE - 1 - np.arange(NE)))
    put("eps", EPS)
    put("cvalid", (p + P * np.arange(8)[None]) >= 31)
    return c


def layout(i):
    w = i["w_in"][0]
    at, cols = 0, {}
    for n, k in zip(_NAMES, _WIDTHS):
        cols[n] = w[:, at:at + k]
        at += k
    t = np.concatenate([cols[n] for n in ("q", "fq", "ks", "kw", "fk", "dq", "dk", "kc", "vc")], 1)
    wt = t.reshape(KC, P, 16, P).transpose(2, 1, 0, 3).reshape(16, P, SEQ)
    n0 = np.concatenate([cols["vs"], cols["vw"], cols["fv"][:, :P]], 1)
    n1 = np.concatenate([cols["fv"][:, P:], cols["dv"], cols["gate"], cols["ff"]], 1)
    kp = lambda x: x.reshape(-1, P, x.shape[-1]).transpose(1, 0, 2).reshape(P, -1)
    row = lambda x: np.broadcast_to(x.reshape(1, -1), (P, x.size))
    pe = [i[n][0].reshape(16, P).T for n in ("cmp_k_pe", "cmp_v_pe")]
    wo = i["w_out"][0].reshape(4, 2, P, D).transpose(0, 2, 1, 3).reshape(4, P, 2 * D)
    gu = np.concatenate([i["w_e_gate"][0], i["w_e_up"][0]], 2)
    return {
        "x": i["x"][0], "g_attn": row(i["norm_attn"]), "consts": constants(),
        "gbias": row(np.concatenate([i["b_gate"][0], i["b_fgt"][0]])),
        "rbias": row(np.concatenate([i["b_grp"][0], i["b_exp"][0]])),
        "subln": row(i["diff_subln"]), "lam": row(i["diff_lambda"]),
        "wn0": kp(n0), "wn1": kp(n1), "wt": wt,
        "w2k": kp(i["cmp_k_w2"][0]), "w2v": kp(i["cmp_v_w2"][0]), "pe": np.concatenate(pe, 1),
        "w1": np.stack([kp(i["cmp_k_w1"][0]), kp(i["cmp_v_w1"][0])]),
        "wo": wo, "wr": kp(np.concatenate([i["w_grp"][0], i["w_exp"][0]], 1)), "g_ffn": row(i["norm_ffn"]),
        "wgu": gu.reshape(NE, KC, P, 2 * DE).transpose(0, 2, 1, 3).reshape(NE, P, KC * 2 * DE),
        "wdn": i["w_e_down"][0].reshape(NE, 2, P, D).transpose(0, 2, 1, 3).reshape(NE, P, 2 * D),
        "g_fin": row(i["norm_final"]),
    }


def kernel(**inputs):
    import concourse.bacc as bacc
    from concourse.bass_utils import run_bass_kernel_spmd

    arrays = {k: np.ascontiguousarray(v) for k, v in layout({k: np.asarray(v) for k, v in inputs.items()}).items()}
    nc = bacc.Bacc("TRN2", target_bir_lowering=False, num_devices=1)
    a = {k: nc.dram_tensor("in_" + k, v.shape, mybir.dt.from_np(v.dtype), kind="ExternalInput").ap()
         for k, v in arrays.items()}
    out = nc.dram_tensor("out_0", (SEQ, D), mybir.dt.float32, kind="ExternalOutput").ap()
    program(nc, a, out)
    r = run_bass_kernel_spmd(nc, [{"in_" + k: v for k, v in arrays.items()}], core_ids=[0])
    return r.results[0]["out_0"].reshape(1, SEQ, D)
```

```python
import numpy as np
import concourse.bass as bass
from concourse import mybir
from contextlib import ExitStack

SEQ, D = 1024, 1024
P = 128
NT = SEQ // P
KC = D // P
HD = 64
VW = HD + 1
NSA_H, FOX_H, DIFF_H = 8, 4, 4
NCMP = 63
EPS = 1e-6
NEG = -1e30
LAM_INIT = 0.8 - 0.6
NE, DE = 32, 256
CAP = 128
MAX_OVF = 2 * SEQ // CAP - 1
NTILES = NE + MAX_OVF
NROWS = NTILES * CAP
ROUT = 36
NGL = 28
WN = (384, 412)
G_KC, G_QN, G_QF, G_KS, G_KW, G_KF, G_QD, G_KD = 0, 2, 6, 8, 9, 10, 12, 14

_CW = [("ident", P), ("scale", 16), ("eps", 1), ("dist", SEQ), ("distw", 640), ("distc", 512), ("tri", P), ("tris", P),
       ("fi4", 4), ("fi32", 32), ("tok", 8), ("thr", 224), ("ecap", 32), ("jj", 16),
       ("e31", 32), ("iota", P), ("cvalid", 8), ("slopes", 12)]
COL, _o = {}, 0
for _n, _w in _CW:
    COL[_n] = (_o, _o + _w)
    _o += _w
CONSTS = _o
SMALL = COL["eps"][1]


def steps_of(kind):
    full = [(t, 0, t + 1) for t in reversed(range(NT))]
    win = [(t, max(0, t - 4), min(t, 4) + 1) for t in reversed(range(NT))]
    out = [("X", *s) for s in full]
    if kind == "nsa":
        out += [("C", 0, 0, 1), ("C", 4, 0, 1)]
    return out + [("Y", *s) for s in (win if kind == "nsa" else full)]


class Seg:
    LAG = 3

    def __init__(self, kind, g, trips, before):
        self.kind, self.g, self.trips = kind, g, trips
        self.steps = steps_of(kind)
        self.L = len(self.steps)
        self.chunks = [1 if t[0] == "C" else (t[3] + 3) // 4 for t in self.steps]
        self.CH = sum(self.chunks)
        self.ends = [3, 7, 8, 9, 13, 17] if kind == "nsa" else [3, 7, 11, 15]
        self.stores = {"nsa": 1, "fox": 2, "diff": 0}[kind]
        self.loads = 128 if kind == "diff" else 96
        if before is None:
            self.step0 = self.chunk0 = self.batch0 = self.load0 = self.store0 = 0
        else:
            b = before
            self.step0, self.chunk0 = b.step0 + b.trips * b.L, b.chunk0 + b.trips * b.CH
            self.batch0, self.load0 = b.batch0 + b.trips * len(b.ends), b.load0 + b.trips * b.loads
            self.store0 = b.store0 + b.trips * b.stores

    def step(self, i, s):
        return i * self.L + (self.step0 + s + 1)

    def chunk(self, i, s, c=0):
        return i * self.CH + (self.chunk0 + sum(self.chunks[:s]) + c)

    def batch(self, i, b):
        return i * len(self.ends) + (self.batch0 + b)

    def buf(self, s):
        return s % (3 if self.L % 3 == 0 else 4)

    def run(self, eng, work, lk=None, per=0):
        for v in range(self.LAG):
            work(v, 0, False)
        if lk:
            lk.settle()
        with eng.Fori(0, self.trips - 1) as i:
            if lk:
                lk.loop(i, per)
            for v in range(self.LAG, self.LAG + self.L):
                work(v, i, False)
        if lk:
            lk.done(self.trips - 1)
        for v in range(self.LAG, self.LAG + self.L):
            work(v, self.trips - 1, True)
        if lk:
            lk.settle()


class Count:

    def __init__(self, start=0):
        self.base, self.i, self.per, self.k = start, 0, 0, 0

    def loop(self, i, per):
        self.i, self.per, self.k = i, per, 0

    def done(self, trips):
        assert self.k == self.per, (self.k, self.per)
        self.base += trips * self.per
        self.i, self.per, self.k = 0, 0, 0

    def settle(self):
        self.base, self.k = self.base + self.k, 0

    def at(self, k):
        return self.base + k if isinstance(self.i, int) else self.i * self.per + (self.base + k)

    def next(self):
        self.k += 1
        return self.at(self.k)


def program(nc, a, out):
    f32, f32r = mybir.dt.float32, mybir.dt.float32r
    u32, i32 = mybir.dt.uint32, mybir.dt.int32
    ALU, ACT, AX = mybir.AluOpType, mybir.ActivationFunctionType, mybir.AxisListType
    ts = bass.ts
    ctx = ExitStack()
    with ctx:
        BASE = 16512

        def at(name, shape, dt, off):
            return nc.alloc_sbuf_tensor_at(name, shape, dt, offset=BASE + off)

        place = [0]

        def small(name, shape, dt=f32):
            n = 4
            for s in shape[1:]:
                n *= s
            t = at(name, shape, dt, place[0])
            place[0] += (n + 31) // 32 * 32
            return t

        cst = small("cst", [P, CONSTS])

        def C(n, lo=0, hi=None):
            s, e = COL[n]
            return cst[:, s + lo:(e if hi is None else s + hi)]

        ident = C("ident")
        ones = small("ones", [P, P])
        gbias = small("gbias", [P, NGL])
        rbias = small("rbias", [P, ROUT])
        subln = small("subln", [P, HD])
        lam4 = small("lam4", [P, 4, 32])
        GL = small("GL", [P, NT, NGL])
        G24 = small("G24", [P, 24, NT])
        cum = small("cum", [P, NT, 4])
        ssq = small("ssq", [P, 40])
        rstd, nv, nz = (small(n, [P, 40]) for n in ("rstd", "nv", "nz"))
        mx = small("mx", [P, 4, 4])
        r4 = small("r4", [P, 4])
        nlam = small("nlam", [P, 4])
        LG = small("LG", [P, NT, ROUT])
        w12 = small("w12", [P, 2, NT])
        slot = small("slot", [P, 2, NT], u32)
        ids = small("ids", [P, NTILES + 1], u32)
        idc = small("idc", [P, 2], u32)
        info = small("info", [1, 16], i32)
        tmpd = small("tmpd", [P, NT, 20])
        lf, lfb = small("lf", [P, NT, 4]), small("lfb", [P, NT, 4])
        kc1, kc2 = small("kc1", [P, P], f32r), small("kc2", [P, P], f32r)
        vcm = small("vcm", [HD, 2, VW])
        KB = 1024
        assert place[0] <= 21 * KB, place[0]
        ZB, ZC, ZD, ZE = 21 * KB, 85 * KB, 110 * KB, 174 * KB
        END = 229344 - BASE

        hTh = at("hTh", [P, KC, SEQ], f32r, ZB)
        hTl = at("hTl", [P, KC, SEQ], f32r, ZB + 32 * KB)
        V = at("V", [P, 12, NT, VW], f32, ZC)
        wn = at("wn", [P, KC * WN[1]], f32, ZD)
        wnh = at("wnh", [P, KC * WN[1]], f32r, ZD + 13 * KB)
        wnl = at("wnl", [P, KC * WN[1]], f32r, ZD + 26 * KB)
        wst = at("wst", [P, 2, SEQ], f32, ZD + 39 * KB)
        wth = at("wth", [P, 2, SEQ], f32r, ZD + 47 * KB)
        wtl = at("wtl", [P, 2, SEQ], f32r, ZD + 55 * KB)
        thi = at("thi", [P, 2, SEQ], f32r, ZE)
        tlo = at("tlo", [P, 2, SEQ], f32r, ZE + 8 * KB)
        xt = at("xt", [P, NT, D], f32, ZE)
        gbc = at("gbc", [P, D], f32, ZD + 55 * KB)
        xn = at("xn", [P, 2, D], f32, ZD + 47 * KB)
        junk = at("junk", [P, D], f32, ZD + 59 * KB)

        w1 = at("w1", [P, 2, 16, 256], f32, ZD)
        w2k = at("w2k", [P, 2, P], f32, ZD + 32 * KB)
        w2v = at("w2v", [P, 2, HD], f32, ZD + 33 * KB)
        pe = at("pe", [P, 2, 16], f32, ZD + 34 * KB)
        ga = at("ga", [P, 256], f32, ZD + 35 * KB)
        gb = at("gb", [P, 256], f32, ZD + 36 * KB)
        gc = at("gc", [P, 256], f32, ZD + 37 * KB)
        hT2 = at("hT2", [P, 2, P], f32, ZD + 38 * KB)
        blk = at("blk", [P, 16, P], f32, ZE + 16 * KB)
        zh = at("zh", [P, SEQ], f32, ZE + 24 * KB)
        zl = at("zl", [P, SEQ], f32, ZE + 28 * KB)
        dg = at("dg", [P, 4, 512], f32, ZE + 24 * KB)
        qs = [at(f"qs{u}", [P, SEQ], f32r, ZB + 12 * KB * u) for u in range(2)]
        k1 = [at(f"k1{u}", [P, SEQ], f32r, ZB + 12 * KB * u + 4 * KB) for u in range(2)]
        k2 = [at(f"k2{u}", [P, SEQ], f32r, ZB + 12 * KB * u + 8 * KB) for u in range(2)]
        sp = at("sp", [P, 4, SEQ], f32, ZB + 24 * KB)
        pt = at("pt", [P, 2, SEQ], f32, ZB + 40 * KB)
        tabX = at("tabX", [P, SEQ], f32, ZB + 48 * KB)
        tabY = at("tabY", [P, SEQ], f32, ZB + 52 * KB)
        oh = at("oh", [P, 2, NT, HD], f32, ZB + 56 * KB)
        tmp = at("tmp", [P, NT, HD], f32, ZB + 60 * KB)
        FX = at("FX", [P, FOX_H, SEQ], f32, ZD)
        od = at("od", [P, NT, DIFF_H, HD], f32, ZE + 16 * KB)
        ot = at("ot", [P, 2, 6 * P], f32, ZE + 24 * KB)
        zrow = at("zrow", [P, D // 4], f32, ZE + 32 * KB)
        woh = at("woh", [P, KC, D], f32r, ZD)
        wol = at("wol", [P, KC, D], f32r, ZD + 32 * KB)
        wraw = at("wraw", [P, KC, D], f32, ZD + 32 * KB)
        oth = at("oth", [P, 2, KC, P], f32r, ZC)
        otl = at("otl", [P, 2, KC, P], f32r, ZC + 8 * KB)
        x2 = at("x2", [P, NT, D], f32, ZB)
        xr = at("xr", [P, 2, D], f32, ZB + 32 * KB)
        h2 = at("h2", [P, 2, D], f32, ZB + 40 * KB)
        h2T = at("h2T", [P, KC, P], f32, ZB + 48 * KB)
        wr = at("wr", [P, KC, ROUT], f32, ZB + 52 * KB)
        gf = at("gf", [P, D], f32, ZB + 54 * KB)
        junk2 = at("junk2", [P, D], f32, ZB + 58 * KB)
        _io = [0]

        def ri(name, shape, dt=f32):
            n = 4
            for s in shape[1:]:
                n *= s
            t = at(name, shape, dt, ZC + _io[0])
            _io[0] += (n + 31) // 32 * 32
            return t

        ra, rb, rc, rd = (ri(n, [P, NT, NE]) for n in ("ra", "rb", "rc", "rd"))
        oh1, oh2, memb = (ri(n, [P, NT, NE]) for n in ("oh1", "oh2", "memb"))
        el = ri("el", [P, NT, NE])
        s8 = ri("s8", [P, 8, NT])
        g4a, g4b = ri("g4a", [P, NT, 4]), ri("g4b", [P, NT, 4])
        mb = ri("mb", [P, NT + 1, NE])
        cntb = ri("cntb", [P, NE])
        cmp7 = ri("cmp7", [P, NE, 7])
        vt = ri("vt", [P, 2, NE])
        eb = ri("eb", [P, NE])
        cj = ri("cj", [P, 16, NE])
        ej = ri("ej", [P, 17])
        slf, shi, slo = (ri(n, [P, 2, NT]) for n in ("slf", "shi", "slo"))
        sint = ri("sint", [P, 2, NT], u32)
        in_tile = ri("in_tile", [P, 2, NT, NTILES])
        in_row = at("in_row", [P, 2, NT, P], f32, ZE + 24 * KB)
        assert _io[0] <= 25 * KB, _io[0]
        XG = at("XG", [P, 2, D], f32, ZD + 48 * KB)
        YO = at("YO", [P, 2, D], f32, ZD + 56 * KB)
        XT = at("XT", [P, 2, KC, P], f32, ZB + 56 * KB)
        ge = at("ge", [P, DE], f32, ZC)
        gd = at("gd", [P, DE], f32, ZC + KB)
        act2 = at("act2", [P, 2, DE], f32, ZC + 2 * KB)
        aT = at("aT", [P, 2, 2, P], f32, ZC + 4 * KB)
        WOFF = [ZE, ZD, ZD + 24 * KB, ZB + 32 * KB]
        wgu = [at(f"wgu{q}", [P, KC, 2 * DE], f32, o) for q, o in enumerate(WOFF)]
        wdn = [at(f"wdn{q}", [P, 2, D], f32, o + 16 * KB) for q, o in enumerate(WOFF)]
        y1 = at("y1", [P, NT, D], f32, ZD)
        y2 = at("y2", [P, NT, D], f32, ZD + 32 * KB)
        gfin = at("gfin", [P, D], f32, ZC + 12 * KB)
        junk3 = at("junk3", [P, D], f32, ZC + 16 * KB)

        PS = ctx.enter_context(nc.psum_tensor("PS", [P, 8, 512], f32))

        T_d = nc.dram_tensor("T_d", [2, 16, P, SEQ], f32).ap()
        T_r = T_d.rearrange("a g p t -> a (g p) t")
        O_d = nc.dram_tensor("O_d", [SEQ, 6 * P], f32).ap()
        O_v = O_d.rearrange("(t p) c -> p t c", p=P)
        h2_d = nc.dram_tensor("h2_d", [SEQ, D], f32).ap()
        Y_d = nc.dram_tensor("Y_d", [NROWS, D], f32).ap()

        def sem(n):
            return ctx.enter_context(nc.semaphore(n))

        const_in, tab_in, gbc_in, waited = map(sem, ("const_in", "tab_in", "gbc_in", "waited"))
        rs_l, rs_0, rs_mid, rs_done, dq_done = map(sem, ("rs_l", "rs_0", "rs_mid", "rs_done", "dq_done"))
        x_in = [sem(f"x_in{t}") for t in range(NT)]
        ss_done, xn_done, a_tr, a_hi, a_free = map(sem, ("ss_done", "xn_done", "a_tr", "a_hi", "a_free"))
        wn_in, wn_hi, wn_split, c_mm, c_free = map(sem, ("wn_in", "wn_hi", "wn_split", "c_mm", "c_free"))
        w_in = [sem(f"w_in{p}") for p in range(2)]
        t_st = [sem(f"t_st{p}") for p in range(2)]
        b_whi, b_split, b_tr, b_hi, b_free = map(sem, ("b_whi", "b_split", "b_tr", "b_hi", "b_free"))
        dve_did, act_did, pe_did, blk_zero, w1_in, z_in = map(
            sem, ("dve_did", "act_did", "pe_did", "blk_zero", "w1_in", "z_in"))
        st_in = [sem("st_inX"), sem("st_inY")]
        s_ready, mx_ready, sub_ready, t_ready, p_ready, pv_done, o_free, tab_ready, oh_ready, oh_st, link = map(
            sem, ("s_ready", "mx_ready", "sub_ready", "t_ready", "p_ready", "pv_done", "o_free", "tab_ready",
                  "oh_ready", "oh_st", "link"))
        wo_in, wo_hi, wo_lo = sem("wo_in"), sem("wo_hi"), sem("wo_lo")
        o_in = [sem(f"o_in{p}") for p in range(2)]
        r_in = [sem(f"r_in{p}") for p in range(2)]
        g_tr, g_hi, g_lo, g_mm, x2_done, h_ss, h_xn, h_tr, h_ev, h_mm, h_lg, hw_in = map(
            sem, ("g_tr", "g_hi", "g_lo", "g_mm", "x2_done", "h_ss", "h_xn", "h_tr", "h_ev", "h_mm",
                  "h_lg", "hw_in"))
        h_st = [sem(f"h_st{p}") for p in range(2)]
        yz_st, ftab_ready, o_norm = map(sem, ("yz_st", "ftab_ready", "o_norm"))
        we_in = [sem(f"we_in{q}") for q in range(4)]
        xg_in = [sem(f"xg_in{p}") for p in range(2)]
        ids_ok, idx_c, m_tr, m_x0, m_x1, m_gu, m_e, m_act, m_ta, m_aT, m_dn, m_y0, m_y1 = map(
            sem, ("ids_ok", "idx_c", "m_tr", "m_x0", "m_x1", "m_gu", "m_e", "m_act", "m_ta", "m_aT",
                  "m_dn", "m_y0", "m_y1"))
        y_st = [sem(f"y_st{p}") for p in range(2)]
        v_pe, v_act, v_dve, v_pool, v_w, v_x, v_y = map(
            sem, ("v_pe", "v_act", "v_dve", "v_pool", "v_w", "v_x", "v_y"))
        k_in = [sem(f"k_in{t}") for t in range(NT)]
        k_acc, k_ss, k_out, gfin_in = map(sem, ("k_acc", "k_ss", "k_out", "gfin_in"))
        k_st = sem("k_st")

        SEGS = []
        for kind, g, trips in (("nsa", 0, 4), ("nsa", 1, 4), ("fox", 0, 2), ("diff", 0, 4)):
            SEGS.append(Seg(kind, g, trips, SEGS[-1] if SEGS else None))
        NSTEP = {x.kind: x.L for x in SEGS}
        FOX0 = SEGS[2].step0
        ALL_STEPS = SEGS[3].step(3, 15)
        RS_D, RS_H, RS_K = 2, 3, 11
        A_BATCH = ((0, 2), (2, 6))
        K_BATCH = ((0, 4), (4, 3), (7, 1))

        class Events:

            def __init__(self, s, names):
                self.s, self.names, self.n = s, names, 0

            def of(self, name):
                return self.names.index(name) + 1

            def did(self, name, ins, eng=None):
                assert self.names[self.n] == name, (self.names[self.n], name)
                self.n += 1
                ins.then_inc(self.s, 1)
                if eng is not None:
                    eng.wait_ge(self.s, self.n)

        gelu_d = ["z0", "b0", "z1", "b1", "q", "u", "d1", "r", "h"]
        blk_d, gelu_d = ["z0", "b0", "z1", "b1"], ["q", "u", "d1", "r", "h"]
        DV = Events(dve_did, ["gl", "nz", "az", "u", "dm", "rd", "er", "g1", "g24", "gcv", "le", "mn", "lf"]
                    + [f"lb{t}" for t in range(NT)] + ["lamp0", "lamp1", "nlam", "cum"]
                    + [n + "k" for n in blk_d + gelu_d] + [n + "v" for n in blk_d] + ["dg0"]
                    + [n + "v" for n in gelu_d] + ["dg1", "dg2", "kc2k", "dg3", "dg4", "dg5", "dg6", "dg7"]
                    + ["gm", "ge1", "ge2", "gx", "g1h", "gs", "gsum", "gpen", "el", "m1", "q1", "q1i", "i1",
                       "o1", "rb", "m2", "q2", "q2i", "i2", "o2", "memb"] + [f"mb{t}" for t in range(NT + 1)] + ["md",
                       "cntb", "cmp", "v"] + [f"s{k}{c}" for k in (1, 2, 4, 8, 16) for c in "ab"]
                    + ["exc", "eb", "ra", "ge", "geb", "rae", "rs", "p1", "sl1", "r1", "sl2", "r2", "slot",
                       "sint", "shi", "slo", "in_tile", "in_tok0", "in_tok1", "in_row", "den0", "den", "w1", "w2", "cj", "ej", "ejc", "nov", "info", "ids"])
        AC = Events(act_did, ["eg", "ef", "ln", "lam", "sqk", "exk", "hTk", "sqv", "exv", "fx0", "c1k", "hTv",
                              "fx1", "fx2", "c1v", "fx3", "fx4", "fx5", "fx6", "fx7", "rge", "re2"])
        PEV = Events(pe_did, ["cum", "hk", "trk", "hv", "fx0", "ok", "trv", "fx1", "fx2", "ov", "fx3", "fx4", "fx5",
                              "fx6", "fx7", "rank", "idt"])

        def flat(b, n=2):
            return PS[:, b:b + n, :].rearrange("p b c -> p (b c)")

        def apart(eng):
            eng.sem_inc(waited, 1)

        block = ctx.enter_context(nc.Block())

        @block.sync
        def _(sp_):
            sp_.dma_start(xt[:, 0, :], a["x"][0:P, :]).then_inc(x_in[0], 16)
            sp_.dma_start(cst[:, 0:SMALL], a["consts"][:, 0:SMALL]).then_inc(const_in, 16)
            for t in range(1, NT):
                sp_.dma_start(xt[:, t, :], a["x"][t * P:(t + 1) * P, :]).then_inc(x_in[t], 16)
            sp_.dma_start(gbc[:], a["g_attn"]).then_inc(gbc_in, 16)
            sp_.dma_start(wn[:, 0:KC * WN[0]], a["wn0"]).then_inc(wn_in, 16)
            sp_.dma_start(wst[:, 0, :], a["wt"][0]).then_inc(w_in[0], 16)
            sp_.dma_start(wst[:, 1, :], a["wt"][1]).then_inc(w_in[1], 16)
            sp_.dma_start(cst[:, SMALL:CONSTS], a["consts"][:, SMALL:CONSTS]).then_inc(tab_in, 16)
            sp_.dma_start(gbias[:], a["gbias"]).then_inc(tab_in, 16)
            sp_.dma_start(rbias[:], a["rbias"]).then_inc(tab_in, 16)
            sp_.dma_start(subln[:], a["subln"]).then_inc(tab_in, 16)
            sp_.dma_start(lam4[:], a["lam"].rearrange("p (a b) -> p a b", a=4)).then_inc(tab_in, 16)
            sp_.wait_ge(wn_split, 1)
            sp_.dma_start(wn[:, 0:KC * WN[1]], a["wn1"]).then_inc(wn_in, 16)

            def store_t(g, p):
                sp_.wait_ge(b_free, 4 + 2 * g + 2)
                sp_.dma_start(T_d[0, g], thi[:, p, :].bitcast(f32)).then_inc(t_st[p], 16)
                sp_.dma_start(T_d[1, g], tlo[:, p, :].bitcast(f32)).then_inc(t_st[p], 16)

            def pair_of_groups(j):
                for p in range(2):
                    sp_.wait_ge(b_split, 2 * j + (p + 1))
                    sp_.dma_start(wst[:, p, :], a["wt"][2 * j + (p + 2)]).then_inc(w_in[p], 16)
                    store_t(2 * j + p, p)

            def load_z(kv, g):
                for part, z in enumerate((zh, zl)):
                    src = T_d[part, G_KC + kv, g * HD:(g + 1) * HD, :]
                    sp_.dma_start(z[0:HD, :], src).then_inc(z_in, 16)
                    sp_.dma_start(z[HD:P, 0:SEQ - 1], src[:, 1:SEQ]).then_inc(z_in, 16)

            pair_of_groups(0)
            sp_.wait_ge(c_free, 4 + 16)
            sp_.dma_start(w2k[:, :, 0:HD], a["w2k"].rearrange("p (c n) -> p c n", c=2)).then_inc(w1_in, 16)
            sp_.dma_start(w2k[:, :, HD:P], a["w2k"].rearrange("p (c n) -> p c n", c=2)).then_inc(w1_in, 16)
            sp_.dma_start(w2v[:], a["w2v"].rearrange("p (c n) -> p c n", c=2)).then_inc(w1_in, 16)
            sp_.dma_start(pe[:], a["pe"].rearrange("p (v c) -> p v c", v=2)).then_inc(w1_in, 16)
            for kv in range(2):
                sp_.dma_start(w1[:, kv], a["w1"][kv].rearrange("p (c n) -> p c n", c=16)).then_inc(w1_in, 16)
            sp_.wait_ge(t_st[0], 32 + 1)
            sp_.wait_ge(t_st[1], 32 + 1)
            load_z(0, 0)
            pair_of_groups(1)
            sp_.wait_ge(dve_did, DV.of("b0k"))
            load_z(0, 1)
            sp_.wait_ge(dve_did, DV.of("b1k"))
            load_z(1, 0)
            pair_of_groups(2)
            sp_.wait_ge(dve_did, DV.of("b0v"))
            load_z(1, 1)
            with sp_.Fori(3, 7) as j:
                pair_of_groups(j)
            def unit_rows(kind, g, i, u):
                if kind == "nsa":
                    return 64 * i + (G_QN * P + 256 * g), (G_KS, G_KW)[u] * P + 64 * g
                if kind == "fox":
                    return P * i + (G_QF * P + 64 * u), P * i + (G_KF * P + 64 * u)
                return HD * i + (G_QD * P + 32 * u), HD * i + (G_KD * P + 32 * u)

            def load_unit(kind, g, i, u):
                q0, k0 = unit_rows(kind, g, i, u)
                w = 32 if kind == "diff" else HD
                for b, part in enumerate((0, 1, 0, 1) if kind == "diff" else (0, 1)):
                    sp_.dma_start(qs[u][w * b:w * b + w, :].bitcast(f32), T_r[part, bass.ds(q0, w), :])\
                       .then_inc(st_in[u], 16)
                if kind == "diff":
                    for b, part in enumerate((0, 0, 1, 1)):
                        sp_.dma_start(k1[u][w * b:w * b + w, :].bitcast(f32), T_r[part, bass.ds(k0, w), :])\
                           .then_inc(st_in[u], 16)
                else:
                    for part, dst in ((0, k1), (1, k2)):
                        for b in range(2):
                            sp_.dma_start(dst[u][w * b:w * b + w, :].bitcast(f32),
                                          T_r[part, bass.ds(k0, w), :]).then_inc(st_in[u], 16)

            store_t(14, 0)
            sp_.wait_ge(t_st[1], 32 * 7 + 1)
            sp_.wait_ge(b_free, 4 + 32)
            load_unit("nsa", 0, 0, 0)
            store_t(15, 1)
            load_unit("nsa", 0, 0, 1)
            for p in range(2):
                sp_.wait_ge(t_st[p], 32 * 8 + 1)
            sp_.wait_ge(blk_zero, 3)
            for c in range(4):
                sp_.dma_start(Y_d[NE * CAP:, c * (D // 4):(c + 1) * (D // 4)].rearrange("(n p) d -> p n d", p=P),
                              zrow[:].unsqueeze(1).broadcast_to([P, MAX_OVF, D // 4])).then_inc(yz_st, 16)
            sdone, ohd = Count(), Count()

            def pair_io(kind, g, i, nxt):
                xs = 10 if kind == "nsa" else 8
                for k in range(NSTEP[kind]):
                    v = sdone.next()
                    if nxt and k == xs - 1:
                        sp_.wait_ge(s_ready, v)
                        load_unit(*nxt, 0)
                    if nxt and k == NSTEP[kind] - 1:
                        sp_.wait_ge(s_ready, v)
                        load_unit(*nxt, 1)
                for u in range({"nsa": 1, "fox": 2, "diff": 0}[kind]):
                    col = {"nsa": HD * i + 256 * g, "fox": P * i + (512 + HD * u)}[kind]
                    sp_.wait_ge(oh_ready, ohd.next())
                    sp_.dma_start(O_v[:, :, bass.ds(col, HD)], oh[:, u]).then_inc(oh_st, 16)

            for n, seg in enumerate(SEGS):
                kind, g, trips = seg.kind, seg.g, seg.trips
                with sp_.Fori(0, trips - 1) as i:
                    sdone.loop(i, NSTEP[kind])
                    ohd.loop(i, seg.stores)
                    pair_io(kind, g, i, (kind, g, i + 1))
                sdone.done(trips - 1)
                ohd.done(trips - 1)
                nxt = (SEGS[n + 1].kind, SEGS[n + 1].g, 0) if n + 1 < len(SEGS) else None
                pair_io(kind, g, trips - 1, nxt)
                sdone.settle()
                ohd.settle()
                if kind == "fox":
                    sp_.wait_ge(oh_st, 16 * 12 + 1)
                    for p in range(2):
                        sp_.dma_start(ot[:, p, :], O_d[p * P:(p + 1) * P, :]).then_inc(o_in[p], 16)
                if n == 0:
                    for c in range(4):
                        sp_.dma_start(wraw[:, 2 * c:2 * c + 2, :],
                                      a["wo"][c].rearrange("p (k n) -> p k n", k=2)).then_inc(wo_in, 16)

            def load_expert(e, q):
                sp_.dma_start(wgu[q][:], a["wgu"][e].rearrange("p (k n) -> p k n", k=KC)).then_inc(we_in[q], 16)
                sp_.dma_start(wdn[q][:], a["wdn"][e].rearrange("p (k n) -> p k n", k=2)).then_inc(we_in[q], 16)

            sp_.wait_ge(pv_done, ALL_STEPS)
            for p in range(2):
                sp_.dma_start(xr[:, p, :], a["x"][p * P:(p + 1) * P, :]).then_inc(r_in[p], 16)
            sp_.wait_ge(dq_done, 4)
            sp_.dma_start(wr[:], a["wr"].rearrange("p (k n) -> p k n", k=KC)).then_inc(hw_in, 16)
            sp_.dma_start(gf[:], a["g_ffn"]).then_inc(hw_in, 16)
            sp_.dma_start(wgu[0][:], a["wgu"][0].rearrange("p (k n) -> p k n", k=KC)).then_inc(we_in[0], 16)

            def h2_store(t, p):
                sp_.wait_ge(h_xn, t + 1)
                sp_.dma_start(h2_d[ts(t, P), :], h2[:, p, :]).then_inc(h_st[p], 16)

            with sp_.Fori(0, 3) as j:
                for p in range(2):
                    sp_.wait_ge(g_tr, 4 * j + (2 * p + 2))
                    sp_.dma_start(ot[:, p, :], O_d[ts(2 * j + (p + 2), P), :]).then_inc(o_in[p], 16)
                    sp_.wait_ge(x2_done, 4 * j + (2 * p + 2))
                    sp_.dma_start(xr[:, p, :], a["x"][ts(2 * j + (p + 2), P), :]).then_inc(r_in[p], 16)
                    h2_store(2 * j + p, p)
            for p in range(2):
                h2_store(6 + p, p)
            sp_.wait_ge(g_mm, 16)
            sp_.dma_start(wdn[0][:], a["wdn"][0].rearrange("p (k n) -> p k n", k=2)).then_inc(we_in[0], 16)
            load_expert(1, 1)
            load_expert(2, 2)
            sp_.wait_ge(h_lg, 8)
            load_expert(3, 3)
            sp_.wait_ge(dve_did, DV.of("ids"))
            sp_.dma_start(gfin[:], a["g_fin"]).then_inc(gfin_in, 16)
            with sp_.Fori(0, 7) as i:
                for q in range(4):
                    sp_.wait_ge(m_dn, 4 * i + (q + 1))
                    load_expert(4 * i + (q + 4), q)
            sp_.wait_ge(m_dn, NE - 3)
            n_ovf = sp_.value_load(info[0:1, 0:1], min_val=0, max_val=MAX_OVF)
            with sp_.Fori(0, MAX_OVF) as j:
                with sp_.If(j < n_ovf):
                    eid = sp_.value_load(info[0:1, bass.ds(j + 1, 1)], min_val=0, max_val=NE - 1)
                    sp_.wait_ge(v_y, 16 * j + 1)
                    sp_.dma_start(wgu[0][:], a["wgu"][eid].rearrange("p (k n) -> p k n", k=KC)).then_inc(v_w, 16)
                    sp_.dma_start(wdn[0][:], a["wdn"][eid].rearrange("p (k n) -> p k n", k=2)).then_inc(v_w, 16)
            for t in range(NT):
                sp_.wait_ge(k_out, t + 1)
                sp_.dma_start(out[t * P:(t + 1) * P, :], y1[:, t, :]).then_inc(k_st, 16)
            sp_.wait_ge(k_st, 16 * NT)
            for p in range(2):
                sp_.wait_ge(y_st[p], 16 * 16 + 1)

        @block.gpsimd
        def _(pool):
            pool.sem_inc(m_tr, 2)
            nc.gpsimd.memset(ones[:], 1.0).then_inc(blk_zero, 1)
            nc.gpsimd.memset(zrow[:], 0.0).then_inc(blk_zero, 1)
            nc.gpsimd.memset(V[:, :, :, HD:VW], 1.0).then_inc(blk_zero, 1)

            def newton(col, w, n, count):
                y, v, z = (b[:, col:col + w] for b in (rstd, nv, nz))

                def did(ins, k):
                    ins.then_inc(rs_mid, 1)
                    pool.wait_ge(rs_mid, 4 * count + k)
                    apart(pool)

                did(nc.gpsimd.tensor_scalar(out=v, in0=ssq[:, col:col + w], scalar1=1.0 / n, scalar2=EPS,
                                            op0=ALU.mult, op1=ALU.add), 1)
                pool.wait_ge(rs_0, count + 1)
                apart(pool)
                did(nc.gpsimd.tensor_tensor(out=z, in0=y, in1=y, op=ALU.mult), 2)
                did(nc.gpsimd.tensor_tensor(out=z, in0=z, in1=v, op=ALU.mult), 3)
                did(nc.gpsimd.tensor_scalar(out=z, in0=z, scalar1=-0.5, scalar2=1.5, op0=ALU.mult,
                                            op1=ALU.add), 4)
                nc.gpsimd.tensor_tensor(out=y, in0=y, in1=z, op=ALU.mult).then_inc(rs_done, 1)

            for b, (t, w) in enumerate(A_BATCH):
                pool.wait_ge(ss_done, t + w)
                newton(t, w, D, b)
            for n in range(2):
                pool.wait_ge(wn_hi, n + 1)
                nc.gpsimd.tensor_tensor(out=wnl[:, 0:KC * WN[n]], in0=wn[:, 0:KC * WN[n]],
                                        in1=wnh[:, 0:KC * WN[n]].bitcast(f32), op=ALU.subtract)\
                  .then_inc(wn_split, 1)
            nc.gpsimd.memset(vcm[:], 1.0).then_inc(blk_zero, 1)
            pool.wait_ge(xn_done, NT)
            nc.gpsimd.memset(blk[:], 0.0).then_inc(blk_zero, 1)
            pool.wait_ge(b_free, 4 + 32)
            pool.wait_ge(tab_in, 16 * 5)
            with pool.Fori(0, 2) as i:
                for s, (u, t, _, nk) in enumerate(steps_of("fox")):
                    tab, L = (tabX, tabY)[s % 2], nk * P
                    pool.wait_ge(ftab_ready, 16 * i + (s + 1))
                    apart(pool)
                    nc.gpsimd.affine_select(out=tab[:, L - P:L], in_=tab[:, L - P:L],
                                            compare_op=ALU.is_ge, fill=NEG, base=0, pattern=[[-1, P]],
                                            channel_multiplier=1).then_inc(tab_ready, 1)
            for n, c in enumerate((2, 3, 0, 1)):
                pool.wait_ge(wo_hi, n + 1)
                nc.gpsimd.tensor_tensor(out=wol[:, 2 * c:2 * c + 2, :], in0=wraw[:, 2 * c:2 * c + 2, :],
                                        in1=woh[:, 2 * c:2 * c + 2, :].bitcast(f32), op=ALU.subtract)\
                  .then_inc(wo_lo, 1)

            pool.wait_ge(dq_done, 4)
            newton(8, 32, HD, RS_D)
            for t in range(NT):
                pool.wait_ge(h_ss, t + 1)
                newton(2 + t, 1, D, RS_H + t)
            pool.wait_ge(dve_did, DV.of("ids"))
            for p in range(2):
                pool.wait_ge(h_st[p], 16 * NT // 2)

            def gather(n, p, into, got):
                nc.gpsimd.tensor_copy(out=idc[:, p:p + 1], in_=ids[:, bass.ds(n, 1)]).then_inc(idx_c, 1)

            with pool.Fori(0, NE // 2) as j:
                for p in range(2):
                    n = 2 * j + p
                    pool.wait_ge(m_tr, n + 1)
                    gather(n, p, None, None)
                    pool.wait_ge(idx_c, n + 1)
                    apart(pool)
                    pool.indirect_dma_start(
                        out=XG[:, p, :], out_offset=None, in_=h2_d,
                        in_offset=bass.IndirectOffsetOnAxis(ap=idc[:, p:p + 1], axis=0)).then_inc(xg_in[p], 16)
            pool.wait_ge(m_tr, 2 + NE - 1)
            n_ovf = pool.value_load(info[0:1, 0:1], min_val=0, max_val=MAX_OVF)
            with pool.Fori(0, MAX_OVF) as j:
                with pool.If(j < n_ovf):
                    pool.wait_ge(v_y, 16 * j + 1)
                    nc.gpsimd.tensor_copy(out=idc[:, 0:1], in_=ids[:, bass.ds(j + NE, 1)]).then_inc(v_pool, 1)
                    pool.wait_ge(v_pool, j + 1)
                    apart(pool)
                    pool.indirect_dma_start(
                        out=XG[:, 0, :], out_offset=None, in_=h2_d,
                        in_offset=bass.IndirectOffsetOnAxis(ap=idc[:, 0:1], axis=0)).then_inc(v_x, 16)
            for p in range(2):
                pool.wait_ge(y_st[p], 16 * 16 + 1)
            pool.wait_ge(yz_st, 16 * 4)
            pool.wait_ge(v_y, 16 * n_ovf + 1)
            apart(pool)
            for t in range(NT):
                for k, dst in enumerate((y1, y2)):
                    pool.indirect_dma_start(
                        out=dst[:, t, :], out_offset=None, in_=Y_d,
                        in_offset=bass.IndirectOffsetOnAxis(ap=slot[:, k, t:t + 1], axis=0))\
                        .then_inc(k_in[t], 16)
            for b, (t, w) in enumerate(K_BATCH):
                pool.wait_ge(k_ss, t + w)
                newton(t, w, D, RS_K + b)

        @block.scalar
        def _(act):
            def copy(o, i, **kw):
                return nc.scalar.activation(o, i, ACT.Identity, **kw)

            def inv_sqrt(col, w, n, count):
                y = rstd[:, col:col + w]
                nc.scalar.activation(y, ssq[:, col:col + w], ACT.Ln, scale=1.0 / n, bias=C("eps")).then_inc(rs_l, 1)
                act.wait_ge(rs_l, count + 1)
                nc.scalar.activation(y, y, ACT.Exp, scale=-0.5).then_inc(rs_0, 1)

            def split_hi(n):
                act.wait_ge(wn_in, 16 * (n + 1))
                copy(wnh[:, 0:KC * WN[n]], wn[:, 0:KC * WN[n]]).then_inc(wn_hi, 1)

            act.sem_inc(c_free, 4)
            act.wait_ge(const_in, 16)
            act.sem_inc(p_ready, 2)
            act.sem_inc(v_y, 1)
            for p in range(2):
                act.sem_inc(t_st[p], 1)
                act.sem_inc(y_st[p], 1)
            for b, (t0, w) in enumerate(A_BATCH):
                for t in range(t0, t0 + w):
                    act.wait_ge(x_in[t], 16)
                    if t:
                        act.wait_ge(ss_done, t)
                    nc.scalar.activation(junk[:], xt[:, t, :], ACT.Square, accum_out=ssq[:, t:t + 1])\
                      .then_inc(ss_done, 1)
                act.wait_ge(ss_done, t0 + w)
                inv_sqrt(t0, w, D, b)
            split_hi(0)
            with act.Fori(0, 4) as j:
                for p in range(2):
                    for c in range(2):
                        act.wait_ge(a_tr, 4 * j + (2 * p + c + 1))
                        apart(act)
                        copy(hTh[:, 4 * c:4 * c + 4, ts(2 * j + p, P)],
                             PS[:, 2 * p + c, :].rearrange("p (k t) -> p k t", k=4)).then_inc(a_hi, 1)

            def project_copy(h):
                for t in range(NT):
                    act.wait_ge(c_mm, NT * h + t + 1)
                    b = 4 + t % 4
                    ins = copy(V[:, 6 * h:6 * h + 6, t, 0:HD],
                               PS[:, b, 0:384].rearrange("p (h d) -> p h d", h=6))
                    if h:
                        ins = copy(GL[:, t, :], PS[:, b, 384:412])
                    ins.then_inc(c_free, 1)

            def w_hi(g, p, k):
                act.wait_ge(w_in[p], k)
                copy(wth[:, p, :], wst[:, p, :]).then_inc(b_whi, 1)

            def t_hi(g, p, j):
                act.wait_ge(t_st[p], 32 * j + 1)
                for h in range(2):
                    act.wait_ge(b_tr, 2 * g + (h + 1))
                    apart(act)
                    nc.scalar.activation(thi[:, p, h * 512:(h + 1) * 512], PS[:, 2 * p + h, :], ACT.Identity,
                                         scale=cst[:, bass.ds(g + COL["scale"][0], 1)]).then_inc(b_hi, 1)

            w_hi(0, 0, 16)
            project_copy(0)
            split_hi(1)
            w_hi(1, 1, 16)

            def pair_of_groups(j):
                for p in range(2):
                    t_hi(2 * j + p, p, j)
                    w_hi(2 * j + (p + 2), p, 16 * j + 32)

            pair_of_groups(0)
            project_copy(1)
            act.wait_ge(dve_did, DV.of("gl"))
            AC.did("eg", nc.scalar.activation(G24[:].rearrange("p c t -> p t c"), GL[:, :, 0:24], ACT.Exp,
                                              scale=-1.0))
            act.wait_ge(dve_did, DV.of("az"))
            AC.did("ef", nc.scalar.activation(tmpd[:, :, 4:8], tmpd[:, :, 0:4], ACT.Exp, scale=-1.0))
            act.wait_ge(dve_did, DV.of("u"))
            AC.did("ln", nc.scalar.activation(tmpd[:, :, 16:20], tmpd[:, :, 8:12], ACT.Ln))
            act.wait_ge(dve_did, DV.of("lamp1"))
            AC.did("lam", nc.scalar.activation(nlam[:, 2:4], nlam[:, 0:2], ACT.Exp))

            def gelu_exp(n):
                act.wait_ge(pe_did, PEV.of("h" + n))
                AC.did("sq" + n, nc.scalar.activation(ga[:], PS[:, 4, 0:256], ACT.Square))
                act.wait_ge(dve_did, DV.of("u" + n))
                AC.did("ex" + n, nc.scalar.activation(gc[:], gb[:], ACT.Exp, scale=-1.5957691216057308))

            def hidden_T(n):
                act.wait_ge(pe_did, PEV.of("tr" + n))
                AC.did("hT" + n, copy(hT2[:].rearrange("p c m -> p (c m)"), PS[:, 5, 0:256]))

            def spread(*ns):
                for n in ns:
                    act.wait_ge(pe_did, PEV.of(f"fx{n}"))
                    AC.did(f"fx{n}", copy(FX[:, n // 2, (n % 2) * 512:(n % 2) * 512 + 512],
                                          PS[:, (7, 4)[n % 2], :], scale=-1.0))

            pair_of_groups(1)
            pair_of_groups(2)
            gelu_exp("k")
            pair_of_groups(3)
            hidden_T("k")
            gelu_exp("v")
            spread(0)
            pair_of_groups(4)
            act.wait_ge(pe_did, PEV.of("ok"))
            AC.did("c1k", copy(kc1[:], PS[:, 6, 0:P]))
            hidden_T("v")
            spread(1, 2)
            pair_of_groups(5)
            act.wait_ge(pe_did, PEV.of("ov"))
            act.wait_ge(blk_zero, 5)
            AC.did("c1v", copy(vcm[:, :, 0:HD], PS[0:HD, 6, 0:P].rearrange("p (g d) -> p g d", g=2)))
            spread(3, 4)
            pair_of_groups(6)
            spread(5, 6)
            t_hi(14, 0, 7)
            t_hi(15, 1, 7)
            spread(7)

            def exps(seg, s, i):
                u, t, k0, nk = seg.steps[s]
                head = {"nsa": i + 4 * seg.g, "fox": None, "diff": i + NSA_H}[seg.kind]
                sc = lambda n: 1.0 if head is None else C("slopes")[0:n, bass.ds(head, 1)]
                for c in range(seg.chunks[s]):
                    bank = 4 + (sum(seg.chunks[:s]) + c) % 2
                    act.wait_ge(t_ready, seg.chunk(i, s, c) + 1)
                    apart(act)
                    if u == "C":
                        ins = nc.scalar.activation(pt[0:HD, s % 2, 0:512], PS[0:HD, bank, :], ACT.Exp, scale=sc(HD))
                    else:
                        w = min(4, nk - 4 * c) * P
                        ins = nc.scalar.activation(pt[:, s % 2, 4 * c * P:4 * c * P + w], PS[:, bank, 0:w],
                                                   ACT.Exp, scale=sc(P))
                    ins.then_inc(p_ready, 1)

            def fox_table(s, i):
                u, t, _, nk = steps_of("fox")[s]
                copy((tabX, tabY)[s % 2][:, 0:nk * P],
                     FX[:, bass.ds(2 * i + "XY".index(u), 1), 0:nk * P].rearrange("p o k -> p (o k)"),
                     bias=cum[:, t, bass.ds(2 * i + "XY".index(u), 1)]).then_inc(ftab_ready, 1)

            def wo_high(c):
                act.wait_ge(wo_in, 16 * 4)
                copy(woh[:, 2 * c:2 * c + 2, :], wraw[:, 2 * c:2 * c + 2, :]).then_inc(wo_hi, 1)

            for n, seg in enumerate(SEGS):
                if seg.kind == "fox":
                    act.wait_ge(mx_ready, FOX0)
                    for s in range(2):
                        fox_table(s, 0)

                def work(v, i, last):
                    if v < 2:
                        return
                    if seg.kind == "fox" and (v < seg.L or not last):
                        act.wait_ge(mx_ready, seg.step(i, v - 2))
                        apart(act)
                        fox_table(v % seg.L, i + v // seg.L)
                    s = v - 2
                    if s < seg.L or not last:
                        exps(seg, s % seg.L, i + s // seg.L)

                seg.run(act, work)
                if n == 1:
                    wo_high(2)
                    wo_high(3)
                if n == 2:
                    wo_high(0)
                    wo_high(1)
            act.wait_ge(dq_done, 4)
            inv_sqrt(8, 32, HD, RS_D)

            def o_high(t, p):
                for c in range(2):
                    act.wait_ge(g_tr, 2 * t + (c + 1))
                    copy(oth[:, p, 4 * c:4 * c + 4, :].rearrange("p k t -> p (k t)"), PS[:, c, :]).then_inc(g_hi, 1)

            def sumsq(t):
                act.wait_ge(x2_done, 2 * t + 2)
                nc.scalar.activation(junk2[:], x2[:, t, :], ACT.Square, accum_out=ssq[:, 2 + t:3 + t])\
                  .then_inc(h_ss, 1)
                act.wait_ge(h_ss, t + 1)
                inv_sqrt(2 + t, 1, D, RS_H + t)

            def hT_copy(t):
                for c in range(2):
                    act.wait_ge(h_tr, 2 * t + c + 1)
                    copy(h2T[:, 4 * c:4 * c + 4, :].rearrange("p k t -> p (k t)"), PS[:, 4 + c, :]).then_inc(h_ev, 1)

            o_high(0, 0)
            for t in range(NT):
                if t + 1 < NT:
                    o_high(t + 1, (t + 1) % 2)
                if t:
                    hT_copy(t - 1)
                sumsq(t)
            hT_copy(NT - 1)
            act.wait_ge(dve_did, DV.of("gs"))
            AC.did("rge", nc.scalar.activation(rb[:, :, 0:4], ra[:, :, 0:4], ACT.Exp))
            act.wait_ge(dve_did, DV.of("md"))
            AC.did("re2", nc.scalar.activation(s8[:, 7, :], s8[:, 7, :], ACT.Exp))

            def m_x(n, p):
                act.wait_ge(m_tr, n + 3)
                copy(XT[:, p, 0:4, :].rearrange("p k t -> p (k t)"), PS[:, 0, :]).then_inc(m_x0, 1)

            def m_exp(n, p):
                act.wait_ge(m_gu, n + 1)
                act.wait_ge(m_act, n)
                nc.scalar.activation(ge[:], PS[:, 2 + p, 0:DE], ACT.Exp, scale=-1.0).then_inc(m_e, 1)

            def m_at(n, p):
                act.wait_ge(m_ta, n + 1)
                copy(aT[:, p].rearrange("p c t -> p (c t)"), PS[:, 4, 0:DE]).then_inc(m_aT, 1)

            def m_out(n, p, k):
                act.wait_ge(m_dn, n + 1)
                act.wait_ge(y_st[p], 16 * k + 1)
                copy(YO[:, p, 0:512], PS[:, 5, :]).then_inc(m_y0, 1)
                act.wait_ge(m_y0, n + 2)
                act.wait_ge(m_y1, n + 2)
                act.dma_start(Y_d[ts(n, P), :], YO[:, p, :]).then_inc(y_st[p], 16)

            def m_slot(n, p, k, before=True, after=True):
                m_exp(n, p)
                if before:
                    m_at(n - 1, 1 - p)
                if after:
                    m_x(n + 1, 1 - p)
                if before:
                    m_out(n - 1, 1 - p, k)

            m_x(0, 0)
            m_slot(0, 0, 0, before=False)
            with act.Fori(0, 7) as i:
                for q in range(1, 5):
                    m_slot(4 * i + q, q % 2, 2 * i + (q - 1) // 2)
            for q in range(1, 4):
                m_slot(28 + q, q % 2, 14 + (q - 1) // 2, after=q < 3)
            m_at(31, 1)
            m_out(31, 1, 15)
            act.wait_ge(m_dn, NE)
            act.wait_ge(yz_st, 16 * 4)
            act.wait_ge(y_st[0], 16 * NE // 2 + 1)
            n_ovf = act.value_load(info[0:1, 0:1], min_val=0, max_val=MAX_OVF)
            with act.Fori(0, MAX_OVF) as j:
                with act.If(j < n_ovf):
                    act.wait_ge(v_pe, 4 * j + 1)
                    copy(XT[:, 0, 0:4, :].rearrange("p k t -> p (k t)"), PS[:, 0, :]).then_inc(v_act, 1)
                    act.wait_ge(v_pe, 4 * j + 2)
                    nc.scalar.activation(ge[:], PS[:, 2, 0:DE], ACT.Exp, scale=-1.0).then_inc(v_act, 1)
                    act.wait_ge(v_pe, 4 * j + 3)
                    copy(aT[:, 0].rearrange("p c t -> p (c t)"), PS[:, 4, 0:DE]).then_inc(v_act, 1)
                    act.wait_ge(v_pe, 4 * j + 4)
                    copy(YO[:, 0, 0:512], PS[:, 5, :]).then_inc(v_act, 1)
                    act.wait_ge(v_act, 4 * j + 4)
                    act.wait_ge(v_dve, 6 * j + 6)
                    act.dma_start(Y_d[ts(j + NE, P), :], YO[:, 0, :]).then_inc(v_y, 16)
            for b, (t0, w) in enumerate(K_BATCH):
                for t in range(t0, t0 + w):
                    act.wait_ge(k_acc, t + 1)
                    if t:
                        act.wait_ge(k_ss, t)
                    nc.scalar.activation(junk3[:], x2[:, t, :], ACT.Square, accum_out=ssq[:, t:t + 1])\
                      .then_inc(k_ss, 1)
                act.wait_ge(k_ss, t0 + w)
                inv_sqrt(t0, w, D, RS_K + b)

        @block.vector
        def _(dve):
            V_ = nc.vector
            lk = Count()

            def chain(ins):
                v = lk.next()
                ins.then_inc(link, 1)
                dve.wait_ge(link, v)

            dve.sem_inc(a_free, 4)
            dve.sem_inc(b_free, 4)
            dve.sem_inc(o_free, 2)
            dve.sem_inc(oh_st, 1)
            dve.sem_inc(m_y0, 1)
            dve.sem_inc(m_y1, 1)
            dve.wait_ge(gbc_in, 16)
            for t in range(NT + 1):
                if t < NT:
                    dve.wait_ge(rs_done, 1 + sum(t >= x for x, _ in A_BATCH[1:]))
                    if t >= 2:
                        dve.wait_ge(a_tr, 2 * t - 2)
                    V_.scalar_tensor_tensor(out=xn[:, t % 2, :], in0=xt[:, t, :], scalar=rstd[:, t:t + 1],
                                            in1=gbc[:], op0=ALU.mult, op1=ALU.mult).then_inc(xn_done, 1)
                if t:
                    for c in range(2):
                        dve.wait_ge(a_hi, 2 * t - 1 + c)
                        o = (slice(None), slice(4 * c, 4 * c + 4), slice((t - 1) * P, t * P))
                        V_.tensor_tensor(out=hTl[o], in0=PS[:, 2 * ((t - 1) % 2) + c, :].rearrange(
                            "p (k t) -> p k t", k=4), in1=hTh[o].bitcast(f32), op=ALU.subtract).then_inc(a_free, 1)

            def w_lo(g, p):
                dve.wait_ge(b_whi, g + 1)
                V_.tensor_tensor(out=wtl[:, p, :], in0=wst[:, p, :], in1=wth[:, p, :].bitcast(f32),
                                 op=ALU.subtract).then_inc(b_split, 1)

            def t_lo(g, p):
                for h in range(2):
                    dve.wait_ge(b_hi, 2 * g + (h + 1))
                    V_.scalar_tensor_tensor(out=tlo[:, p, h * 512:(h + 1) * 512], in0=PS[:, 2 * p + h, :],
                                            scalar=cst[:, bass.ds(g + COL["scale"][0], 1)],
                                            in1=thi[:, p, h * 512:(h + 1) * 512].bitcast(f32),
                                            op0=ALU.mult, op1=ALU.subtract).then_inc(b_free, 1)

            w_lo(0, 0)
            w_lo(1, 1)

            def pair_of_groups(j):
                for p in range(2):
                    t_lo(2 * j + p, p)
                    w_lo(2 * j + (p + 2), p)

            pair_of_groups(0)
            dve.wait_ge(c_free, 4 + 16)
            dve.wait_ge(tab_in, 16 * 5)
            D_ = lambda n, ins: DV.did(n, ins, dve)
            D_("gl", V_.tensor_tensor(out=GL[:], in0=GL[:], in1=gbias[:].unsqueeze(1).broadcast_to([P, NT, NGL]),
                                      op=ALU.add))
            z = GL[:, :, 24:28]
            td = lambda k: tmpd[:, :, 4 * k:4 * k + 4]
            D_("nz", V_.tensor_scalar(out=td(0), in0=z, scalar1=-1.0, scalar2=None, op0=ALU.mult))
            D_("az", V_.tensor_tensor(out=td(0), in0=td(0), in1=z, op=ALU.max))
            dve.wait_ge(act_did, AC.of("ef"))
            D_("u", V_.tensor_scalar(out=td(2), in0=td(1), scalar1=1.0, scalar2=None, op0=ALU.add))
            D_("dm", V_.tensor_scalar(out=td(3), in0=td(2), scalar1=-1.0, scalar2=1e-30, op0=ALU.add, op1=ALU.max))
            D_("rd", V_.reciprocal(out=td(3), in_=td(3)))
            D_("er", V_.tensor_tensor(out=td(3), in0=td(3), in1=td(1), op=ALU.mult))
            D_("g1", V_.tensor_scalar(out=G24[:], in0=G24[:], scalar1=1.0, scalar2=None, op0=ALU.add))
            D_("g24", V_.reciprocal(out=G24[:], in_=G24[:]))
            g24c = G24[:].rearrange("p (h b) t -> p h b t", b=3)[:, :, 0, :]
            D_("gcv", V_.tensor_tensor(out=g24c, in0=g24c, in1=C("cvalid").unsqueeze(1).broadcast_to([P, NSA_H, NT]),
                                       op=ALU.mult))
            dve.wait_ge(act_did, AC.of("ln"))
            D_("le", V_.tensor_tensor(out=td(3), in0=td(3), in1=td(4), op=ALU.mult))
            D_("mn", V_.tensor_scalar(out=td(0), in0=z, scalar1=0.0, scalar2=None, op0=ALU.min))
            D_("lf", V_.tensor_tensor(out=lf[:], in0=td(0), in1=td(3), op=ALU.subtract))
            D_("lb0", V_.tensor_scalar(out=lfb[:, 0], in0=lf[:, 0], scalar1=0.0, scalar2=None, op0=ALU.mult))
            for t in range(1, NT):
                D_(f"lb{t}", V_.tensor_tensor(out=lfb[:, t], in0=lfb[:, t - 1], in1=lf[:, t - 1], op=ALU.add))
            for k in range(2):
                D_(f"lamp{k}", V_.tensor_tensor_reduce(out=ga[:, 0:32], in0=lam4[:, 2 * k, :],
                                                       in1=lam4[:, 2 * k + 1, :], scale=1.0, scalar=0.0,
                                                       op0=ALU.mult, op1=ALU.add, accum_out=nlam[:, k:k + 1]))
            dve.wait_ge(act_did, AC.of("lam"))
            D_("nlam", V_.scalar_tensor_tensor(out=nlam[:, 0:1], in0=nlam[:, 3:4], scalar=LAM_INIT,
                                               in1=nlam[:, 2:3], op0=ALU.subtract, op1=ALU.subtract))
            pair_of_groups(1)
            dve.wait_ge(pe_did, PEV.of("cum"))
            D_("cum", V_.tensor_copy(out=cum[:].rearrange("p t f -> p (t f)"), in_=PS[:, 7, 0:32]))

            def build_blocks(kv, n):
                for g in range(2):
                    dve.wait_ge(z_in, 64 * (2 * kv + g + 1))
                    D_(f"z{g}" + n, V_.tensor_tensor(out=zh[:, 0:SEQ - 1], in0=zh[:, 0:SEQ - 1],
                                                     in1=zl[:, 0:SEQ - 1], op=ALU.add))
                    zv = zh[:].rearrange("p (m s two) -> p s two m", s=8, two=2)
                    for b in range(2):
                        ins = V_.tensor_tensor(
                            out=blk[:, 8 * b:8 * b + 8, g * HD:g * HD + NCMP], in0=zv[:, :, 0, b:b + NCMP],
                            in1=pe[:, kv, 8 * b:8 * b + 8].unsqueeze(2).broadcast_to([P, 8, NCMP]), op=ALU.add)
                    D_(f"b{g}" + n, ins)

            def gelu(n):
                dve.wait_ge(act_did, AC.of("sq" + n))
                D_("q" + n, V_.tensor_scalar(out=gb[:], in0=ga[:], scalar1=0.044715, scalar2=1.0, op0=ALU.mult,
                                             op1=ALU.add))
                D_("u" + n, V_.tensor_tensor(out=gb[:], in0=gb[:], in1=PS[:, 4, 0:256], op=ALU.mult))
                dve.wait_ge(act_did, AC.of("ex" + n))
                D_("d1" + n, V_.tensor_scalar(out=gc[:], in0=gc[:], scalar1=1.0, scalar2=None, op0=ALU.add))
                D_("r" + n, V_.reciprocal(out=gc[:], in_=gc[:]))
                D_("h" + n, V_.tensor_tensor(out=ga[:], in0=gc[:], in1=PS[:, 4, 0:256], op=ALU.mult))

            dve.wait_ge(w1_in, 16 * 6)
            dve.wait_ge(blk_zero, 5)
            build_blocks(0, "k")
            pair_of_groups(2)
            gelu("k")
            dve.wait_ge(pe_did, PEV.of("hk"))
            build_blocks(1, "v")

            def diagonal(*ns):
                for n in ns:
                    f, h = n // 2, n % 2
                    if n >= 4:
                        dve.wait_ge(pe_did, PEV.of(f"fx{n - 4}"))
                    D_(f"dg{n}", V_.tensor_tensor(
                        out=dg[:, n % 4].rearrange("p (t c) -> p t c", t=4),
                        in0=ident.unsqueeze(1).broadcast_to([P, 4, P]),
                        in1=cum[:, 4 * h:4 * h + 4, f].unsqueeze(2).broadcast_to([P, 4, P]), op=ALU.mult))

            diagonal(0)
            pair_of_groups(3)
            gelu("v")
            diagonal(1, 2)
            pair_of_groups(4)
            dve.wait_ge(act_did, AC.of("c1k"))
            D_("kc2k", V_.tensor_tensor(out=kc2[:], in0=PS[:, 6, 0:P], in1=kc1[:].bitcast(f32), op=ALU.subtract))
            diagonal(3, 4)
            pair_of_groups(5)
            diagonal(5, 6)
            pair_of_groups(6)
            diagonal(7)
            t_lo(14, 0)
            t_lo(15, 1)

            def softmax_step(seg, s, i):
                kind = seg.kind
                u, t, k0, nk = seg.steps[s]
                if kind == "fox":
                    dve.wait_ge(tab_ready, 16 * i + (s + 1))
                dve.wait_ge(s_ready, seg.step(i, s))
                apart(dve)
                b, bank = seg.buf(s), 2 * (s % 2)
                if u == "C":
                    sv = sp[:, b, 0:256].rearrange("p (t c) -> p t c", t=4)
                    chain(V_.tensor_tensor(out=sp[:, b, 0:256], in0=PS[:, bank, 0:256],
                                           in1=C("distc", HD * t, HD * t + 256), op=ALU.add))
                    V_.tensor_reduce(out=mx[:, b, :], in_=sv, axis=AX.X, op=ALU.max).then_inc(mx_ready, 1)
                    return
                L = nk * P
                if kind == "fox":
                    tab = (tabX, tabY)[s % 2][:, 0:L]
                elif kind == "nsa" and u == "Y":
                    off = P * (4 - min(t, 4))
                    tab = C("distw", off, off + L)
                else:
                    tab = C("dist", (NT - 1 - t) * P, (NT - 1 - t) * P + L)
                V_.tensor_tensor_reduce(out=sp[:, b, 0:L], in0=flat(bank)[:, 0:L], in1=tab, scale=1.0,
                                        scalar=-3e38, op0=ALU.add, op1=ALU.max,
                                        accum_out=mx[:, b, 0:1]).then_inc(mx_ready, 1)

            def subtract(seg, s, i):
                u, t, k0, nk = seg.steps[s]
                b = seg.buf(s)
                dve.wait_ge(mx_ready, seg.step(i, s))
                if u == "C":
                    apart(dve)
                    sv = sp[:, b, 0:256].rearrange("p (t c) -> p t c", t=4)
                    V_.tensor_tensor(out=sv, in0=sv, in1=mx[:, b, :].unsqueeze(2).broadcast_to([P, 4, HD]),
                                     op=ALU.subtract).then_inc(sub_ready, 1)
                    return
                L = nk * P
                V_.tensor_scalar(out=sp[:, b, 0:L], in0=sp[:, b, 0:L], scalar1=mx[:, b, 0:1],
                                 scalar2=None, op0=ALU.subtract).then_inc(sub_ready, 1)

            def out_batch(seg, i, b):
                kind, g = seg.kind, seg.g
                unit = ("XCY" if kind == "nsa" else "XY")[b // 2]
                if unit == "C":
                    t4 = 4 * (b % 2)
                else:
                    t4 = 4 - 4 * (b % 2)
                bank = 6 + b % 2
                dve.wait_ge(pv_done, seg.step(i, seg.ends[b]))
                o = PS[:, bank, 0:4 * VW].rearrange("p (j c) -> p j c", c=VW)
                chain(V_.reciprocal(out=r4[:].unsqueeze(2), in_=o[:, :, HD:VW]))
                if kind == "nsa":
                    br = "CXY".index(unit)
                    gate = G24[:].rearrange("p c t -> p (c t)")[:, bass.ds(24 * i + (96 * g + 8 * br + t4), 4)]
                    chain(V_.tensor_tensor(out=r4[:], in0=r4[:], in1=gate, op=ALU.mult))
                rb_ = r4[:].unsqueeze(2).broadcast_to([P, 4, HD])
                if kind == "nsa":
                    dst = oh[:, 0, t4:t4 + 4, :]
                    into = dst if unit == "X" else tmp[:, t4:t4 + 4, :]
                else:
                    u = "XY".index(unit)
                    into = oh[:, u, t4:t4 + 4, :] if kind == "fox" else (tmp[:, t4:t4 + 4, :] if u else
                                                                         oh[:, 1, t4:t4 + 4, :])
                V_.tensor_tensor(out=into, in0=o[:, :, 0:HD], in1=rb_, op=ALU.mult).then_inc(o_free, 1)
                dve.wait_ge(o_free, seg.batch(i, b) + 3)
                if kind == "nsa" and unit != "X":
                    chain(V_.tensor_tensor(out=dst, in0=dst, in1=into, op=ALU.add))
                if b == 5 or kind == "fox" and t4 == 0:
                    dve.sem_inc(oh_ready, 1)

            def diff_end(i):
                chain(V_.scalar_tensor_tensor(out=tmp[:], in0=tmp[:], scalar=nlam[:, 0:1], in1=oh[:, 1],
                                              op0=ALU.mult, op1=ALU.add))
                V_.scalar_tensor_tensor(out=od[:, :, bass.ds(i, 1), :].rearrange("p t o d -> p t (o d)"), in0=tmp[:],
                                        scalar=1.0 - LAM_INIT, in1=subln[:].unsqueeze(1).broadcast_to([P, NT, HD]),
                                        op0=ALU.mult, op1=ALU.mult)
                chain(V_.tensor_tensor(out=oh[:, 1], in0=tmp[:], in1=tmp[:], op=ALU.mult))
                V_.tensor_reduce(out=ssq[:, bass.ds(8 * i + 8, 8)], in_=oh[:, 1], axis=AX.X, op=ALU.add)\
                  .then_inc(dq_done, 1)
                dve.wait_ge(dq_done, i + 1)

            for seg in SEGS:
                def work(v, i, last):
                    if v < seg.L or not last:
                        softmax_step(seg, v % seg.L, i + v // seg.L)
                    s = v - 1
                    if s >= 0 and (s < seg.L or not last):
                        subtract(seg, s % seg.L, i + s // seg.L)
                    for b, e in enumerate(seg.ends):
                        if v == min(e + 4, seg.L + 2):
                            if b == 0:
                                dve.wait_ge(oh_st, 16 * seg.stores * i + (16 * seg.store0 + 1))
                            out_batch(seg, i, b)
                    if v == seg.L + 2 and seg.kind == "diff":
                        diff_end(i)

                seg.run(dve, work, lk, {"nsa": 18, "fox": 4, "diff": 6}[seg.kind])

            dve.wait_ge(rs_done, RS_D + 1)
            for t in range(NT):
                V_.tensor_tensor(out=od[:, t], in0=od[:, t], in1=rstd[:, 8 + t:40:8].unsqueeze(2)
                                 .broadcast_to([P, 4, HD]), op=ALU.mult).then_inc(o_norm, 1)

            def o_lo(t, p):
                for c in range(2):
                    dve.wait_ge(g_hi, 2 * t + c + 1)
                    V_.tensor_tensor(out=otl[:, p, 4 * c:4 * c + 4, :].rearrange("p k t -> p (k t)"),
                                     in0=PS[:, c, :],
                                     in1=oth[:, p, 4 * c:4 * c + 4, :].rearrange("p k t -> p (k t)").bitcast(f32),
                                     op=ALU.subtract).then_inc(g_lo, 1)

            def normalise(t):
                dve.wait_ge(rs_done, RS_H + t + 1)
                if t >= 2:
                    dve.wait_ge(h_st[t % 2], 16 * (t // 2))
                dve.wait_ge(hw_in, 32)
                V_.scalar_tensor_tensor(out=h2[:, t % 2, :], in0=x2[:, t, :], scalar=rstd[:, 2 + t:3 + t],
                                        in1=gf[:], op0=ALU.mult, op1=ALU.mult).then_inc(h_xn, 1)

            def logits(t):
                dve.wait_ge(h_mm, t + 1)
                V_.tensor_tensor(out=LG[:, t, :], in0=PS[:, 6, 0:ROUT], in1=rbias[:], op=ALU.add).then_inc(h_lg, 1)

            o_lo(0, 0)
            for t in range(NT):
                if t >= 1:
                    normalise(t - 1)
                dve.wait_ge(r_in[t % 2], 16 * (t // 2 + 1))
                for h in range(2):
                    if h and t >= 2:
                        logits(t - 2)
                    dve.wait_ge(g_mm, 2 * t + h + 1)
                    V_.tensor_tensor(out=x2[:, t, h * 512:h * 512 + 512], in0=PS[:, 2 + h, :],
                                     in1=xr[:, t % 2, h * 512:h * 512 + 512], op=ALU.add).then_inc(x2_done, 1)
                if t + 1 < NT:
                    o_lo(t + 1, (t + 1) % 2)
            logits(NT - 2)
            normalise(NT - 1)
            logits(NT - 1)
            dve.wait_ge(h_lg, NT)

            bc = lambda x, w: x.unsqueeze(2).broadcast_to([P, NT, w])
            tt = lambda n, o, i0, i1, op: D_(n, V_.tensor_tensor(out=o, in0=i0, in1=i1, op=op))
            red = lambda n, o, i0, op: D_(n, V_.tensor_reduce(out=o, in_=i0, axis=AX.X, op=op))
            gl, ex = LG[:, :, 0:4], LG[:, :, 4:ROUT]
            fi4 = C("fi4").unsqueeze(1).broadcast_to([P, NT, 4])
            fi32 = C("fi32").unsqueeze(1).broadcast_to([P, NT, NE])
            red("gm", s8[:, 0, :], gl, ALU.max)
            tt("ge1", g4a[:], gl, bc(s8[:, 0, :], 4), ALU.is_equal)
            tt("ge2", g4a[:], g4a[:], fi4, ALU.mult)
            red("gx", s8[:, 1, :], g4a[:], ALU.max)
            tt("g1h", g4b[:], g4a[:], bc(s8[:, 1, :], 4), ALU.is_equal)
            tt("gs", ra[:, :, 0:4], gl, bc(s8[:, 0, :], 4), ALU.subtract)
            dve.wait_ge(act_did, AC.of("rge"))
            red("gsum", s8[:, 2, :], rb[:, :, 0:4], ALU.add)
            D_("gpen", V_.tensor_scalar(out=g4a[:], in0=g4b[:], scalar1=-1.0, scalar2=1e30, op0=ALU.add,
                                        op1=ALU.mult))
            r48 = lambda x: x.rearrange("p t (g e) -> p t g e", g=4)
            tt("el", r48(el[:]), r48(ex), g4a[:].unsqueeze(3).broadcast_to([P, NT, 4, 8]), ALU.add)
            red("m1", s8[:, 3, :], el[:], ALU.max)
            tt("q1", ra[:], el[:], bc(s8[:, 3, :], NE), ALU.is_equal)
            tt("q1i", ra[:], ra[:], fi32, ALU.mult)
            red("i1", s8[:, 4, :], ra[:], ALU.max)
            tt("o1", oh1[:], ra[:], bc(s8[:, 4, :], NE), ALU.is_equal)
            D_("rb", V_.scalar_tensor_tensor(out=rb[:], in0=oh1[:], scalar=-1e35, in1=el[:], op0=ALU.mult,
                                             op1=ALU.add))
            red("m2", s8[:, 5, :], rb[:], ALU.max)
            tt("q2", rc[:], rb[:], bc(s8[:, 5, :], NE), ALU.is_equal)
            tt("q2i", rc[:], rc[:], fi32, ALU.mult)
            red("i2", s8[:, 6, :], rc[:], ALU.max)
            tt("o2", oh2[:], rc[:], bc(s8[:, 6, :], NE), ALU.is_equal)
            tt("memb", memb[:], oh1[:], oh2[:], ALU.add)
            D_("mb0", V_.tensor_scalar(out=mb[:, 0, :], in0=memb[:, 0, :], scalar1=0.0, scalar2=None, op0=ALU.mult))
            for t in range(1, NT + 1):
                tt(f"mb{t}", mb[:, t, :], mb[:, t - 1, :], memb[:, t - 1, :], ALU.add)
            tt("md", s8[:, 7, :], s8[:, 5, :], s8[:, 3, :], ALU.subtract)
            dve.wait_ge(pe_did, PEV.of("rank"))
            D_("cntb", V_.tensor_copy(out=cntb[:], in_=PS[:, 1, 0:NE]))
            tt("cmp", cmp7[:], cntb[:].unsqueeze(2).broadcast_to([P, NE, 7]),
               C("thr").rearrange("p (e j) -> p e j", j=7), ALU.is_gt)
            red("v", vt[:, 0, :], cmp7[:], ALU.add)
            src = 0
            for k in (1, 2, 4, 8, 16):
                D_(f"s{k}a", V_.tensor_copy(out=vt[:, 1 - src, :], in_=vt[:, src, :]))
                tt(f"s{k}b", vt[:, 1 - src, k:NE], vt[:, 1 - src, k:NE], vt[:, src, 0:NE - k], ALU.add)
                src = 1 - src
            inc = vt[:, src, :]
            red("exc", eb[:], cmp7[:], ALU.add)
            tt("eb", eb[:], inc, eb[:], ALU.subtract)
            D_("ra", V_.tensor_copy(out=ra[:], in_=PS[:, 0, 0:NT * NE].rearrange("p (t e) -> p t e", e=NE)))
            D_("ge", V_.tensor_scalar(out=rb[:], in0=ra[:], scalar1=float(CAP), scalar2=None, op0=ALU.is_ge))
            D_("geb", V_.scalar_tensor_tensor(out=rc[:, 0, :], in0=eb[:], scalar=float(CAP), in1=C("e31"),
                                              op0=ALU.mult, op1=ALU.add))
            tt("rae", rb[:], rb[:], rc[:, 0, :].unsqueeze(1).broadcast_to([P, NT, NE]), ALU.mult)
            tt("rs", ra[:], ra[:], C("ecap").unsqueeze(1).broadcast_to([P, NT, NE]), ALU.add)
            tt("p1", ra[:], ra[:], rb[:], ALU.add)
            tt("sl1", rb[:], ra[:], oh1[:], ALU.mult)
            red("r1", slf[:, 0, :], rb[:], ALU.add)
            tt("sl2", rb[:], ra[:], oh2[:], ALU.mult)
            red("r2", slf[:, 1, :], rb[:], ALU.add)
            D_("slot", V_.tensor_copy(out=slot[:], in_=slf[:]))
            D_("sint", V_.tensor_scalar(out=sint[:], in0=slot[:], scalar1=7, scalar2=None,
                                        op0=ALU.logical_shift_right))
            D_("shi", V_.tensor_copy(out=shi[:], in_=sint[:]))
            D_("slo", V_.scalar_tensor_tensor(out=slo[:], in0=shi[:], scalar=-float(CAP), in1=slf[:],
                                              op0=ALU.mult, op1=ALU.add))
            kt = lambda x, w: x.rearrange("p k t -> p (k t)").unsqueeze(2).broadcast_to([P, 2 * NT, w])
            tt("in_tile", in_tile[:].rearrange("p k t n -> p (k t) n"), kt(shi[:], NTILES),
               C("iota", 0, NTILES).unsqueeze(1).broadcast_to([P, 2 * NT, NTILES]), ALU.is_equal)
            for k in range(2):
                tt(f"in_tok{k}", in_tile[:, k], in_tile[:, k],
                   C("tok").unsqueeze(2).broadcast_to([P, NT, NTILES]), ALU.mult)
            tt("in_row", in_row[:].rearrange("p k t r -> p (k t) r"), kt(slo[:], P),
               C("iota").unsqueeze(1).broadcast_to([P, 2 * NT, P]), ALU.is_equal)
            dve.wait_ge(act_did, AC.of("re2"))
            D_("den0", V_.tensor_scalar(out=s8[:, 0, :], in0=s8[:, 7, :], scalar1=1.0, scalar2=None, op0=ALU.add))
            tt("den", s8[:, 0, :], s8[:, 0, :], s8[:, 2, :], ALU.mult)
            D_("w1", V_.reciprocal(out=w12[:, 0, :], in_=s8[:, 0, :]))
            tt("w2", w12[:, 1, :], w12[:, 0, :], s8[:, 7, :], ALU.mult)
            tt("cj", cj[:], inc.unsqueeze(1).broadcast_to([P, 16, NE]),
               C("jj").unsqueeze(2).broadcast_to([P, 16, NE]), ALU.is_le)
            red("ej", ej[:, 1:17], cj[:], ALU.add)
            D_("ejc", V_.tensor_scalar(out=ej[:, 1:17], in0=ej[:, 1:17], scalar1=float(NE - 1), scalar2=None,
                                       op0=ALU.min))
            D_("nov", V_.tensor_copy(out=ej[:, 0:1], in_=inc[:, NE - 1:NE]))
            D_("info", V_.tensor_copy(out=info[0:1, 0:16], in_=ej[0:1, 0:16]))
            dve.wait_ge(pe_did, PEV.of("idt"))
            D_("ids", V_.tensor_copy(out=ids[:, 0:NTILES], in_=PS[:, 2, 0:NTILES]))

            def m_x(n, p):
                dve.wait_ge(m_tr, n + 3)
                V_.tensor_copy(out=XT[:, p, 4:8, :].rearrange("p k t -> p (k t)"), in_=PS[:, 1, :]).then_inc(m_x1, 1)

            def m_gate(n, p):
                dve.wait_ge(m_e, n + 1)
                chain(V_.tensor_scalar(out=gd[:], in0=ge[:], scalar1=1.0, scalar2=None, op0=ALU.add))
                chain(V_.reciprocal(out=gd[:], in_=gd[:]))
                chain(V_.tensor_tensor(out=gd[:], in0=gd[:], in1=PS[:, 2 + p, 0:DE], op=ALU.mult))
                V_.tensor_tensor(out=act2[:, p, :], in0=gd[:], in1=PS[:, 2 + p, DE:2 * DE], op=ALU.mult)\
                  .then_inc(m_act, 1)

            def m_out(n, p, k):
                dve.wait_ge(m_dn, n + 1)
                dve.wait_ge(y_st[p], 16 * k + 1)
                V_.tensor_copy(out=YO[:, p, 512:D], in_=PS[:, 6, :]).then_inc(m_y1, 1)

            def m_slot(n, p, k, before=True, after=True):
                m_gate(n, p)
                if after:
                    m_x(n + 1, 1 - p)
                if before:
                    m_out(n - 1, 1 - p, k)

            m_x(0, 0)
            m_slot(0, 0, 0, before=False)
            lk.settle()
            with dve.Fori(0, 7) as i:
                lk.loop(i, 12)
                for q in range(1, 5):
                    m_slot(4 * i + q, q % 2, 2 * i + (q - 1) // 2)
            lk.done(7)
            for q in range(1, 4):
                m_slot(28 + q, q % 2, 14 + (q - 1) // 2, after=q < 3)
            m_out(31, 1, 15)
            dve.wait_ge(m_dn, NE)
            dve.wait_ge(y_st[0], 16 * NE // 2 + 1)
            n_ovf = dve.value_load(info[0:1, 0:1], min_val=0, max_val=MAX_OVF)
            with dve.Fori(0, MAX_OVF) as j:
                with dve.If(j < n_ovf):
                    dve.wait_ge(v_pe, 4 * j + 1)
                    V_.tensor_copy(out=XT[:, 0, 4:8, :].rearrange("p k t -> p (k t)"), in_=PS[:, 1, :]).then_inc(v_dve, 1)
                    dve.wait_ge(v_act, 4 * j + 2)
                    V_.tensor_scalar(out=gd[:], in0=ge[:], scalar1=1.0, scalar2=None, op0=ALU.add).then_inc(v_dve, 1)
                    dve.wait_ge(v_dve, 6 * j + 2)
                    V_.reciprocal(out=gd[:], in_=gd[:]).then_inc(v_dve, 1)
                    dve.wait_ge(v_dve, 6 * j + 3)
                    V_.tensor_tensor(out=gd[:], in0=gd[:], in1=PS[:, 2, 0:DE], op=ALU.mult).then_inc(v_dve, 1)
                    dve.wait_ge(v_dve, 6 * j + 4)
                    V_.tensor_tensor(out=act2[:, 0, :], in0=gd[:], in1=PS[:, 2, DE:2 * DE], op=ALU.mult)\
                      .then_inc(v_dve, 1)
                    dve.wait_ge(v_pe, 4 * j + 4)
                    V_.tensor_copy(out=YO[:, 0, 512:D], in_=PS[:, 6, :]).then_inc(v_dve, 1)
            dve.wait_ge(gfin_in, 16)
            dve.wait_ge(k_in[0], 32)
            def k_final(b):
                t0, w = K_BATCH[b]
                dve.wait_ge(rs_done, RS_K + b + 1)
                for t in range(t0, t0 + w):
                    V_.scalar_tensor_tensor(out=y1[:, t, :], in0=x2[:, t, :], scalar=rstd[:, t:t + 1],
                                            in1=gfin[:], op0=ALU.mult, op1=ALU.mult).then_inc(k_out, 1)

            for t in range(NT):
                dve.wait_ge(k_in[t], 32)
                for k, y in enumerate((y1, y2)):
                    V_.scalar_tensor_tensor(out=x2[:, t, :], in0=y[:, t, :], scalar=w12[:, k, t:t + 1],
                                            in1=x2[:, t, :], op0=ALU.mult, op1=ALU.add).then_inc((link, k_acc)[k], 1)
                    if k == 0:
                        dve.wait_ge(link, lk.next())
                if t == 5:
                    k_final(0)
            k_final(1)
            k_final(2)

        @block.tensor
        def _(pe_):
            mm, tp = nc.tensor.matmul, nc.tensor.transpose
            pe_.wait_ge(const_in, 16)
            with pe_.Fori(0, 4) as j:
                for p in range(2):
                    pe_.wait_ge(xn_done, 2 * j + (p + 1))
                    for c in range(2):
                        pe_.wait_ge(a_free, 4 * j + (2 * p + c + 1))
                        for q in range(4):
                            k = 4 * c + q
                            ins = tp(PS[:, 2 * p + c, q * P:(q + 1) * P], xn[:, p, k * P:(k + 1) * P], ident)
                        ins.then_inc(a_tr, 1)
            pe_.wait_ge(a_free, 4 + 16)

            def project(h):
                pe_.wait_ge(wn_split, h + 1)
                n = WN[h]
                wv = [w[:, 0:KC * n].rearrange("p (k n) -> p k n", k=KC) for w in (wnh, wnl)]
                for t in range(NT):
                    pe_.wait_ge(c_free, NT * h + t + 1)
                    o = PS[:, 4 + t % 4, 0:n]
                    for k in range(KC):
                        for x, w in ((hTh, 0), (hTh, 1), (hTl, 0)):
                            ins = mm(o, x[:, k, t * P:(t + 1) * P], wv[w][:, k, :],
                                     start=(k == 0 and x is hTh and w == 0), stop=(k == KC - 1 and x is hTl))
                    ins.then_inc(c_mm, 1)

            def pair_of_groups(j):
                for p in range(2):
                    pe_.wait_ge(b_split, 2 * j + (p + 1))
                    for h in range(2):
                        pe_.wait_ge(b_free, 4 * j + (2 * p + h + 1))
                        for k in range(KC):
                            for w, x in ((wth, hTh), (wth, hTl), (wtl, hTh)):
                                ins = mm(PS[:, 2 * p + h, :], w[:, p, k * P:(k + 1) * P],
                                         x[:, k, h * 512:(h + 1) * 512],
                                         start=(k == 0 and w is wth and x is hTh), stop=(k == KC - 1 and w is wtl))
                        ins.then_inc(b_tr, 1)

            project(0)
            pair_of_groups(0)
            project(1)
            pair_of_groups(1)

            def prefix(o, tri, src, before, w):
                mm(o[:, 0:NT * w], C(tri), src, start=True, stop=False)
                return mm(o[:, 0:NT * w], ones[:], before, start=False, stop=True)

            pe_.wait_ge(tab_in, 16 * 5)
            pe_.wait_ge(dve_did, DV.of(f"lb{NT - 1}"))
            pe_.wait_ge(blk_zero, 5)
            PEV.did("cum", prefix(PS[:, 7, :], "tri", lf[:].rearrange("p t f -> p (t f)"),
                                  lfb[:, 0:NT].rearrange("p t f -> p (t f)"), 4))

            def hidden(kv, n):
                pe_.wait_ge(dve_did, DV.of("b1" + n))
                for c in range(16):
                    ins = mm(PS[:, 4, 0:256], blk[:, c, :], w1[:, kv, c, :], start=(c == 0), stop=(c == 15))
                PEV.did("h" + n, ins)

            def hidden_T(n):
                pe_.wait_ge(dve_did, DV.of("h" + n))
                for c in range(2):
                    ins = tp(PS[:, 5, c * P:(c + 1) * P], ga[:, c * P:(c + 1) * P], ident)
                PEV.did("tr" + n, ins)

            def spread(*ns):
                for n in ns:
                    pe_.wait_ge(dve_did, DV.of(f"dg{n}"))
                    if n >= 2:
                        pe_.wait_ge(act_did, AC.of(f"fx{n - 2}"))
                    PEV.did(f"fx{n}", mm(PS[:, (7, 4)[n % 2], :], ones[:], dg[:, n % 4], start=True, stop=True))

            pair_of_groups(2)
            pe_.wait_ge(w1_in, 16 * 6)
            hidden(0, "k")
            pair_of_groups(3)
            hidden_T("k")
            hidden(1, "v")
            spread(0)
            pair_of_groups(4)
            pe_.wait_ge(act_did, AC.of("hTk"))
            for c in range(2):
                ins = mm(PS[:, 6, 0:P], w2k[:, c, :], hT2[:, c, :], start=(c == 0), stop=(c == 1))
            PEV.did("ok", ins)
            hidden_T("v")
            spread(1, 2)
            pair_of_groups(5)
            pe_.wait_ge(act_did, AC.of("hTv"))
            pe_.wait_ge(dve_did, DV.of("kc2k"))
            for g in range(2):
                for c in range(2):
                    ins = mm(PS[0:HD, 6, g * HD:(g + 1) * HD], hT2[:, c, g * HD:(g + 1) * HD],
                             w2v[:, c, :], start=(c == 0), stop=(c == 1))
            PEV.did("ov", ins)
            spread(3, 4)
            pair_of_groups(6)
            spread(5, 6)
            pair_of_groups(7)
            spread(7)
            pe_.wait_ge(b_free, 4 + 32)
            pe_.wait_ge(act_did, AC.of("fx7"))
            for seg in SEGS:
                kind, g = seg.kind, seg.g

                def scores(s, i):
                    u, t, k0, nk = seg.steps[s]
                    un = 1 if u == "Y" else 0
                    if s == 0 or u == "Y" and seg.steps[s - 1][0] != "Y":
                        pe_.wait_ge(st_in[un], seg.loads * i + (seg.load0 + seg.loads))
                    if u == "C":
                        for q in range(4):
                            for n, kk in enumerate((kc1, kc2)):
                                ins = mm(PS[:, 2 * (s % 2), q * HD:(q + 1) * HD],
                                         qs[0][:, (t + q) * P:(t + q + 1) * P],
                                         kk[:, g * HD:(g + 1) * HD], start=(n == 0), stop=(n == 1))
                        ins.then_inc(s_ready, 1)
                        return
                    ks = (k1[un],) if kind == "diff" else (k1[un], k2[un])
                    for c in range(0, nk, 4):
                        w = min(4, nk - c) * P
                        for n, kk in enumerate(ks):
                            ins = mm(PS[:, 2 * (s % 2) + c // 4, 0:w], qs[un][:, t * P:(t + 1) * P],
                                     kk[:, (k0 + c) * P:(k0 + c) * P + w],
                                     start=(n == 0), stop=(n == len(ks) - 1))
                    ins.then_inc(s_ready, 1)

                def transposes(s, i):
                    u, t, k0, nk = seg.steps[s]
                    pe_.wait_ge(sub_ready, seg.step(i, s))
                    for c in range(seg.chunks[s]):
                        pe_.wait_ge(p_ready, seg.chunk(i, s, c) + 1)
                        if u == "C":
                            apart(pe_)
                        bank = 4 + (sum(seg.chunks[:s]) + c) % 2
                        for q in range(4 if u == "C" else min(4, nk - 4 * c)):
                            w = HD if u == "C" else P
                            ins = tp(PS[0:w, bank, q * P:(q + 1) * P],
                                     sp[:, seg.buf(s), (4 * c + q) * w:(4 * c + q + 1) * w], ident)
                        ins.then_inc(t_ready, 1)

                def values(s, i):
                    u, t, k0, nk = seg.steps[s]
                    pe_.wait_ge(p_ready, seg.chunk(i, s + 1) + 2)
                    b = sum(e < s for e in seg.ends)
                    if s == 0 or s - 1 in seg.ends:
                        pe_.wait_ge(o_free, seg.batch(i, b) + 1)
                    bank = 6 + b % 2
                    if u == "C":
                        for q in range(4):
                            ins = mm(PS[:, bank, q * VW:(q + 1) * VW], pt[0:HD, s % 2, q * P:(q + 1) * P],
                                     vcm[:, g, :], start=True, stop=True)
                        ins.then_inc(pv_done, 1)
                        return
                    if kind == "nsa":
                        vh = V[:, g if u == "X" else 2 + g]
                    elif kind == "fox":
                        vh = V[:, bass.ds(2 * i + (4 + "XY".index(u)), 1)].rearrange("p o t d -> p (o t) d")
                    else:
                        vh = V[:, bass.ds(i + 8, 1)].rearrange("p o t d -> p (o t) d")
                    for q in range(nk):
                        ins = mm(PS[:, bank, (t % 4) * VW:(t % 4 + 1) * VW],
                                 pt[:, s % 2, q * P:(q + 1) * P], vh[:, k0 + q, :],
                                 start=(q == 0), stop=(q == nk - 1))
                    ins.then_inc(pv_done, 1)

                def work(v, i, last):
                    if v == 2:
                        pe_.wait_ge(mx_ready, seg.step(i, 0))
                    if v < seg.L or not last:
                        scores(v % seg.L, i + v // seg.L)
                    s = v - 2
                    if s >= 0 and (s < seg.L or not last):
                        transposes(s % seg.L, i + s // seg.L)
                    if v >= 3:
                        values(v - 3, i)

                seg.run(pe_, work)
            pe_.wait_ge(o_free, 2 + SEGS[3].batch(4, 0))

            def o_transposes(t):
                pe_.wait_ge(o_in[t % 2], 16 * (t // 2 + 1))
                for c in range(2):
                    if c == 1:
                        pe_.wait_ge(o_norm, t + 1)
                    for q in range(4):
                        k = 4 * c + q
                        src = ot[:, t % 2, k * P:(k + 1) * P] if k < 6 else \
                            od[:, t, 2 * k - 12:2 * k - 10, :].rearrange("p h d -> p (h d)")
                        ins = tp(PS[:, c, q * P:(q + 1) * P], src, ident)
                    ins.then_inc(g_tr, 1)

            def h_transposes(t):
                pe_.wait_ge(h_xn, t + 1)
                for c in range(2):
                    for q in range(4):
                        k = 4 * c + q
                        ins = tp(PS[:, 4 + c, q * P:(q + 1) * P], h2[:, t % 2, k * P:(k + 1) * P], ident)
                    ins.then_inc(h_tr, 1)

            def router(t):
                pe_.wait_ge(h_ev, 2 * t + 2)
                pe_.wait_ge(hw_in, 32)
                if t:
                    pe_.wait_ge(h_lg, t)
                for k in range(KC):
                    ins = mm(PS[:, 6, 0:ROUT], h2T[:, k, :], wr[:, k, :], start=(k == 0), stop=(k == KC - 1))
                ins.then_inc(h_mm, 1)

            o_transposes(0)
            pe_.wait_ge(wo_lo, 4)
            for t in range(NT):
                pe_.wait_ge(g_lo, 2 * t + 2)
                for h in range(2):
                    if h and t >= 2:
                        router(t - 2)
                    if t:
                        pe_.wait_ge(x2_done, 2 * (t - 1) + h + 1)
                    for k in range(KC):
                        for x, w in ((oth, woh), (oth, wol), (otl, woh)):
                            ins = mm(PS[:, 2 + h, :], x[:, t % 2, k, :], w[:, k, h * 512:(h + 1) * 512],
                                     start=(k == 0 and x is oth and w is woh), stop=(k == KC - 1 and x is otl))
                    ins.then_inc(g_mm, 1)
                if t + 1 < NT:
                    o_transposes(t + 1)
                if t:
                    h_transposes(t - 1)
            router(NT - 2)
            h_transposes(NT - 1)
            router(NT - 1)
            pe_.wait_ge(dve_did, DV.of(f"mb{NT}"))
            prefix(PS[:, 0, :], "tris", memb[:].rearrange("p t e -> p (t e)"),
                   mb[:, 0:NT].rearrange("p t e -> p (t e)"), NE)
            PEV.did("rank", mm(PS[:, 1, 0:NE], ones[:], mb[:, NT, :], start=True, stop=True))
            pe_.wait_ge(x2_done, 16)
            pe_.wait_ge(dve_did, DV.of("in_row"))
            for k in range(2):
                for t in range(NT):
                    ins = mm(PS[:, 2, 0:NTILES], in_row[:, k, t, :], in_tile[:, k, t, :],
                             start=(k == 0 and t == 0), stop=(k == 1 and t == NT - 1))
            PEV.did("idt", ins)
            pe_.wait_ge(dve_did, DV.of("ids"))

            def m_transposes(n, p, k):
                pe_.wait_ge(xg_in[p], k)
                for c in range(2):
                    for q in range(4):
                        kk = 4 * c + q
                        ins = tp(PS[:, c, q * P:(q + 1) * P], XG[:, p, kk * P:(kk + 1) * P], ident)
                ins.then_inc(m_tr, 1)

            def m_up(n, p, q, k):
                pe_.wait_ge(m_x0, n + 1)
                pe_.wait_ge(m_x1, n + 1)
                pe_.wait_ge(we_in[q], k)
                for c in range(KC):
                    ins = mm(PS[:, 2 + p, :], XT[:, p, c, :], wgu[q][:, c, :], start=(c == 0), stop=(c == KC - 1))
                ins.then_inc(m_gu, 1)

            def m_act_t(n, p):
                pe_.wait_ge(m_act, n + 1)
                for c in range(2):
                    ins = tp(PS[:, 4, c * P:(c + 1) * P], act2[:, p, c * P:(c + 1) * P], ident)
                ins.then_inc(m_ta, 1)

            def m_down(n, p, q):
                pe_.wait_ge(m_aT, n + 1)
                pe_.wait_ge(m_y0, n + 1)
                pe_.wait_ge(m_y1, n + 1)
                for h in range(2):
                    for c in range(2):
                        ins = mm(PS[:, 5 + h, :], aT[:, p, c, :], wdn[q][:, c, h * 512:(h + 1) * 512],
                                 start=(c == 0), stop=(c == 1))
                ins.then_inc(m_dn, 1)

            def m_slot(n, q, kw_, kx, before=True, after=True):
                p = q % 2
                m_up(n, p, q % 4, kw_)
                if before:
                    m_act_t(n - 1, 1 - p)
                if after:
                    m_transposes(n + 1, 1 - p, kx)
                if before:
                    m_down(n - 1, 1 - p, (q - 1) % 4)

            m_transposes(0, 0, 16)
            m_slot(0, 0, 32, 16, before=False)
            with pe_.Fori(0, 7) as i:
                for q in range(1, 5):
                    m_slot(4 * i + q, q, 32 * i + 32 * (1 + q // 4), 32 * i + 16 * ((q + 1) // 2 + 1))
            for q in range(1, 4):
                m_slot(28 + q, q, 32 * 8, 32 * 7 + 16 * ((q + 1) // 2 + 1), after=q < 3)
            m_act_t(31, 1)
            m_down(31, 1, 3)
            pe_.wait_ge(m_y0, NE + 1)
            pe_.wait_ge(m_y1, NE + 1)
            n_ovf = pe_.value_load(info[0:1, 0:1], min_val=0, max_val=MAX_OVF)
            with pe_.Fori(0, MAX_OVF) as j:
                with pe_.If(j < n_ovf):
                    pe_.wait_ge(v_x, 16 * j + 16)
                    for c in range(2):
                        for q in range(4):
                            kk = 4 * c + q
                            ins = tp(PS[:, c, q * P:(q + 1) * P], XG[:, 0, kk * P:(kk + 1) * P], ident)
                    ins.then_inc(v_pe, 1)
                    pe_.wait_ge(v_act, 4 * j + 1)
                    pe_.wait_ge(v_dve, 6 * j + 1)
                    pe_.wait_ge(v_w, 32 * j + 32)
                    for c in range(KC):
                        ins = mm(PS[:, 2, :], XT[:, 0, c, :], wgu[0][:, c, :], start=(c == 0), stop=(c == KC - 1))
                    ins.then_inc(v_pe, 1)
                    pe_.wait_ge(v_dve, 6 * j + 5)
                    for c in range(2):
                        ins = tp(PS[:, 4, c * P:(c + 1) * P], act2[:, 0, c * P:(c + 1) * P], ident)
                    ins.then_inc(v_pe, 1)
                    pe_.wait_ge(v_act, 4 * j + 3)
                    for h in range(2):
                        for c in range(2):
                            ins = mm(PS[:, 5 + h, :], aT[:, 0, c, :], wdn[0][:, c, h * 512:(h + 1) * 512],
                                     start=(c == 0), stop=(c == 1))
                    ins.then_inc(v_pe, 1)


_WIDTHS = (512, 128, 128, 128, 128, 128, 128, 24, 256, 256, 256, 4, 256, 256, 256)
_NAMES = ("q", "kc", "vc", "ks", "vs", "kw", "vw", "gate", "fq", "fk", "fv", "ff", "dq", "dk", "dv")


def slope(h, n):
    return 2.0 ** (-8.0 * (h + 1) / n)


def constants():
    c = np.zeros((P, CONSTS), np.float32)
    p = np.arange(P)[:, None]

    def put(name, v):
        s, e = COL[name]
        c[:, s:e] = np.broadcast_to(np.asarray(v, np.float32).reshape(-1, e - s) if np.ndim(v) else v, (P, e - s))

    put("ident", np.eye(P))
    d = p - np.arange(SEQ)[None] + (SEQ - P)
    put("dist", np.where(d >= 0, -d, NEG))
    d = p - np.arange(640)[None] + 512
    put("distw", np.where((d >= 0) & (d < 512), -d, NEG))
    d = (p[:, :, None] + P * np.arange(NT)[None, :, None]) - (16 * np.arange(64)[None, None] + 31)
    put("distc", np.where(d >= 0, -d, NEG).reshape(P, 512))
    m = np.arange(P)[None]
    put("tri", p <= m)
    put("tris", p < m)
    sc = np.ones((P, 16))
    for h in range(NSA_H):
        sc[HD * (h % 2):HD * (h % 2 + 1), G_QN + h // 2] = HD ** -0.5 / slope(h, NSA_H)
    sc[:, G_QF:G_KS] = HD ** -0.5
    for h in range(DIFF_H):
        sc[HD * (h % 2):HD * (h % 2 + 1), G_QD + h // 2] = 32 ** -0.5 / slope(h, DIFF_H)
    c[:, COL["scale"][0]:COL["scale"][1]] = sc
    put("slopes", [slope(h, NSA_H) for h in range(NSA_H)] + [slope(h, DIFF_H) for h in range(DIFF_H)])
    put("fi4", 4 - np.arange(4))
    put("fi32", NE - np.arange(NE))
    put("tok", p + P * np.arange(8)[None])
    put("iota", np.arange(P))
    put("thr", np.tile(CAP * np.arange(1, 8), NE))
    put("ecap", CAP * np.arange(NE))
    put("jj", np.arange(16))
    put("e31", CAP * (NE - 1 - np.arange(NE)))
    put("eps", EPS)
    put("cvalid", (p + P * np.arange(8)[None]) >= 31)
    return c


def layout(i):
    w = i["w_in"][0]
    at, cols = 0, {}
    for n, k in zip(_NAMES, _WIDTHS):
        cols[n] = w[:, at:at + k]
        at += k
    t = np.concatenate([cols[n] for n in ("kc", "vc", "q", "fq", "ks", "kw", "fk", "dq", "dk")], 1)
    wt = t.reshape(KC, P, 16, P).transpose(2, 1, 0, 3).reshape(16, P, SEQ)
    n0 = np.concatenate([cols["vs"], cols["vw"], cols["fv"][:, :P]], 1)
    n1 = np.concatenate([cols["fv"][:, P:], cols["dv"], cols["gate"], cols["ff"]], 1)
    kp = lambda x: x.reshape(-1, P, x.shape[-1]).transpose(1, 0, 2).reshape(P, -1)
    row = lambda x: np.broadcast_to(x.reshape(1, -1), (P, x.size))
    pe = [i[n][0].reshape(16, P).T for n in ("cmp_k_pe", "cmp_v_pe")]
    wo = i["w_out"][0].reshape(4, 2, P, D).transpose(0, 2, 1, 3).reshape(4, P, 2 * D)
    gu = np.concatenate([i["w_e_gate"][0], i["w_e_up"][0]], 2)
    return {
        "x": i["x"][0], "g_attn": row(i["norm_attn"]), "consts": constants(),
        "gbias": row(np.concatenate([i["b_gate"][0], i["b_fgt"][0]])),
        "rbias": row(np.concatenate([i["b_grp"][0], i["b_exp"][0]])),
        "subln": row(i["diff_subln"]), "lam": row(i["diff_lambda"]),
        "wn0": kp(n0), "wn1": kp(n1), "wt": wt,
        "w2k": kp(i["cmp_k_w2"][0]), "w2v": kp(i["cmp_v_w2"][0]), "pe": np.concatenate(pe, 1),
        "w1": np.stack([kp(i["cmp_k_w1"][0]), kp(i["cmp_v_w1"][0])]),
        "wo": wo, "wr": kp(np.concatenate([i["w_grp"][0], i["w_exp"][0]], 1)), "g_ffn": row(i["norm_ffn"]),
        "wgu": gu.reshape(NE, KC, P, 2 * DE).transpose(0, 2, 1, 3).reshape(NE, P, KC * 2 * DE),
        "wdn": i["w_e_down"][0].reshape(NE, 2, P, D).transpose(0, 2, 1, 3).reshape(NE, P, 2 * D),
        "g_fin": row(i["norm_final"]),
    }


def kernel(**inputs):
    import concourse.bacc as bacc
    from concourse.bass_utils import run_bass_kernel_spmd

    arrays = {k: np.ascontiguousarray(v) for k, v in layout({k: np.asarray(v) for k, v in inputs.items()}).items()}
    nc = bacc.Bacc("TRN2", target_bir_lowering=False, num_devices=1)
    a = {k: nc.dram_tensor("in_" + k, v.shape, mybir.dt.from_np(v.dtype), kind="ExternalInput").ap()
         for k, v in arrays.items()}
    out = nc.dram_tensor("out_0", (SEQ, D), mybir.dt.float32, kind="ExternalOutput").ap()
    program(nc, a, out)
    r = run_bass_kernel_spmd(nc, [{"in_" + k: v for k, v in arrays.items()}], core_ids=[0])
    return r.results[0]["out_0"].reshape(1, SEQ, D)
```

```python
import numpy as np
import concourse.bass as bass
from concourse import mybir
from contextlib import ExitStack

SEQ, D = 1024, 1024
P = 128
NT = SEQ // P
KC = D // P
HD = 64
VW = HD + 1
NSA_H, FOX_H, DIFF_H = 8, 4, 4
NCMP = 63
EPS = 1e-6
NEG = -1e30
LAM_INIT = 0.8 - 0.6
NE, DE = 32, 256
CAP = 128
MAX_OVF = 2 * SEQ // CAP - 1
NTILES = NE + MAX_OVF
NROWS = NTILES * CAP
TCOLS = NTILES + NTILES % 2
ROUT = 36
NGL = 28
WN = (384, 412)
GELU = 2 * (2 / np.pi) ** 0.5
MIN_ARG = -87.0
G_KC, G_QN, G_QF, G_KS, G_KW, G_KF, G_QD, G_KD = 0, 2, 6, 8, 9, 10, 12, 14

_CW = [("ident", P), ("scale", 16), ("eps", 1), ("dist", SEQ), ("distw", 640), ("distc", 512), ("tri", P), ("tris", P),
       ("fi4", 4), ("fi32", 32), ("tok", 8), ("thr", 224), ("ecap", 32), ("jj", 16),
       ("e31", 32), ("iota", P), ("cvalid", 8), ("slopes", 12)]
COL, _o = {}, 0
for _n, _w in _CW:
    COL[_n] = (_o, _o + _w)
    _o += _w
CONSTS = _o
SMALL = COL["eps"][1]


def steps_of(kind):
    full = [(t, 0, t + 1) for t in reversed(range(NT))]
    win = [(t, max(0, t - 4), min(t, 4) + 1) for t in reversed(range(NT))]
    out = [("X", *s) for s in full]
    if kind == "nsa":
        out += [("C", 0, 0, 1), ("C", 4, 0, 1)]
    return out + [("Y", *s) for s in (win if kind == "nsa" else full)]


class Seg:
    LAG = 3

    def __init__(self, kind, g, trips, before):
        self.kind, self.g, self.trips = kind, g, trips
        self.steps = steps_of(kind)
        self.L = len(self.steps)
        self.chunks = [1 if t[0] == "C" else (t[3] + 3) // 4 for t in self.steps]
        self.CH = sum(self.chunks)
        self.ends = [3, 7, 8, 9, 13, 17] if kind == "nsa" else [3, 7, 11, 15]
        self.stores = {"nsa": 1, "fox": 2, "diff": 0}[kind]
        self.loads = 128 if kind == "diff" else 96
        if before is None:
            self.step0 = self.chunk0 = self.batch0 = self.load0 = self.store0 = 0
        else:
            b = before
            self.step0, self.chunk0 = b.step0 + b.trips * b.L, b.chunk0 + b.trips * b.CH
            self.batch0, self.load0 = b.batch0 + b.trips * len(b.ends), b.load0 + b.trips * b.loads
            self.store0 = b.store0 + b.trips * b.stores

    def step(self, i, s):
        return i * self.L + (self.step0 + s + 1)

    def chunk(self, i, s, c=0):
        return i * self.CH + (self.chunk0 + sum(self.chunks[:s]) + c)

    def batch(self, i, b):
        return i * len(self.ends) + (self.batch0 + b)

    def buf(self, s):
        return s % (3 if self.L % 3 == 0 else 4)

    def run(self, eng, work, lk=None, per=0):
        for v in range(self.LAG):
            work(v, 0, False)
        if lk:
            lk.settle()
        with eng.Fori(0, self.trips - 1) as i:
            if lk:
                lk.loop(i, per)
            for v in range(self.LAG, self.LAG + self.L):
                work(v, i, False)
        if lk:
            lk.done(self.trips - 1)
        for v in range(self.LAG, self.LAG + self.L):
            work(v, self.trips - 1, True)
        if lk:
            lk.settle()


class Count:

    def __init__(self, start=0):
        self.base, self.i, self.per, self.k = start, 0, 0, 0

    def loop(self, i, per):
        self.i, self.per, self.k = i, per, 0

    def done(self, trips):
        assert self.k == self.per, (self.k, self.per)
        self.base += trips * self.per
        self.i, self.per, self.k = 0, 0, 0

    def settle(self):
        self.base, self.k = self.base + self.k, 0

    def at(self, k):
        return self.base + k if isinstance(self.i, int) else self.i * self.per + (self.base + k)

    def next(self):
        self.k += 1
        return self.at(self.k)


def program(nc, a, out):
    f32, f32r = mybir.dt.float32, mybir.dt.float32r
    u32, i32 = mybir.dt.uint32, mybir.dt.int32
    ALU, ACT, AX = mybir.AluOpType, mybir.ActivationFunctionType, mybir.AxisListType
    ts = bass.ts
    ctx = ExitStack()
    with ctx:
        BASE = 16512

        def at(name, shape, dt, off):
            return nc.alloc_sbuf_tensor_at(name, shape, dt, offset=BASE + off)

        place = [0]

        def small(name, shape, dt=f32):
            n = 4
            for s in shape[1:]:
                n *= s
            t = at(name, shape, dt, place[0])
            place[0] += (n + 31) // 32 * 32
            return t

        cst = small("cst", [P, CONSTS])

        def C(n, lo=0, hi=None):
            s, e = COL[n]
            return cst[:, s + lo:(e if hi is None else s + hi)]

        ident = C("ident")
        ones = small("ones", [P, P])
        gbias = small("gbias", [P, NGL])
        rbias = small("rbias", [P, ROUT])
        subln = small("subln", [P, HD])
        lam4 = small("lam4", [P, 4, 32])
        GL = small("GL", [P, NT, NGL])
        G24 = small("G24", [P, 24, NT])
        cum = small("cum", [P, NT, 4])
        ssq = small("ssq", [P, 40])
        rstd, nv, nz = (small(n, [P, 40]) for n in ("rstd", "nv", "nz"))
        mx = small("mx", [P, 4, 4])
        r4 = small("r4", [P, 4])
        nlam = small("nlam", [P, 4])
        LG = small("LG", [P, NT, ROUT])
        w12 = small("w12", [P, 2, NT])
        slot = small("slot", [P, 2, NT], u32)
        ids = small("ids", [P, NTILES + 1], u32)
        idc = small("idc", [P, 2], u32)
        info = small("info", [1, 16], i32)
        tmpd = small("tmpd", [P, NT, 20])
        lf, lfb = small("lf", [P, NT, 4]), small("lfb", [P, NT, 4])
        kc1, kc2 = small("kc1", [P, P], f32r), small("kc2", [P, P], f32r)
        vcm = small("vcm", [HD, 2, VW])
        KB = 1024
        assert place[0] <= 21 * KB, place[0]
        ZB, ZC, ZD, ZE = 21 * KB, 85 * KB, 110 * KB, 174 * KB
        END = 229344 - BASE

        hTh = at("hTh", [P, KC, SEQ], f32r, ZB)
        hTl = at("hTl", [P, KC, SEQ], f32r, ZB + 32 * KB)
        V = at("V", [P, 12, NT, VW], f32, ZC)
        wn = at("wn", [P, KC * WN[1]], f32, ZD)
        wnh = at("wnh", [P, KC * WN[1]], f32r, ZD + 13 * KB)
        wnl = at("wnl", [P, KC * WN[1]], f32r, ZD + 26 * KB)
        wst = at("wst", [P, 2, SEQ], f32, ZD + 39 * KB)
        wth = at("wth", [P, 2, SEQ], f32r, ZD + 47 * KB)
        wtl = at("wtl", [P, 2, SEQ], f32r, ZD + 55 * KB)
        thi = at("thi", [P, 2, SEQ], f32r, ZE)
        tlo = at("tlo", [P, 2, SEQ], f32r, ZE + 8 * KB)
        xt = at("xt", [P, NT, D], f32, ZE)
        gbc = at("gbc", [P, D], f32, ZD + 55 * KB)
        xn = at("xn", [P, 2, D], f32, ZD + 47 * KB)
        junk = at("junk", [P, D], f32, ZD + 59 * KB)

        w1 = at("w1", [P, 2, 16, 256], f32, ZD)
        w2k = at("w2k", [P, 2, P], f32, ZD + 32 * KB)
        w2v = at("w2v", [P, 2, HD], f32, ZD + 33 * KB)
        pe = at("pe", [P, 2, 16], f32, ZD + 34 * KB)
        ga = at("ga", [P, 256], f32, ZD + 35 * KB)
        gb = at("gb", [P, 256], f32, ZD + 36 * KB)
        gc = at("gc", [P, 256], f32, ZD + 37 * KB)
        hT2 = at("hT2", [P, 2, P], f32, ZD + 38 * KB)
        blk = at("blk", [P, 16, P], f32, ZE + 16 * KB)
        zh = at("zh", [P, SEQ], f32, ZE + 24 * KB)
        zl = at("zl", [P, SEQ], f32, ZE + 28 * KB)
        dg = at("dg", [P, 4, 512], f32, ZE + 24 * KB)
        qs = [at(f"qs{u}", [P, SEQ], f32r, ZB + 12 * KB * u) for u in range(2)]
        k1 = [at(f"k1{u}", [P, SEQ], f32r, ZB + 12 * KB * u + 4 * KB) for u in range(2)]
        k2 = [at(f"k2{u}", [P, SEQ], f32r, ZB + 12 * KB * u + 8 * KB) for u in range(2)]
        sp = at("sp", [P, 4, SEQ], f32, ZB + 24 * KB)
        pt = at("pt", [P, 2, SEQ], f32, ZB + 40 * KB)
        tabX = at("tabX", [P, SEQ], f32, ZB + 48 * KB)
        tabY = at("tabY", [P, SEQ], f32, ZB + 52 * KB)
        oh = at("oh", [P, 2, NT, HD], f32, ZB + 56 * KB)
        tmp = at("tmp", [P, NT, HD], f32, ZB + 60 * KB)
        FX = at("FX", [P, FOX_H, SEQ], f32, ZD)
        od = at("od", [P, NT, DIFF_H, HD], f32, ZE + 16 * KB)
        ot = at("ot", [P, 2, 6 * P], f32, ZE + 24 * KB)
        zrow = at("zrow", [P, D // 4], f32, ZE + 32 * KB)
        woh = at("woh", [P, KC, D], f32r, ZD)
        wol = at("wol", [P, KC, D], f32r, ZD + 32 * KB)
        wraw = at("wraw", [P, KC, D], f32, ZD + 32 * KB)
        oth = at("oth", [P, 2, KC, P], f32r, ZC)
        otl = at("otl", [P, 2, KC, P], f32r, ZC + 8 * KB)
        x2 = at("x2", [P, NT, D], f32, ZB)
        xr = at("xr", [P, 2, D], f32, ZB + 32 * KB)
        h2 = at("h2", [P, 2, D], f32, ZB + 40 * KB)
        h2T = at("h2T", [P, KC, P], f32, ZB + 48 * KB)
        wr = at("wr", [P, KC, ROUT], f32, ZB + 52 * KB)
        gf = at("gf", [P, D], f32, ZB + 54 * KB)
        junk2 = at("junk2", [P, D], f32, ZB + 58 * KB)
        _io = [0]

        def ri(name, shape, dt=f32):
            n = 4
            for s in shape[1:]:
                n *= s
            t = at(name, shape, dt, ZC + _io[0])
            _io[0] += (n + 31) // 32 * 32
            return t

        ra, rb, rc, rd = (ri(n, [P, NT, NE]) for n in ("ra", "rb", "rc", "rd"))
        onehot, sel = (ri(n, [P, 2, NT, NE]) for n in ("onehot", "sel"))
        memb = ri("memb", [P, NT, NE], f32r)
        trisr, onesr = (ri(n, [P, P], f32r) for n in ("trisr", "onesr"))
        el = ri("el", [P, NT, NE])
        s8 = ri("s8", [P, 8, NT])
        g4a, g4b = ri("g4a", [P, NT, 4]), ri("g4b", [P, NT, 4])
        cntb = ri("cntb", [P, NE])
        cmp7 = ri("cmp7", [P, NE, 7])
        vt = ri("vt", [P, 2, 16 + NE])
        eb = ri("eb", [P, NE])
        cj = ri("cj", [P, 16, NE])
        ej = ri("ej", [P, 17])
        slf, shi, slo = (ri(n, [P, 2, NT]) for n in ("slf", "shi", "slo"))
        sint = ri("sint", [P, 2, NT], u32)
        in_tile = ri("in_tile", [P, 2, NT, TCOLS], f32r)
        in_row = at("in_row", [P, 2, NT, P], f32r, ZE + 24 * KB)
        assert _io[0] <= 25 * KB, _io[0]
        XG = at("XG", [P, 2, D], f32, ZD + 48 * KB)
        YO = at("YO", [P, 2, D], f32, ZD + 56 * KB)
        XT = at("XT", [P, 2, KC, P], f32, ZB + 56 * KB)
        ge = at("ge", [P, DE], f32, ZC)
        gd = at("gd", [P, DE], f32, ZC + KB)
        act2 = at("act2", [P, 2, DE], f32, ZC + 2 * KB)
        aT = at("aT", [P, 2, 2, P], f32, ZC + 4 * KB)
        WOFF = [ZE, ZD, ZD + 24 * KB, ZB + 32 * KB]
        wgu = [at(f"wgu{q}", [P, KC, 2 * DE], f32, o) for q, o in enumerate(WOFF)]
        wdn = [at(f"wdn{q}", [P, 2, D], f32, o + 16 * KB) for q, o in enumerate(WOFF)]
        y1 = at("y1", [P, NT, D], f32, ZD)
        y2 = at("y2", [P, NT, D], f32, ZD + 32 * KB)
        gfin = at("gfin", [P, D], f32, ZC + 12 * KB)
        junk3 = at("junk3", [P, D], f32, ZC + 16 * KB)

        PS = ctx.enter_context(nc.psum_tensor("PS", [P, 8, 512], f32))

        T_d = nc.dram_tensor("T_d", [2, 16, P, SEQ], f32).ap()
        T_r = T_d.rearrange("a g p t -> a (g p) t")
        O_d = nc.dram_tensor("O_d", [SEQ, 6 * P], f32).ap()
        O_v = O_d.rearrange("(t p) c -> p t c", p=P)
        h2_d = nc.dram_tensor("h2_d", [SEQ, D], f32).ap()
        Y_d = nc.dram_tensor("Y_d", [NROWS, D], f32).ap()

        def sem(n):
            return ctx.enter_context(nc.semaphore(n))

        const_in = sem("const_in")
        tab_in = sem("tab_in")
        gbc_in = sem("gbc_in")
        waited = sem("waited")
        rs_ln = sem("rs_ln")
        rs_guess = sem("rs_guess")
        rs_mid = sem("rs_mid")
        rs_done = sem("rs_done")
        dq_done = sem("dq_done")
        x_in = [sem(f"x_in{t}") for t in range(NT)]
        ss_done = sem("ss_done")
        xn_done = sem("xn_done")
        a_tr = sem("a_tr")
        a_hi = sem("a_hi")
        a_free = sem("a_free")
        wn_in = sem("wn_in")
        wn_hi = sem("wn_hi")
        wn_split = sem("wn_split")
        c_mm = sem("c_mm")
        c_free = sem("c_free")
        w_in = [sem(f"w_in{p}") for p in range(2)]
        b_whi = sem("b_whi")
        b_split = sem("b_split")
        b_mm = sem("b_mm")
        b_hi = sem("b_hi")
        b_free = sem("b_free")
        t_st = [sem(f"t_st{p}") for p in range(2)]
        dve_did = sem("dve_did")
        act_did = sem("act_did")
        pe_did = sem("pe_did")
        blk_zero = sem("blk_zero")
        w1_in = sem("w1_in")
        z_in = sem("z_in")
        st_in = [sem(f"st_in{u}") for u in "XY"]
        s_ready = sem("s_ready")
        mx_ready = sem("mx_ready")
        sub_ready = sem("sub_ready")
        t_ready = sem("t_ready")
        p_ready = sem("p_ready")
        pv_done = sem("pv_done")
        o_free = sem("o_free")
        ftab_ready = sem("ftab_ready")
        tab_ready = sem("tab_ready")
        oh_ready = sem("oh_ready")
        oh_st = sem("oh_st")
        o_norm = sem("o_norm")
        link = sem("link")
        yz_st = sem("yz_st")
        wo_in = sem("wo_in")
        wo_hi = sem("wo_hi")
        wo_lo = sem("wo_lo")
        o_in = [sem(f"o_in{p}") for p in range(2)]
        r_in = [sem(f"r_in{p}") for p in range(2)]
        g_tr = sem("g_tr")
        g_hi = sem("g_hi")
        g_lo = sem("g_lo")
        g_mm = sem("g_mm")
        x2_done = sem("x2_done")
        h_ss = sem("h_ss")
        h_xg = sem("h_xg")
        h_xn = sem("h_xn")
        h_tr = sem("h_tr")
        h_ev = sem("h_ev")
        h_mm = sem("h_mm")
        h_lg = sem("h_lg")
        router_in = sem("router_in")
        h_st = [sem(f"h_st{p}") for p in range(2)]
        we_in = [sem(f"we_in{q}") for q in range(4)]
        idx_c = sem("idx_c")
        xg_in = [sem(f"xg_in{p}") for p in range(2)]
        m_tr = sem("m_tr")
        m_x0 = sem("m_x0")
        m_x1 = sem("m_x1")
        m_gu = sem("m_gu")
        m_cl = sem("m_cl")
        m_e = sem("m_e")
        m_act = sem("m_act")
        m_ta = sem("m_ta")
        m_aT = sem("m_aT")
        m_dn = sem("m_dn")
        m_y0 = sem("m_y0")
        m_y1 = sem("m_y1")
        y_st = [sem(f"y_st{p}") for p in range(2)]
        ovf_pe = sem("ovf_pe")
        ovf_act = sem("ovf_act")
        ovf_dve = sem("ovf_dve")
        ovf_pool = sem("ovf_pool")
        ovf_w = sem("ovf_w")
        ovf_x = sem("ovf_x")
        ovf_y = sem("ovf_y")
        k_in = [sem(f"k_in{t}") for t in range(NT)]
        k_acc = sem("k_acc")
        k_ss = sem("k_ss")
        k_out = sem("k_out")
        gfin_in = sem("gfin_in")
        k_st = sem("k_st")

        SEGS = []
        for kind, g, trips in (("nsa", 0, 4), ("nsa", 1, 4), ("fox", 0, 2), ("diff", 0, 4)):
            SEGS.append(Seg(kind, g, trips, SEGS[-1] if SEGS else None))
        NSTEP = {x.kind: x.L for x in SEGS}
        ALL_STEPS = SEGS[3].step(3, 15)
        RS_D, RS_H, RS_K = 2, 3, 11
        A_BATCH = ((0, 2), (2, 6))
        K_BATCH = ((0, 4), (4, 3), (7, 1))

        class Events:

            def __init__(self, s, names):
                self.s, self.names, self.n = s, names, 0

            def of(self, name):
                return self.names.index(name) + 1

            def did(self, name, ins, eng=None):
                assert self.names[self.n] == name, (self.names[self.n], name)
                self.n += 1
                ins.then_inc(self.s, 1)
                if eng is not None:
                    eng.wait_ge(self.s, self.n)

        blk_d, gelu_d = ["z0", "b0", "z1", "b1"], ["q", "u", "uc", "d1", "r", "h"]
        DV = Events(dve_did, ["gl", "gc", "nz", "az", "u", "dm", "rd", "er", "g1", "g24", "gcv", "le", "mn", "lf"]
                    + [f"lb{t}" for t in range(NT)] + ["lamp0", "lamp1", "nlam", "cum"]
                    + [n + "k" for n in blk_d + gelu_d] + [n + "v" for n in blk_d] + ["dg0"]
                    + [n + "v" for n in gelu_d] + ["dg1", "dg2", "kc2k", "dg3", "dg4", "dg5", "dg6", "dg7"]
                    + ["gm", "ge1", "ge2", "gx", "g1h", "gs", "gsum", "gpen", "el", "m1", "q1", "q1i", "i1",
                       "o1", "rb", "m2", "q2", "q2i", "i2", "o2", "memb", "md", "vz",
                       "cntb", "cmp", "v"] + [f"s{k}" for k in (1, 2, 4, 8, 16)]
                    + ["exc", "eb", "ge", "geb", "rae", "rs", "p1", "sl", "r", "slot",
                       "sint", "shi", "slo", "in_tile", "in_tok0", "in_tok1", "in_row0", "in_row1", "den0", "den",
                       "w1", "w2", "ids", "cj", "ej", "ejc", "nov", "info"])
        AC = Events(act_did, ["eg", "ef", "ln", "lam", "sqk", "exk", "hTk", "sqv", "exv", "fx0", "c1k", "hTv",
                              "fx1", "fx2", "c1v", "fx3", "fx4", "fx5", "fx6", "fx7", "trisr", "onesr",
                              "rge", "re2"])
        PEV = Events(pe_did, ["cum", "hk", "trk", "hv", "fx0", "ok", "trv", "fx1", "fx2", "ov", "fx3", "fx4", "fx5",
                              "fx6", "fx7", "cnt", "rank", "idt"])

        def flat(b, n=2):
            return PS[:, b:b + n, :].rearrange("p b c -> p (b c)")

        def apart(eng):
            eng.sem_inc(waited, 1)

        block = ctx.enter_context(nc.Block())

        @block.sync
        def _(sp_):
            sp_.dma_start(xt[:, 0, :], a["x"][0:P, :]).then_inc(x_in[0], 16)
            sp_.dma_start(cst[:, 0:SMALL], a["consts"][:, 0:SMALL]).then_inc(const_in, 16)
            for t in range(1, NT):
                sp_.dma_start(xt[:, t, :], a["x"][t * P:(t + 1) * P, :]).then_inc(x_in[t], 16)
            sp_.dma_start(gbc[:], a["g_attn"]).then_inc(gbc_in, 16)
            sp_.dma_start(wn[:, 0:KC * WN[0]], a["wn0"]).then_inc(wn_in, 16)
            sp_.dma_start(wst[:, 0, :], a["wt"][0]).then_inc(w_in[0], 16)
            sp_.dma_start(wst[:, 1, :], a["wt"][1]).then_inc(w_in[1], 16)
            sp_.dma_start(cst[:, SMALL:CONSTS], a["consts"][:, SMALL:CONSTS]).then_inc(tab_in, 16)
            sp_.dma_start(gbias[:], a["gbias"]).then_inc(tab_in, 16)
            sp_.dma_start(rbias[:], a["rbias"]).then_inc(tab_in, 16)
            sp_.dma_start(subln[:], a["subln"]).then_inc(tab_in, 16)
            sp_.dma_start(lam4[:], a["lam"].rearrange("p (a b) -> p a b", a=4)).then_inc(tab_in, 16)
            sp_.wait_ge(wn_split, 1)
            sp_.dma_start(wn[:, 0:KC * WN[1]], a["wn1"]).then_inc(wn_in, 16)

            def store_t(g, p):
                sp_.wait_ge(b_free, 4 + 2 * g + 2)
                sp_.dma_start(T_d[0, g], thi[:, p, :].bitcast(f32)).then_inc(t_st[p], 16)
                sp_.dma_start(T_d[1, g], tlo[:, p, :].bitcast(f32)).then_inc(t_st[p], 16)

            def pair_of_groups(j):
                for p in range(2):
                    sp_.wait_ge(b_split, 2 * j + (p + 1))
                    sp_.dma_start(wst[:, p, :], a["wt"][2 * j + (p + 2)]).then_inc(w_in[p], 16)
                    store_t(2 * j + p, p)

            def load_z(kv, g):
                for part, z in enumerate((zh, zl)):
                    src = T_d[part, G_KC + kv, g * HD:(g + 1) * HD, :]
                    sp_.dma_start(z[0:HD, :], src).then_inc(z_in, 16)
                    sp_.dma_start(z[HD:P, 0:SEQ - 1], src[:, 1:SEQ]).then_inc(z_in, 16)

            pair_of_groups(0)
            sp_.wait_ge(c_free, 4 + 16)
            sp_.dma_start(w2k[:, :, 0:HD], a["w2k"].rearrange("p (c n) -> p c n", c=2)).then_inc(w1_in, 16)
            sp_.dma_start(w2k[:, :, HD:P], a["w2k"].rearrange("p (c n) -> p c n", c=2)).then_inc(w1_in, 16)
            sp_.dma_start(w2v[:], a["w2v"].rearrange("p (c n) -> p c n", c=2)).then_inc(w1_in, 16)
            sp_.dma_start(pe[:], a["pe"].rearrange("p (v c) -> p v c", v=2)).then_inc(w1_in, 16)
            for kv in range(2):
                sp_.dma_start(w1[:, kv], a["w1"][kv].rearrange("p (c n) -> p c n", c=16)).then_inc(w1_in, 16)
            sp_.wait_ge(t_st[0], 32 + 1)
            sp_.wait_ge(t_st[1], 32 + 1)
            load_z(0, 0)
            pair_of_groups(1)
            sp_.wait_ge(dve_did, DV.of("b0k"))
            load_z(0, 1)
            sp_.wait_ge(dve_did, DV.of("b1k"))
            load_z(1, 0)
            pair_of_groups(2)
            sp_.wait_ge(dve_did, DV.of("b0v"))
            load_z(1, 1)
            with sp_.Fori(3, 7) as j:
                pair_of_groups(j)
            def unit_rows(kind, g, i, u):
                if kind == "nsa":
                    return 64 * i + (G_QN * P + 256 * g), (G_KS, G_KW)[u] * P + 64 * g
                if kind == "fox":
                    return P * i + (G_QF * P + 64 * u), P * i + (G_KF * P + 64 * u)
                return HD * i + (G_QD * P + 32 * u), HD * i + (G_KD * P + 32 * u)

            def load_unit(kind, g, i, u):
                q0, k0 = unit_rows(kind, g, i, u)
                w = 32 if kind == "diff" else HD
                for b, part in enumerate((0, 1, 0, 1) if kind == "diff" else (0, 1)):
                    sp_.dma_start(qs[u][w * b:w * b + w, :].bitcast(f32), T_r[part, bass.ds(q0, w), :])\
                       .then_inc(st_in[u], 16)
                if kind == "diff":
                    for b, part in enumerate((0, 0, 1, 1)):
                        sp_.dma_start(k1[u][w * b:w * b + w, :].bitcast(f32), T_r[part, bass.ds(k0, w), :])\
                           .then_inc(st_in[u], 16)
                else:
                    for part, dst in ((0, k1), (1, k2)):
                        for b in range(2):
                            sp_.dma_start(dst[u][w * b:w * b + w, :].bitcast(f32),
                                          T_r[part, bass.ds(k0, w), :]).then_inc(st_in[u], 16)

            store_t(14, 0)
            sp_.wait_ge(t_st[1], 32 * 7 + 1)
            sp_.wait_ge(b_free, 4 + 32)
            load_unit("nsa", 0, 0, 0)
            store_t(15, 1)
            load_unit("nsa", 0, 0, 1)
            for p in range(2):
                sp_.wait_ge(t_st[p], 32 * 8 + 1)
            sp_.wait_ge(blk_zero, 3)
            for c in range(4):
                sp_.dma_start(Y_d[NE * CAP:, c * (D // 4):(c + 1) * (D // 4)].rearrange("(n p) d -> p n d", p=P),
                              zrow[:].unsqueeze(1).broadcast_to([P, MAX_OVF, D // 4])).then_inc(yz_st, 16)
            sdone, ohd = Count(), Count()

            def pair_io(kind, g, i, nxt):
                xs = 10 if kind == "nsa" else 8
                for k in range(NSTEP[kind]):
                    v = sdone.next()
                    if nxt and k == xs - 1:
                        sp_.wait_ge(s_ready, v)
                        load_unit(*nxt, 0)
                    if nxt and k == NSTEP[kind] - 1:
                        sp_.wait_ge(s_ready, v)
                        load_unit(*nxt, 1)
                for u in range({"nsa": 1, "fox": 2, "diff": 0}[kind]):
                    col = {"nsa": HD * i + 256 * g, "fox": P * i + (512 + HD * u)}[kind]
                    sp_.wait_ge(oh_ready, ohd.next())
                    sp_.dma_start(O_v[:, :, bass.ds(col, HD)], oh[:, u]).then_inc(oh_st, 16)

            for n, seg in enumerate(SEGS):
                kind, g, trips = seg.kind, seg.g, seg.trips
                with sp_.Fori(0, trips - 1) as i:
                    sdone.loop(i, NSTEP[kind])
                    ohd.loop(i, seg.stores)
                    pair_io(kind, g, i, (kind, g, i + 1))
                sdone.done(trips - 1)
                ohd.done(trips - 1)
                nxt = (SEGS[n + 1].kind, SEGS[n + 1].g, 0) if n + 1 < len(SEGS) else None
                pair_io(kind, g, trips - 1, nxt)
                sdone.settle()
                ohd.settle()
                if kind == "fox":
                    sp_.wait_ge(oh_st, 16 * 12 + 1)
                    for p in range(2):
                        sp_.dma_start(ot[:, p, :], O_d[p * P:(p + 1) * P, :]).then_inc(o_in[p], 16)
                if n == 0:
                    for c in range(4):
                        sp_.dma_start(wraw[:, 2 * c:2 * c + 2, :],
                                      a["wo"][c].rearrange("p (k n) -> p k n", k=2)).then_inc(wo_in, 16)

            def load_expert(e, q):
                sp_.dma_start(wgu[q][:], a["wgu"][e].rearrange("p (k n) -> p k n", k=KC)).then_inc(we_in[q], 16)
                sp_.dma_start(wdn[q][:], a["wdn"][e].rearrange("p (k n) -> p k n", k=2)).then_inc(we_in[q], 16)

            sp_.wait_ge(pv_done, ALL_STEPS)
            for p in range(2):
                sp_.dma_start(xr[:, p, :], a["x"][p * P:(p + 1) * P, :]).then_inc(r_in[p], 16)
            sp_.wait_ge(dq_done, 4)
            sp_.dma_start(wr[:], a["wr"].rearrange("p (k n) -> p k n", k=KC)).then_inc(router_in, 16)
            sp_.dma_start(gf[:], a["g_ffn"]).then_inc(router_in, 16)
            sp_.dma_start(wgu[0][:], a["wgu"][0].rearrange("p (k n) -> p k n", k=KC)).then_inc(we_in[0], 16)

            def h2_store(t, p):
                sp_.wait_ge(h_xn, t + 1)
                sp_.dma_start(h2_d[ts(t, P), :], h2[:, p, :]).then_inc(h_st[p], 16)

            with sp_.Fori(0, 3) as j:
                for p in range(2):
                    sp_.wait_ge(g_tr, 4 * j + (2 * p + 2))
                    sp_.dma_start(ot[:, p, :], O_d[ts(2 * j + (p + 2), P), :]).then_inc(o_in[p], 16)
                    sp_.wait_ge(x2_done, 4 * j + (2 * p + 2))
                    sp_.dma_start(xr[:, p, :], a["x"][ts(2 * j + (p + 2), P), :]).then_inc(r_in[p], 16)
                    h2_store(2 * j + p, p)
            for p in range(2):
                h2_store(6 + p, p)
            sp_.wait_ge(g_mm, 16)
            sp_.dma_start(wdn[0][:], a["wdn"][0].rearrange("p (k n) -> p k n", k=2)).then_inc(we_in[0], 16)
            load_expert(1, 1)
            load_expert(2, 2)
            sp_.wait_ge(h_lg, 8)
            load_expert(3, 3)
            sp_.wait_ge(dve_did, DV.of("info"))
            sp_.dma_start(gfin[:], a["g_fin"]).then_inc(gfin_in, 16)
            with sp_.Fori(0, 7) as i:
                for q in range(4):
                    sp_.wait_ge(m_dn, 4 * i + (q + 1))
                    load_expert(4 * i + (q + 4), q)
            sp_.wait_ge(m_dn, NE - 3)
            n_ovf = sp_.value_load(info[0:1, 0:1], min_val=0, max_val=MAX_OVF)
            with sp_.Fori(0, MAX_OVF) as j:
                with sp_.If(j < n_ovf):
                    eid = sp_.value_load(info[0:1, bass.ds(j + 1, 1)], min_val=0, max_val=NE - 1)
                    sp_.wait_ge(ovf_y, 16 * j + 1)
                    sp_.dma_start(wgu[0][:], a["wgu"][eid].rearrange("p (k n) -> p k n", k=KC)).then_inc(ovf_w, 16)
                    sp_.dma_start(wdn[0][:], a["wdn"][eid].rearrange("p (k n) -> p k n", k=2)).then_inc(ovf_w, 16)
            for t in range(NT):
                sp_.wait_ge(k_out, t + 1)
                sp_.dma_start(out[t * P:(t + 1) * P, :], y1[:, t, :]).then_inc(k_st, 16)
            sp_.wait_ge(k_st, 16 * NT)
            for p in range(2):
                sp_.wait_ge(y_st[p], 16 * 16 + 1)

        @block.gpsimd
        def _(pool):
            pool.sem_inc(m_tr, 2)
            nc.gpsimd.memset(ones[:], 1.0).then_inc(blk_zero, 1)
            nc.gpsimd.memset(zrow[:], 0.0).then_inc(blk_zero, 1)
            nc.gpsimd.memset(V[:, :, :, HD:VW], 1.0).then_inc(blk_zero, 1)

            def newton(col, w, n, count):
                y, v, z = (b[:, col:col + w] for b in (rstd, nv, nz))

                def did(ins, k):
                    ins.then_inc(rs_mid, 1)
                    pool.wait_ge(rs_mid, 4 * count + k)
                    apart(pool)

                did(nc.gpsimd.tensor_scalar(out=v, in0=ssq[:, col:col + w], scalar1=1.0 / n, scalar2=EPS,
                                            op0=ALU.mult, op1=ALU.add), 1)
                pool.wait_ge(rs_guess, count + 1)
                apart(pool)
                did(nc.gpsimd.tensor_tensor(out=z, in0=y, in1=y, op=ALU.mult), 2)
                did(nc.gpsimd.tensor_tensor(out=z, in0=z, in1=v, op=ALU.mult), 3)
                did(nc.gpsimd.tensor_scalar(out=z, in0=z, scalar1=-0.5, scalar2=1.5, op0=ALU.mult,
                                            op1=ALU.add), 4)
                nc.gpsimd.tensor_tensor(out=y, in0=y, in1=z, op=ALU.mult).then_inc(rs_done, 1)

            for b, (t, w) in enumerate(A_BATCH):
                pool.wait_ge(ss_done, t + w)
                newton(t, w, D, b)
            for n in range(2):
                pool.wait_ge(wn_hi, n + 1)
                nc.gpsimd.tensor_tensor(out=wnl[:, 0:KC * WN[n]], in0=wn[:, 0:KC * WN[n]],
                                        in1=wnh[:, 0:KC * WN[n]].bitcast(f32), op=ALU.subtract)\
                  .then_inc(wn_split, 1)
            nc.gpsimd.memset(vcm[:], 1.0).then_inc(blk_zero, 1)
            pool.wait_ge(xn_done, NT)
            nc.gpsimd.memset(blk[:], 0.0).then_inc(blk_zero, 1)
            pool.wait_ge(b_free, 4 + 32)
            pool.wait_ge(tab_in, 16 * 5)
            with pool.Fori(0, 2) as i:
                for s, (u, t, _, nk) in enumerate(steps_of("fox")):
                    tab, L = (tabX, tabY)[s % 2], nk * P
                    pool.wait_ge(ftab_ready, 16 * i + (s + 1))
                    apart(pool)
                    nc.gpsimd.affine_select(out=tab[:, L - P:L], in_=tab[:, L - P:L],
                                            compare_op=ALU.is_ge, fill=NEG, base=0, pattern=[[-1, P]],
                                            channel_multiplier=1).then_inc(tab_ready, 1)
            for n, c in enumerate((2, 3, 0, 1)):
                pool.wait_ge(wo_hi, n + 1)
                nc.gpsimd.tensor_tensor(out=wol[:, 2 * c:2 * c + 2, :], in0=wraw[:, 2 * c:2 * c + 2, :],
                                        in1=woh[:, 2 * c:2 * c + 2, :].bitcast(f32), op=ALU.subtract)\
                  .then_inc(wo_lo, 1)

            pool.wait_ge(dq_done, 4)
            newton(8, 32, HD, RS_D)
            for t in range(NT):
                pool.wait_ge(h_ss, t + 1)
                newton(2 + t, 1, D, RS_H + t)
            pool.wait_ge(dve_did, DV.of("ids"))
            for p in range(2):
                pool.wait_ge(h_st[p], 16 * NT // 2)

            with pool.Fori(0, NE // 2) as j:
                for p in range(2):
                    n = 2 * j + p
                    pool.wait_ge(m_tr, n + 1)
                    nc.gpsimd.tensor_copy(out=idc[:, p:p + 1], in_=ids[:, bass.ds(n, 1)]).then_inc(idx_c, 1)
                    pool.wait_ge(idx_c, n + 1)
                    apart(pool)
                    pool.indirect_dma_start(
                        out=XG[:, p, :], out_offset=None, in_=h2_d,
                        in_offset=bass.IndirectOffsetOnAxis(ap=idc[:, p:p + 1], axis=0)).then_inc(xg_in[p], 16)
            pool.wait_ge(m_tr, 2 + NE - 1)
            n_ovf = pool.value_load(info[0:1, 0:1], min_val=0, max_val=MAX_OVF)
            with pool.Fori(0, MAX_OVF) as j:
                with pool.If(j < n_ovf):
                    pool.wait_ge(ovf_y, 16 * j + 1)
                    nc.gpsimd.tensor_copy(out=idc[:, 0:1], in_=ids[:, bass.ds(j + NE, 1)]).then_inc(ovf_pool, 1)
                    pool.wait_ge(ovf_pool, j + 1)
                    apart(pool)
                    pool.indirect_dma_start(
                        out=XG[:, 0, :], out_offset=None, in_=h2_d,
                        in_offset=bass.IndirectOffsetOnAxis(ap=idc[:, 0:1], axis=0)).then_inc(ovf_x, 16)
            for p in range(2):
                pool.wait_ge(y_st[p], 16 * 16 + 1)
            pool.wait_ge(yz_st, 16 * 4)
            pool.wait_ge(ovf_y, 16 * n_ovf + 1)
            apart(pool)
            for t in range(NT):
                for k, dst in enumerate((y1, y2)):
                    pool.indirect_dma_start(
                        out=dst[:, t, :], out_offset=None, in_=Y_d,
                        in_offset=bass.IndirectOffsetOnAxis(ap=slot[:, k, t:t + 1], axis=0))\
                        .then_inc(k_in[t], 16)
            for b, (t, w) in enumerate(K_BATCH):
                pool.wait_ge(k_ss, t + w)
                newton(t, w, D, RS_K + b)

        @block.scalar
        def _(act):
            def copy(o, i, **kw):
                return nc.scalar.activation(o, i, ACT.Identity, **kw)

            def inv_sqrt(col, w, n, count):
                y = rstd[:, col:col + w]
                nc.scalar.activation(y, ssq[:, col:col + w], ACT.Ln, scale=1.0 / n, bias=C("eps")).then_inc(rs_ln, 1)
                act.wait_ge(rs_ln, count + 1)
                nc.scalar.activation(y, y, ACT.Exp, scale=-0.5).then_inc(rs_guess, 1)

            def split_hi(n):
                act.wait_ge(wn_in, 16 * (n + 1))
                copy(wnh[:, 0:KC * WN[n]], wn[:, 0:KC * WN[n]]).then_inc(wn_hi, 1)

            act.sem_inc(c_free, 4)
            act.wait_ge(const_in, 16)
            act.sem_inc(p_ready, 2)
            act.sem_inc(ovf_y, 1)
            for p in range(2):
                act.sem_inc(t_st[p], 1)
                act.sem_inc(y_st[p], 1)
            for b, (t0, w) in enumerate(A_BATCH):
                for t in range(t0, t0 + w):
                    act.wait_ge(x_in[t], 16)
                    if t:
                        act.wait_ge(ss_done, t)
                    nc.scalar.activation(junk[:], xt[:, t, :], ACT.Square, accum_out=ssq[:, t:t + 1])\
                      .then_inc(ss_done, 1)
                act.wait_ge(ss_done, t0 + w)
                inv_sqrt(t0, w, D, b)
            split_hi(0)
            with act.Fori(0, 4) as j:
                for p in range(2):
                    for c in range(2):
                        act.wait_ge(a_tr, 4 * j + (2 * p + c + 1))
                        apart(act)
                        copy(hTh[:, 4 * c:4 * c + 4, ts(2 * j + p, P)],
                             PS[:, 2 * p + c, :].rearrange("p (k t) -> p k t", k=4)).then_inc(a_hi, 1)

            def project_copy(h):
                for t in range(NT):
                    act.wait_ge(c_mm, NT * h + t + 1)
                    b = 4 + t % 4
                    ins = copy(V[:, 6 * h:6 * h + 6, t, 0:HD],
                               PS[:, b, 0:384].rearrange("p (h d) -> p h d", h=6))
                    if h:
                        ins = copy(GL[:, t, :], PS[:, b, 384:412])
                    ins.then_inc(c_free, 1)

            def w_hi(g, p, k):
                act.wait_ge(w_in[p], k)
                copy(wth[:, p, :], wst[:, p, :]).then_inc(b_whi, 1)

            def t_hi(g, p, j):
                act.wait_ge(t_st[p], 32 * j + 1)
                for h in range(2):
                    act.wait_ge(b_mm, 2 * g + (h + 1))
                    apart(act)
                    nc.scalar.activation(thi[:, p, h * 512:(h + 1) * 512], PS[:, 2 * p + h, :], ACT.Identity,
                                         scale=cst[:, bass.ds(g + COL["scale"][0], 1)]).then_inc(b_hi, 1)

            w_hi(0, 0, 16)
            project_copy(0)
            split_hi(1)
            w_hi(1, 1, 16)

            def pair_of_groups(j):
                for p in range(2):
                    t_hi(2 * j + p, p, j)
                    w_hi(2 * j + (p + 2), p, 16 * j + 32)

            pair_of_groups(0)
            project_copy(1)
            act.wait_ge(dve_did, DV.of("gc"))
            AC.did("eg", nc.scalar.activation(G24[:].rearrange("p c t -> p t c"), GL[:, :, 0:24], ACT.Exp,
                                              scale=-1.0))
            act.wait_ge(dve_did, DV.of("az"))
            AC.did("ef", nc.scalar.activation(tmpd[:, :, 4:8], tmpd[:, :, 0:4], ACT.Exp, scale=-1.0))
            act.wait_ge(dve_did, DV.of("u"))
            AC.did("ln", nc.scalar.activation(tmpd[:, :, 16:20], tmpd[:, :, 8:12], ACT.Ln))
            act.wait_ge(dve_did, DV.of("lamp1"))
            AC.did("lam", nc.scalar.activation(nlam[:, 2:4], nlam[:, 0:2], ACT.Exp))

            def gelu_exp(n):
                act.wait_ge(pe_did, PEV.of("h" + n))
                AC.did("sq" + n, nc.scalar.activation(ga[:], PS[:, 4, 0:256], ACT.Square))
                act.wait_ge(dve_did, DV.of("uc" + n))
                AC.did("ex" + n, nc.scalar.activation(gc[:], gb[:], ACT.Exp, scale=-GELU))

            def hidden_T(n):
                act.wait_ge(pe_did, PEV.of("tr" + n))
                AC.did("hT" + n, copy(hT2[:].rearrange("p c m -> p (c m)"), PS[:, 5, 0:256]))

            def spread(*ns):
                for n in ns:
                    act.wait_ge(pe_did, PEV.of(f"fx{n}"))
                    AC.did(f"fx{n}", copy(FX[:, n // 2, (n % 2) * 512:(n % 2) * 512 + 512],
                                          PS[:, (7, 4)[n % 2], :], scale=-1.0))

            pair_of_groups(1)
            pair_of_groups(2)
            gelu_exp("k")
            pair_of_groups(3)
            hidden_T("k")
            gelu_exp("v")
            spread(0)
            pair_of_groups(4)
            act.wait_ge(pe_did, PEV.of("ok"))
            AC.did("c1k", copy(kc1[:], PS[:, 6, 0:P]))
            hidden_T("v")
            spread(1, 2)
            pair_of_groups(5)
            act.wait_ge(pe_did, PEV.of("ov"))
            act.wait_ge(blk_zero, 5)
            AC.did("c1v", copy(vcm[:, :, 0:HD], PS[0:HD, 6, 0:P].rearrange("p (g d) -> p g d", g=2)))
            spread(3, 4)
            pair_of_groups(6)
            spread(5, 6)
            t_hi(14, 0, 7)
            t_hi(15, 1, 7)
            spread(7)

            def exps(seg, s, i):
                u, t, k0, nk = seg.steps[s]
                head = {"nsa": i + 4 * seg.g, "fox": None, "diff": i + NSA_H}[seg.kind]
                sc = lambda n: 1.0 if head is None else C("slopes")[0:n, bass.ds(head, 1)]
                for c in range(seg.chunks[s]):
                    bank = 4 + (sum(seg.chunks[:s]) + c) % 2
                    act.wait_ge(t_ready, seg.chunk(i, s, c) + 1)
                    apart(act)
                    if u == "C":
                        ins = nc.scalar.activation(pt[0:HD, s % 2, 0:512], PS[0:HD, bank, :], ACT.Exp, scale=sc(HD))
                    else:
                        w = min(4, nk - 4 * c) * P
                        ins = nc.scalar.activation(pt[:, s % 2, 4 * c * P:4 * c * P + w], PS[:, bank, 0:w],
                                                   ACT.Exp, scale=sc(P))
                    ins.then_inc(p_ready, 1)

            def fox_table(s, i):
                u, t, _, nk = steps_of("fox")[s]
                copy((tabX, tabY)[s % 2][:, 0:nk * P],
                     FX[:, bass.ds(2 * i + "XY".index(u), 1), 0:nk * P].rearrange("p o k -> p (o k)"),
                     bias=cum[:, t, bass.ds(2 * i + "XY".index(u), 1)]).then_inc(ftab_ready, 1)

            def wo_high(c):
                act.wait_ge(wo_in, 16 * 4)
                copy(woh[:, 2 * c:2 * c + 2, :], wraw[:, 2 * c:2 * c + 2, :]).then_inc(wo_hi, 1)

            act.wait_ge(b_free, 4 + 32)
            for s in range(2):
                fox_table(s, 0)
            for n, seg in enumerate(SEGS):
                def work(v, i, last):
                    if v < 2:
                        return
                    if seg.kind == "fox" and (v < seg.L or not last):
                        act.wait_ge(mx_ready, seg.step(i, v - 2))
                        apart(act)
                        fox_table(v % seg.L, i + v // seg.L)
                    s = v - 2
                    if s < seg.L or not last:
                        exps(seg, s % seg.L, i + s // seg.L)

                seg.run(act, work)
                if n == 1:
                    wo_high(2)
                    wo_high(3)
                if n == 2:
                    wo_high(0)
                    wo_high(1)

            def o_high(t, p, halves=(0, 1)):
                for c in halves:
                    act.wait_ge(g_tr, 2 * t + (c + 1))
                    copy(oth[:, p, 4 * c:4 * c + 4, :].rearrange("p k t -> p (k t)"), PS[:, c, :]).then_inc(g_hi, 1)

            o_high(0, 0, (0,))
            act.wait_ge(dq_done, 4)
            inv_sqrt(8, 32, HD, RS_D)
            o_high(0, 0, (1,))

            def sumsq(t):
                act.wait_ge(x2_done, 2 * t + 2)
                nc.scalar.activation(junk2[:], x2[:, t, :], ACT.Square, accum_out=ssq[:, 2 + t:3 + t])\
                  .then_inc(h_ss, 1)
                act.wait_ge(h_ss, t + 1)
                inv_sqrt(2 + t, 1, D, RS_H + t)

            def hT_copy(t):
                for c in range(2):
                    act.wait_ge(h_tr, 2 * t + c + 1)
                    copy(h2T[:, 4 * c:4 * c + 4, :].rearrange("p k t -> p (k t)"), PS[:, 4 + c, :]).then_inc(h_ev, 1)

            for t in range(NT):
                if t:
                    hT_copy(t - 1)
                if t + 1 < NT:
                    o_high(t + 1, (t + 1) % 2)
                sumsq(t)
            act.wait_ge(g_mm, 2 * NT)
            AC.did("trisr", copy(trisr[:], C("tris")))
            AC.did("onesr", copy(onesr[:], ones[:]))
            act.wait_ge(dve_did, DV.of("gs"))
            AC.did("rge", nc.scalar.activation(rb[:, :, 0:4], ra[:, :, 0:4], ACT.Exp))
            act.wait_ge(dve_did, DV.of("md"))
            AC.did("re2", nc.scalar.activation(s8[:, 7, :], s8[:, 7, :], ACT.Exp))

            def m_x(n, p):
                act.wait_ge(m_tr, n + 3)
                copy(XT[:, p, 0:4, :].rearrange("p k t -> p (k t)"), PS[:, 0, :]).then_inc(m_x0, 1)

            def m_exp(n, p):
                act.wait_ge(m_cl, n + 1)
                nc.scalar.activation(ge[:], ge[:], ACT.Exp, scale=-1.0).then_inc(m_e, 1)

            def m_at(n, p):
                act.wait_ge(m_ta, n + 1)
                copy(aT[:, p].rearrange("p c t -> p (c t)"), PS[:, 4, 0:DE]).then_inc(m_aT, 1)

            def m_out(n, p, k):
                act.wait_ge(m_dn, n + 1)
                act.wait_ge(y_st[p], 16 * k + 1)
                copy(YO[:, p, 0:512], PS[:, 5, :]).then_inc(m_y0, 1)
                act.wait_ge(m_y0, n + 2)
                act.wait_ge(m_y1, n + 2)
                act.dma_start(Y_d[ts(n, P), :], YO[:, p, :]).then_inc(y_st[p], 16)

            def m_slot(n, p, k, before=True, after=True):
                if before:
                    m_at(n - 1, 1 - p)
                m_exp(n, p)
                if after:
                    m_x(n + 1, 1 - p)
                if before:
                    m_out(n - 1, 1 - p, k)

            m_x(0, 0)
            m_slot(0, 0, 0, before=False)
            with act.Fori(0, 7) as i:
                for q in range(1, 5):
                    m_slot(4 * i + q, q % 2, 2 * i + (q - 1) // 2)
            for q in range(1, 4):
                m_slot(28 + q, q % 2, 14 + (q - 1) // 2, after=q < 3)
            m_at(31, 1)
            m_out(31, 1, 15)
            act.wait_ge(m_dn, NE)
            act.wait_ge(yz_st, 16 * 4)
            act.wait_ge(y_st[0], 16 * NE // 2 + 1)
            n_ovf = act.value_load(info[0:1, 0:1], min_val=0, max_val=MAX_OVF)
            with act.Fori(0, MAX_OVF) as j:
                with act.If(j < n_ovf):
                    act.wait_ge(ovf_pe, 4 * j + 1)
                    copy(XT[:, 0, 0:4, :].rearrange("p k t -> p (k t)"), PS[:, 0, :]).then_inc(ovf_act, 1)
                    act.wait_ge(ovf_dve, 7 * j + 2)
                    nc.scalar.activation(ge[:], ge[:], ACT.Exp, scale=-1.0).then_inc(ovf_act, 1)
                    act.wait_ge(ovf_pe, 4 * j + 3)
                    copy(aT[:, 0].rearrange("p c t -> p (c t)"), PS[:, 4, 0:DE]).then_inc(ovf_act, 1)
                    act.wait_ge(ovf_pe, 4 * j + 4)
                    copy(YO[:, 0, 0:512], PS[:, 5, :]).then_inc(ovf_act, 1)
                    act.wait_ge(ovf_act, 4 * j + 4)
                    act.wait_ge(ovf_dve, 7 * j + 7)
                    act.dma_start(Y_d[ts(j + NE, P), :], YO[:, 0, :]).then_inc(ovf_y, 16)
            for b, (t0, w) in enumerate(K_BATCH):
                for t in range(t0, t0 + w):
                    act.wait_ge(k_acc, t + 1)
                    if t:
                        act.wait_ge(k_ss, t)
                    nc.scalar.activation(junk3[:], x2[:, t, :], ACT.Square, accum_out=ssq[:, t:t + 1])\
                      .then_inc(k_ss, 1)
                act.wait_ge(k_ss, t0 + w)
                inv_sqrt(t0, w, D, RS_K + b)

        @block.vector
        def _(dve):
            V_ = nc.vector
            lk = Count()

            def chain(ins):
                v = lk.next()
                ins.then_inc(link, 1)
                dve.wait_ge(link, v)

            dve.sem_inc(a_free, 4)
            dve.sem_inc(b_free, 4)
            dve.sem_inc(o_free, 2)
            dve.sem_inc(oh_st, 1)
            dve.sem_inc(m_y0, 1)
            dve.sem_inc(m_y1, 1)
            dve.wait_ge(gbc_in, 16)
            for t in range(NT + 1):
                if t < NT:
                    dve.wait_ge(rs_done, 1 + sum(t >= x for x, _ in A_BATCH[1:]))
                    if t >= 2:
                        dve.wait_ge(a_tr, 2 * t - 2)
                    V_.scalar_tensor_tensor(out=xn[:, t % 2, :], in0=xt[:, t, :], scalar=rstd[:, t:t + 1],
                                            in1=gbc[:], op0=ALU.mult, op1=ALU.mult).then_inc(xn_done, 1)
                if t:
                    for c in range(2):
                        dve.wait_ge(a_hi, 2 * t - 1 + c)
                        o = (slice(None), slice(4 * c, 4 * c + 4), slice((t - 1) * P, t * P))
                        V_.tensor_tensor(out=hTl[o], in0=PS[:, 2 * ((t - 1) % 2) + c, :].rearrange(
                            "p (k t) -> p k t", k=4), in1=hTh[o].bitcast(f32), op=ALU.subtract).then_inc(a_free, 1)

            def w_lo(g, p):
                dve.wait_ge(b_whi, g + 1)
                V_.tensor_tensor(out=wtl[:, p, :], in0=wst[:, p, :], in1=wth[:, p, :].bitcast(f32),
                                 op=ALU.subtract).then_inc(b_split, 1)

            def t_lo(g, p):
                for h in range(2):
                    dve.wait_ge(b_hi, 2 * g + (h + 1))
                    V_.scalar_tensor_tensor(out=tlo[:, p, h * 512:(h + 1) * 512], in0=PS[:, 2 * p + h, :],
                                            scalar=cst[:, bass.ds(g + COL["scale"][0], 1)],
                                            in1=thi[:, p, h * 512:(h + 1) * 512].bitcast(f32),
                                            op0=ALU.mult, op1=ALU.subtract).then_inc(b_free, 1)

            w_lo(0, 0)
            w_lo(1, 1)

            def pair_of_groups(j):
                for p in range(2):
                    t_lo(2 * j + p, p)
                    w_lo(2 * j + (p + 2), p)

            pair_of_groups(0)
            dve.wait_ge(c_free, 4 + 16)
            dve.wait_ge(tab_in, 16 * 5)
            D_ = lambda n, ins: DV.did(n, ins, dve)
            D_("gl", V_.tensor_tensor(out=GL[:], in0=GL[:], in1=gbias[:].unsqueeze(1).broadcast_to([P, NT, NGL]),
                                      op=ALU.add))
            D_("gc", V_.tensor_scalar(out=GL[:, :, 0:24], in0=GL[:, :, 0:24], scalar1=MIN_ARG, scalar2=None,
                                      op0=ALU.max))
            z = GL[:, :, 24:28]
            td = lambda k: tmpd[:, :, 4 * k:4 * k + 4]
            D_("nz", V_.tensor_scalar(out=td(0), in0=z, scalar1=-1.0, scalar2=None, op0=ALU.mult))
            D_("az", V_.tensor_tensor(out=td(0), in0=td(0), in1=z, op=ALU.max))
            dve.wait_ge(act_did, AC.of("ef"))
            D_("u", V_.tensor_scalar(out=td(2), in0=td(1), scalar1=1.0, scalar2=None, op0=ALU.add))
            D_("dm", V_.tensor_scalar(out=td(3), in0=td(2), scalar1=-1.0, scalar2=1e-30, op0=ALU.add, op1=ALU.max))
            D_("rd", V_.reciprocal(out=td(3), in_=td(3)))
            D_("er", V_.tensor_tensor(out=td(3), in0=td(3), in1=td(1), op=ALU.mult))
            D_("g1", V_.tensor_scalar(out=G24[:], in0=G24[:], scalar1=1.0, scalar2=None, op0=ALU.add))
            D_("g24", V_.reciprocal(out=G24[:], in_=G24[:]))
            g24c = G24[:].rearrange("p (h b) t -> p h b t", b=3)[:, :, 0, :]
            D_("gcv", V_.tensor_tensor(out=g24c, in0=g24c, in1=C("cvalid").unsqueeze(1).broadcast_to([P, NSA_H, NT]),
                                       op=ALU.mult))
            dve.wait_ge(act_did, AC.of("ln"))
            D_("le", V_.tensor_tensor(out=td(3), in0=td(3), in1=td(4), op=ALU.mult))
            D_("mn", V_.tensor_scalar(out=td(0), in0=z, scalar1=0.0, scalar2=None, op0=ALU.min))
            D_("lf", V_.tensor_tensor(out=lf[:], in0=td(0), in1=td(3), op=ALU.subtract))
            D_("lb0", V_.tensor_scalar(out=lfb[:, 0], in0=lf[:, 0], scalar1=0.0, scalar2=None, op0=ALU.mult))
            for t in range(1, NT):
                D_(f"lb{t}", V_.tensor_tensor(out=lfb[:, t], in0=lfb[:, t - 1], in1=lf[:, t - 1], op=ALU.add))
            for k in range(2):
                D_(f"lamp{k}", V_.tensor_tensor_reduce(out=ga[:, 0:32], in0=lam4[:, 2 * k, :],
                                                       in1=lam4[:, 2 * k + 1, :], scale=1.0, scalar=0.0,
                                                       op0=ALU.mult, op1=ALU.add, accum_out=nlam[:, k:k + 1]))
            dve.wait_ge(act_did, AC.of("lam"))
            D_("nlam", V_.scalar_tensor_tensor(out=nlam[:, 0:1], in0=nlam[:, 3:4], scalar=LAM_INIT,
                                               in1=nlam[:, 2:3], op0=ALU.subtract, op1=ALU.subtract))
            pair_of_groups(1)
            dve.wait_ge(pe_did, PEV.of("cum"))
            D_("cum", V_.tensor_copy(out=cum[:].rearrange("p t f -> p (t f)"), in_=PS[:, 7, 0:32]))

            def build_blocks(kv, n):
                for g in range(2):
                    dve.wait_ge(z_in, 64 * (2 * kv + g + 1))
                    D_(f"z{g}" + n, V_.tensor_tensor(out=zh[:, 0:SEQ - 1], in0=zh[:, 0:SEQ - 1],
                                                     in1=zl[:, 0:SEQ - 1], op=ALU.add))
                    zv = zh[:].rearrange("p (m s two) -> p s two m", s=8, two=2)
                    for b in range(2):
                        ins = V_.tensor_tensor(
                            out=blk[:, 8 * b:8 * b + 8, g * HD:g * HD + NCMP], in0=zv[:, :, 0, b:b + NCMP],
                            in1=pe[:, kv, 8 * b:8 * b + 8].unsqueeze(2).broadcast_to([P, 8, NCMP]), op=ALU.add)
                    D_(f"b{g}" + n, ins)

            def gelu(n):
                dve.wait_ge(act_did, AC.of("sq" + n))
                D_("q" + n, V_.tensor_scalar(out=gb[:], in0=ga[:], scalar1=0.044715, scalar2=1.0, op0=ALU.mult,
                                             op1=ALU.add))
                D_("u" + n, V_.tensor_tensor(out=gb[:], in0=gb[:], in1=PS[:, 4, 0:256], op=ALU.mult))
                D_("uc" + n, V_.tensor_scalar(out=gb[:], in0=gb[:], scalar1=MIN_ARG / GELU, scalar2=None,
                                              op0=ALU.max))
                dve.wait_ge(act_did, AC.of("ex" + n))
                D_("d1" + n, V_.tensor_scalar(out=gc[:], in0=gc[:], scalar1=1.0, scalar2=None, op0=ALU.add))
                D_("r" + n, V_.reciprocal(out=gc[:], in_=gc[:]))
                D_("h" + n, V_.tensor_tensor(out=ga[:], in0=gc[:], in1=PS[:, 4, 0:256], op=ALU.mult))

            dve.wait_ge(w1_in, 16 * 6)
            dve.wait_ge(blk_zero, 5)
            build_blocks(0, "k")
            pair_of_groups(2)
            gelu("k")
            dve.wait_ge(pe_did, PEV.of("hk"))
            build_blocks(1, "v")

            def diagonal(*ns):
                for n in ns:
                    f, h = n // 2, n % 2
                    if n >= 4:
                        dve.wait_ge(pe_did, PEV.of(f"fx{n - 4}"))
                    D_(f"dg{n}", V_.tensor_tensor(
                        out=dg[:, n % 4].rearrange("p (t c) -> p t c", t=4),
                        in0=ident.unsqueeze(1).broadcast_to([P, 4, P]),
                        in1=cum[:, 4 * h:4 * h + 4, f].unsqueeze(2).broadcast_to([P, 4, P]), op=ALU.mult))

            diagonal(0)
            pair_of_groups(3)
            gelu("v")
            diagonal(1, 2)
            pair_of_groups(4)
            dve.wait_ge(act_did, AC.of("c1k"))
            D_("kc2k", V_.tensor_tensor(out=kc2[:], in0=PS[:, 6, 0:P], in1=kc1[:].bitcast(f32), op=ALU.subtract))
            diagonal(3, 4)
            pair_of_groups(5)
            diagonal(5, 6)
            pair_of_groups(6)
            diagonal(7)
            t_lo(14, 0)
            t_lo(15, 1)

            def softmax_step(seg, s, i):
                kind = seg.kind
                u, t, k0, nk = seg.steps[s]
                if kind == "fox":
                    dve.wait_ge(tab_ready, 16 * i + (s + 1))
                dve.wait_ge(s_ready, seg.step(i, s))
                apart(dve)
                b, bank = seg.buf(s), 2 * (s % 2)
                if u == "C":
                    sv = sp[:, b, 0:256].rearrange("p (t c) -> p t c", t=4)
                    chain(V_.tensor_tensor(out=sp[:, b, 0:256], in0=PS[:, bank, 0:256],
                                           in1=C("distc", HD * t, HD * t + 256), op=ALU.add))
                    V_.tensor_reduce(out=mx[:, b, :], in_=sv, axis=AX.X, op=ALU.max).then_inc(mx_ready, 1)
                    return
                L = nk * P
                if kind == "fox":
                    tab = (tabX, tabY)[s % 2][:, 0:L]
                elif kind == "nsa" and u == "Y":
                    off = P * (4 - min(t, 4))
                    tab = C("distw", off, off + L)
                else:
                    tab = C("dist", (NT - 1 - t) * P, (NT - 1 - t) * P + L)
                V_.tensor_tensor_reduce(out=sp[:, b, 0:L], in0=flat(bank)[:, 0:L], in1=tab, scale=1.0,
                                        scalar=-3e38, op0=ALU.add, op1=ALU.max,
                                        accum_out=mx[:, b, 0:1]).then_inc(mx_ready, 1)

            def subtract(seg, s, i):
                u, t, k0, nk = seg.steps[s]
                b = seg.buf(s)
                dve.wait_ge(mx_ready, seg.step(i, s))
                if u == "C":
                    apart(dve)
                    sv = sp[:, b, 0:256].rearrange("p (t c) -> p t c", t=4)
                    V_.tensor_tensor(out=sv, in0=sv, in1=mx[:, b, :].unsqueeze(2).broadcast_to([P, 4, HD]),
                                     op=ALU.subtract).then_inc(sub_ready, 1)
                    return
                L = nk * P
                V_.tensor_scalar(out=sp[:, b, 0:L], in0=sp[:, b, 0:L], scalar1=mx[:, b, 0:1],
                                 scalar2=None, op0=ALU.subtract).then_inc(sub_ready, 1)

            def out_batch(seg, i, b):
                kind, g = seg.kind, seg.g
                unit = ("XCY" if kind == "nsa" else "XY")[b // 2]
                if unit == "C":
                    t4 = 4 * (b % 2)
                else:
                    t4 = 4 - 4 * (b % 2)
                bank = 6 + b % 2
                dve.wait_ge(pv_done, seg.step(i, seg.ends[b]))
                o = PS[:, bank, 0:4 * VW].rearrange("p (j c) -> p j c", c=VW)
                chain(V_.reciprocal(out=r4[:].unsqueeze(2), in_=o[:, :, HD:VW]))
                if kind == "nsa":
                    br = "CXY".index(unit)
                    gate = G24[:].rearrange("p c t -> p (c t)")[:, bass.ds(24 * i + (96 * g + 8 * br + t4), 4)]
                    chain(V_.tensor_tensor(out=r4[:], in0=r4[:], in1=gate, op=ALU.mult))
                rb_ = r4[:].unsqueeze(2).broadcast_to([P, 4, HD])
                if kind == "nsa":
                    dst = oh[:, 0, t4:t4 + 4, :]
                    into = dst if unit == "X" else tmp[:, t4:t4 + 4, :]
                else:
                    u = "XY".index(unit)
                    into = oh[:, u, t4:t4 + 4, :] if kind == "fox" else (tmp[:, t4:t4 + 4, :] if u else
                                                                         oh[:, 1, t4:t4 + 4, :])
                V_.tensor_tensor(out=into, in0=o[:, :, 0:HD], in1=rb_, op=ALU.mult).then_inc(o_free, 1)
                dve.wait_ge(o_free, seg.batch(i, b) + 3)
                if kind == "nsa" and unit != "X":
                    chain(V_.tensor_tensor(out=dst, in0=dst, in1=into, op=ALU.add))
                if b == 5 or kind == "fox" and t4 == 0:
                    dve.sem_inc(oh_ready, 1)

            def diff_end(i):
                chain(V_.scalar_tensor_tensor(out=tmp[:], in0=tmp[:], scalar=nlam[:, 0:1], in1=oh[:, 1],
                                              op0=ALU.mult, op1=ALU.add))
                V_.scalar_tensor_tensor(out=od[:, :, bass.ds(i, 1), :].rearrange("p t o d -> p t (o d)"), in0=tmp[:],
                                        scalar=1.0 - LAM_INIT, in1=subln[:].unsqueeze(1).broadcast_to([P, NT, HD]),
                                        op0=ALU.mult, op1=ALU.mult)
                chain(V_.tensor_tensor(out=oh[:, 1], in0=tmp[:], in1=tmp[:], op=ALU.mult))
                V_.tensor_reduce(out=ssq[:, bass.ds(8 * i + 8, 8)], in_=oh[:, 1], axis=AX.X, op=ALU.add)\
                  .then_inc(dq_done, 1)
                dve.wait_ge(dq_done, i + 1)

            for seg in SEGS:
                def work(v, i, last):
                    if v < seg.L or not last:
                        softmax_step(seg, v % seg.L, i + v // seg.L)
                    s = v - 1
                    if s >= 0 and (s < seg.L or not last):
                        subtract(seg, s % seg.L, i + s // seg.L)
                    for b, e in enumerate(seg.ends):
                        if v == min(e + 4, seg.L + 2):
                            if b == 0:
                                dve.wait_ge(oh_st, 16 * seg.stores * i + (16 * seg.store0 + 1))
                            out_batch(seg, i, b)
                    if v == seg.L + 2 and seg.kind == "diff":
                        diff_end(i)

                seg.run(dve, work, lk, {"nsa": 18, "fox": 4, "diff": 6}[seg.kind])

            def o_lo(t, p, halves=(0, 1)):
                for c in halves:
                    dve.wait_ge(g_hi, 2 * t + c + 1)
                    V_.tensor_tensor(out=otl[:, p, 4 * c:4 * c + 4, :].rearrange("p k t -> p (k t)"),
                                     in0=PS[:, c, :],
                                     in1=oth[:, p, 4 * c:4 * c + 4, :].rearrange("p k t -> p (k t)").bitcast(f32),
                                     op=ALU.subtract).then_inc(g_lo, 1)

            o_lo(0, 0, (0,))
            dve.wait_ge(rs_done, RS_D + 1)
            for t in range(NT):
                V_.tensor_tensor(out=od[:, t], in0=od[:, t], in1=rstd[:, 8 + t:40:8].unsqueeze(2)
                                 .broadcast_to([P, 4, HD]), op=ALU.mult).then_inc(o_norm, 1)

            def gained(t, h):
                if t >= 2 and h == 0:
                    dve.wait_ge(h_st[t % 2], 16 * (t // 2))
                dve.wait_ge(x2_done, 2 * t + h + 1)
                V_.tensor_tensor(out=h2[:, t % 2, h * 512:h * 512 + 512], in0=x2[:, t, h * 512:h * 512 + 512],
                                 in1=gf[:, h * 512:h * 512 + 512], op=ALU.mult).then_inc(h_xg, 1)

            def normalise(t):
                dve.wait_ge(rs_done, RS_H + t + 1)
                dve.wait_ge(h_tr, 2 * t + 2)
                V_.tensor_scalar(out=h2[:, t % 2, :], in0=h2[:, t % 2, :], scalar1=rstd[:, 2 + t:3 + t],
                                 scalar2=None, op0=ALU.mult).then_inc(h_xn, 1)

            def logits(t):
                dve.wait_ge(rs_done, RS_H + t + 1)
                dve.wait_ge(h_mm, t + 1)
                V_.scalar_tensor_tensor(out=LG[:, t, :], in0=PS[:, 6, 0:ROUT], scalar=rstd[:, 2 + t:3 + t],
                                        in1=rbias[:], op0=ALU.mult, op1=ALU.add).then_inc(h_lg, 1)

            o_lo(0, 0, (1,))
            dve.wait_ge(router_in, 32)
            for t in range(NT):
                dve.wait_ge(r_in[t % 2], 16 * (t // 2 + 1))
                for h in range(2):
                    dve.wait_ge(g_mm, 2 * t + h + 1)
                    V_.tensor_tensor(out=x2[:, t, h * 512:h * 512 + 512], in0=PS[:, 2 + h, :],
                                     in1=xr[:, t % 2, h * 512:h * 512 + 512], op=ALU.add).then_inc(x2_done, 1)
                    gained(t, h)
                    if h == 0 and t:
                        normalise(t - 1)
                if t + 1 < NT:
                    o_lo(t + 1, (t + 1) % 2)
                if t:
                    logits(t - 1)
            for c in range(2):
                dve.wait_ge(h_tr, 2 * NT - 1 + c)
                if c == 0:
                    dve.wait_ge(h_mm, NT - 1)
                V_.tensor_copy(out=h2T[:, 4 * c:4 * c + 4, :].rearrange("p k t -> p (k t)"),
                               in_=PS[:, 4 + c, :]).then_inc(h_ev, 1)
            normalise(NT - 1)
            logits(NT - 1)
            dve.wait_ge(h_lg, NT)

            bc = lambda x, w: x.unsqueeze(2).broadcast_to([P, NT, w])
            tt = lambda n, o, i0, i1, op: D_(n, V_.tensor_tensor(out=o, in0=i0, in1=i1, op=op))
            red = lambda n, o, i0, op: D_(n, V_.tensor_reduce(out=o, in_=i0, axis=AX.X, op=op))
            gl, ex = LG[:, :, 0:4], LG[:, :, 4:ROUT]
            fi4 = C("fi4").unsqueeze(1).broadcast_to([P, NT, 4])
            fi32 = C("fi32").unsqueeze(1).broadcast_to([P, NT, NE])
            red("gm", s8[:, 0, :], gl, ALU.max)
            tt("ge1", g4a[:], gl, bc(s8[:, 0, :], 4), ALU.is_equal)
            tt("ge2", g4a[:], g4a[:], fi4, ALU.mult)
            red("gx", s8[:, 1, :], g4a[:], ALU.max)
            tt("g1h", g4b[:], g4a[:], bc(s8[:, 1, :], 4), ALU.is_equal)
            tt("gs", ra[:, :, 0:4], gl, bc(s8[:, 0, :], 4), ALU.subtract)
            dve.wait_ge(act_did, AC.of("rge"))
            red("gsum", s8[:, 2, :], rb[:, :, 0:4], ALU.add)
            D_("gpen", V_.tensor_scalar(out=g4a[:], in0=g4b[:], scalar1=-1.0, scalar2=1e30, op0=ALU.add,
                                        op1=ALU.mult))
            r48 = lambda x: x.rearrange("p t (g e) -> p t g e", g=4)
            tt("el", r48(el[:]), r48(ex), g4a[:].unsqueeze(3).broadcast_to([P, NT, 4, 8]), ALU.add)
            red("m1", s8[:, 3, :], el[:], ALU.max)
            tt("q1", ra[:], el[:], bc(s8[:, 3, :], NE), ALU.is_equal)
            tt("q1i", ra[:], ra[:], fi32, ALU.mult)
            red("i1", s8[:, 4, :], ra[:], ALU.max)
            tt("o1", onehot[:, 0], ra[:], bc(s8[:, 4, :], NE), ALU.is_equal)
            D_("rb", V_.scalar_tensor_tensor(out=rb[:], in0=onehot[:, 0], scalar=-1e35, in1=el[:], op0=ALU.mult,
                                             op1=ALU.add))
            red("m2", s8[:, 5, :], rb[:], ALU.max)
            tt("q2", rc[:], rb[:], bc(s8[:, 5, :], NE), ALU.is_equal)
            tt("q2i", rc[:], rc[:], fi32, ALU.mult)
            red("i2", s8[:, 6, :], rc[:], ALU.max)
            tt("o2", onehot[:, 1], rc[:], bc(s8[:, 6, :], NE), ALU.is_equal)
            tt("memb", memb[:], onehot[:, 0], onehot[:, 1], ALU.add)
            tt("md", s8[:, 7, :], s8[:, 5, :], s8[:, 3, :], ALU.subtract)
            D_("vz", V_.memset(vt[:], 0.0))
            dve.wait_ge(pe_did, PEV.of("cnt"))
            D_("cntb", V_.tensor_copy(out=cntb[:], in_=PS[:, 1, 0:NE]))
            tt("cmp", cmp7[:], cntb[:].unsqueeze(2).broadcast_to([P, NE, 7]),
               C("thr").rearrange("p (e j) -> p e j", j=7), ALU.is_gt)
            red("v", vt[:, 0, 16:], cmp7[:], ALU.add)
            src = 0
            for k in (1, 2, 4, 8, 16):
                tt(f"s{k}", vt[:, 1 - src, 16:], vt[:, src, 16:], vt[:, src, 16 - k:16 + NE - k], ALU.add)
                src = 1 - src
            inc = vt[:, src, 16:]
            red("exc", eb[:], cmp7[:], ALU.add)
            tt("eb", eb[:], inc, eb[:], ALU.subtract)
            dve.wait_ge(pe_did, PEV.of("rank"))
            rank = PS[:, 0, 0:NT * NE].rearrange("p (t e) -> p t e", e=NE)
            D_("ge", V_.tensor_scalar(out=rb[:], in0=rank, scalar1=float(CAP), scalar2=None, op0=ALU.is_ge))
            D_("geb", V_.scalar_tensor_tensor(out=rc[:, 0, :], in0=eb[:], scalar=float(CAP), in1=C("e31"),
                                              op0=ALU.mult, op1=ALU.add))
            tt("rae", rb[:], rb[:], rc[:, 0, :].unsqueeze(1).broadcast_to([P, NT, NE]), ALU.mult)
            tt("rs", ra[:], rank, C("ecap").unsqueeze(1).broadcast_to([P, NT, NE]), ALU.add)
            tt("p1", ra[:], ra[:], rb[:], ALU.add)
            tt("sl", sel[:], ra[:].unsqueeze(1).broadcast_to([P, 2, NT, NE]), onehot[:], ALU.mult)
            red("r", slf[:], sel[:], ALU.add)
            D_("slot", V_.tensor_copy(out=slot[:], in_=slf[:]))
            D_("sint", V_.tensor_scalar(out=sint[:], in0=slot[:], scalar1=7, scalar2=None,
                                        op0=ALU.logical_shift_right))
            D_("shi", V_.tensor_copy(out=shi[:], in_=sint[:]))
            D_("slo", V_.scalar_tensor_tensor(out=slo[:], in0=shi[:], scalar=-float(CAP), in1=slf[:],
                                              op0=ALU.mult, op1=ALU.add))
            kt = lambda x, w: x.rearrange("p k t -> p (k t)").unsqueeze(2).broadcast_to([P, 2 * NT, w])
            tt("in_tile", in_tile[:].rearrange("p k t n -> p (k t) n"), kt(shi[:], TCOLS),
               C("iota", 0, TCOLS).unsqueeze(1).broadcast_to([P, 2 * NT, TCOLS]), ALU.is_equal)
            for k in range(2):
                tt(f"in_tok{k}", in_tile[:, k], in_tile[:, k].bitcast(f32),
                   C("tok").unsqueeze(2).broadcast_to([P, NT, TCOLS]), ALU.mult)
            for k in range(2):
                tt(f"in_row{k}", in_row[:, k], slo[:, k].unsqueeze(2).broadcast_to([P, NT, P]),
                   C("iota").unsqueeze(1).broadcast_to([P, NT, P]), ALU.is_equal)
            dve.wait_ge(act_did, AC.of("re2"))
            D_("den0", V_.tensor_scalar(out=s8[:, 0, :], in0=s8[:, 7, :], scalar1=1.0, scalar2=None, op0=ALU.add))
            tt("den", s8[:, 0, :], s8[:, 0, :], s8[:, 2, :], ALU.mult)
            D_("w1", V_.reciprocal(out=w12[:, 0, :], in_=s8[:, 0, :]))
            tt("w2", w12[:, 1, :], w12[:, 0, :], s8[:, 7, :], ALU.mult)
            dve.wait_ge(pe_did, PEV.of("idt"))
            D_("ids", V_.tensor_copy(out=ids[:, 0:NTILES], in_=PS[:, 2, 0:NTILES]))
            tt("cj", cj[:], inc.unsqueeze(1).broadcast_to([P, 16, NE]),
               C("jj").unsqueeze(2).broadcast_to([P, 16, NE]), ALU.is_le)
            red("ej", ej[:, 1:17], cj[:], ALU.add)
            D_("ejc", V_.tensor_scalar(out=ej[:, 1:17], in0=ej[:, 1:17], scalar1=float(NE - 1), scalar2=None,
                                       op0=ALU.min))
            D_("nov", V_.tensor_copy(out=ej[:, 0:1], in_=inc[:, NE - 1:NE]))
            D_("info", V_.tensor_copy(out=info[0:1, 0:16], in_=ej[0:1, 0:16]))

            def m_x(n, p):
                dve.wait_ge(m_tr, n + 3)
                V_.tensor_copy(out=XT[:, p, 4:8, :].rearrange("p k t -> p (k t)"), in_=PS[:, 1, :]).then_inc(m_x1, 1)

            def m_gate(n, p, after):
                dve.wait_ge(m_gu, n + 1)
                V_.tensor_scalar(out=ge[:], in0=PS[:, 2 + p, 0:DE], scalar1=MIN_ARG, scalar2=None,
                                 op0=ALU.max).then_inc(m_cl, 1)
                dve.wait_ge(m_e, n + 1)
                chain(V_.tensor_scalar(out=gd[:], in0=ge[:], scalar1=1.0, scalar2=None, op0=ALU.add))
                chain(V_.reciprocal(out=gd[:], in_=gd[:]))
                if after:
                    m_x(n + 1, 1 - p)
                chain(V_.tensor_tensor(out=gd[:], in0=gd[:], in1=PS[:, 2 + p, 0:DE], op=ALU.mult))
                V_.tensor_tensor(out=act2[:, p, :], in0=gd[:], in1=PS[:, 2 + p, DE:2 * DE], op=ALU.mult)\
                  .then_inc(m_act, 1)

            def m_out(n, p, k):
                dve.wait_ge(m_dn, n + 1)
                dve.wait_ge(y_st[p], 16 * k + 1)
                V_.tensor_copy(out=YO[:, p, 512:D], in_=PS[:, 6, :]).then_inc(m_y1, 1)

            def m_slot(n, p, k, before=True, after=True):
                m_gate(n, p, after)
                if before:
                    m_out(n - 1, 1 - p, k)

            m_x(0, 0)
            m_slot(0, 0, 0, before=False)
            lk.settle()
            with dve.Fori(0, 7) as i:
                lk.loop(i, 12)
                for q in range(1, 5):
                    m_slot(4 * i + q, q % 2, 2 * i + (q - 1) // 2)
            lk.done(7)
            for q in range(1, 4):
                m_slot(28 + q, q % 2, 14 + (q - 1) // 2, after=q < 3)
            m_out(31, 1, 15)
            dve.wait_ge(m_dn, NE)
            dve.wait_ge(y_st[0], 16 * NE // 2 + 1)
            n_ovf = dve.value_load(info[0:1, 0:1], min_val=0, max_val=MAX_OVF)
            with dve.Fori(0, MAX_OVF) as j:
                with dve.If(j < n_ovf):
                    dve.wait_ge(ovf_pe, 4 * j + 1)
                    V_.tensor_copy(out=XT[:, 0, 4:8, :].rearrange("p k t -> p (k t)"), in_=PS[:, 1, :])\
                      .then_inc(ovf_dve, 1)
                    dve.wait_ge(ovf_pe, 4 * j + 2)
                    V_.tensor_scalar(out=ge[:], in0=PS[:, 2, 0:DE], scalar1=MIN_ARG, scalar2=None,
                                     op0=ALU.max).then_inc(ovf_dve, 1)
                    dve.wait_ge(ovf_act, 4 * j + 2)
                    V_.tensor_scalar(out=gd[:], in0=ge[:], scalar1=1.0, scalar2=None, op0=ALU.add).then_inc(ovf_dve, 1)
                    dve.wait_ge(ovf_dve, 7 * j + 3)
                    V_.reciprocal(out=gd[:], in_=gd[:]).then_inc(ovf_dve, 1)
                    dve.wait_ge(ovf_dve, 7 * j + 4)
                    V_.tensor_tensor(out=gd[:], in0=gd[:], in1=PS[:, 2, 0:DE], op=ALU.mult).then_inc(ovf_dve, 1)
                    dve.wait_ge(ovf_dve, 7 * j + 5)
                    V_.tensor_tensor(out=act2[:, 0, :], in0=gd[:], in1=PS[:, 2, DE:2 * DE], op=ALU.mult)\
                      .then_inc(ovf_dve, 1)
                    dve.wait_ge(ovf_pe, 4 * j + 4)
                    V_.tensor_copy(out=YO[:, 0, 512:D], in_=PS[:, 6, :]).then_inc(ovf_dve, 1)
            dve.wait_ge(gfin_in, 16)
            dve.wait_ge(k_in[0], 32)
            def k_final(b):
                t0, w = K_BATCH[b]
                dve.wait_ge(rs_done, RS_K + b + 1)
                for t in range(t0, t0 + w):
                    V_.scalar_tensor_tensor(out=y1[:, t, :], in0=x2[:, t, :], scalar=rstd[:, t:t + 1],
                                            in1=gfin[:], op0=ALU.mult, op1=ALU.mult).then_inc(k_out, 1)

            for t in range(NT):
                dve.wait_ge(k_in[t], 32)
                for k, y in enumerate((y1, y2)):
                    V_.scalar_tensor_tensor(out=x2[:, t, :], in0=y[:, t, :], scalar=w12[:, k, t:t + 1],
                                            in1=x2[:, t, :], op0=ALU.mult, op1=ALU.add).then_inc((link, k_acc)[k], 1)
                    if k == 0:
                        dve.wait_ge(link, lk.next())
                if t == 5:
                    k_final(0)
            k_final(1)
            k_final(2)

        @block.tensor
        def _(pe_):
            mm, tp = nc.tensor.matmul, nc.tensor.transpose
            pe_.wait_ge(const_in, 16)
            with pe_.Fori(0, 4) as j:
                for p in range(2):
                    pe_.wait_ge(xn_done, 2 * j + (p + 1))
                    for c in range(2):
                        pe_.wait_ge(a_free, 4 * j + (2 * p + c + 1))
                        for q in range(4):
                            k = 4 * c + q
                            ins = tp(PS[:, 2 * p + c, q * P:(q + 1) * P], xn[:, p, k * P:(k + 1) * P], ident)
                        ins.then_inc(a_tr, 1)
            pe_.wait_ge(a_free, 4 + 16)

            def project(h):
                pe_.wait_ge(wn_split, h + 1)
                n = WN[h]
                wv = [w[:, 0:KC * n].rearrange("p (k n) -> p k n", k=KC) for w in (wnh, wnl)]
                for t in range(NT):
                    pe_.wait_ge(c_free, NT * h + t + 1)
                    o = PS[:, 4 + t % 4, 0:n]
                    for k in range(KC):
                        for x, w in ((hTh, 0), (hTh, 1), (hTl, 0)):
                            ins = mm(o, x[:, k, t * P:(t + 1) * P], wv[w][:, k, :],
                                     start=(k == 0 and x is hTh and w == 0), stop=(k == KC - 1 and x is hTl))
                    ins.then_inc(c_mm, 1)

            def pair_of_groups(j):
                for p in range(2):
                    pe_.wait_ge(b_split, 2 * j + (p + 1))
                    for h in range(2):
                        pe_.wait_ge(b_free, 4 * j + (2 * p + h + 1))
                        for k in range(KC):
                            for w, x in ((wth, hTh), (wth, hTl), (wtl, hTh)):
                                ins = mm(PS[:, 2 * p + h, :], w[:, p, k * P:(k + 1) * P],
                                         x[:, k, h * 512:(h + 1) * 512],
                                         start=(k == 0 and w is wth and x is hTh), stop=(k == KC - 1 and w is wtl))
                        ins.then_inc(b_mm, 1)

            project(0)
            pair_of_groups(0)
            project(1)
            pair_of_groups(1)

            def prefix(o, tri, src, before, w):
                mm(o[:, 0:NT * w], C(tri), src, start=True, stop=False)
                return mm(o[:, 0:NT * w], ones[:], before, start=False, stop=True)

            pe_.wait_ge(tab_in, 16 * 5)
            pe_.wait_ge(dve_did, DV.of(f"lb{NT - 1}"))
            pe_.wait_ge(blk_zero, 5)
            PEV.did("cum", prefix(PS[:, 7, :], "tri", lf[:].rearrange("p t f -> p (t f)"),
                                  lfb[:, 0:NT].rearrange("p t f -> p (t f)"), 4))

            def hidden(kv, n):
                pe_.wait_ge(dve_did, DV.of("b1" + n))
                for c in range(16):
                    ins = mm(PS[:, 4, 0:256], blk[:, c, :], w1[:, kv, c, :], start=(c == 0), stop=(c == 15))
                PEV.did("h" + n, ins)

            def hidden_T(n):
                pe_.wait_ge(dve_did, DV.of("h" + n))
                for c in range(2):
                    ins = tp(PS[:, 5, c * P:(c + 1) * P], ga[:, c * P:(c + 1) * P], ident)
                PEV.did("tr" + n, ins)

            def spread(*ns):
                for n in ns:
                    pe_.wait_ge(dve_did, DV.of(f"dg{n}"))
                    if n >= 2:
                        pe_.wait_ge(act_did, AC.of(f"fx{n - 2}"))
                    PEV.did(f"fx{n}", mm(PS[:, (7, 4)[n % 2], :], ones[:], dg[:, n % 4], start=True, stop=True))

            pair_of_groups(2)
            pe_.wait_ge(w1_in, 16 * 6)
            hidden(0, "k")
            pair_of_groups(3)
            hidden_T("k")
            hidden(1, "v")
            spread(0)
            pair_of_groups(4)
            pe_.wait_ge(act_did, AC.of("hTk"))
            for c in range(2):
                ins = mm(PS[:, 6, 0:P], w2k[:, c, :], hT2[:, c, :], start=(c == 0), stop=(c == 1))
            PEV.did("ok", ins)
            hidden_T("v")
            spread(1, 2)
            pair_of_groups(5)
            pe_.wait_ge(act_did, AC.of("hTv"))
            pe_.wait_ge(dve_did, DV.of("kc2k"))
            for g in range(2):
                for c in range(2):
                    ins = mm(PS[0:HD, 6, g * HD:(g + 1) * HD], hT2[:, c, g * HD:(g + 1) * HD],
                             w2v[:, c, :], start=(c == 0), stop=(c == 1))
            PEV.did("ov", ins)
            spread(3, 4)
            pair_of_groups(6)
            spread(5, 6)
            pair_of_groups(7)
            spread(7)
            pe_.wait_ge(b_free, 4 + 32)
            pe_.wait_ge(act_did, AC.of("fx7"))
            for seg in SEGS:
                kind, g = seg.kind, seg.g

                def scores(s, i):
                    u, t, k0, nk = seg.steps[s]
                    un = 1 if u == "Y" else 0
                    if s == 0 or u == "Y" and seg.steps[s - 1][0] != "Y":
                        pe_.wait_ge(st_in[un], seg.loads * i + (seg.load0 + seg.loads))
                    if u == "C":
                        for q in range(4):
                            for n, kk in enumerate((kc1, kc2)):
                                ins = mm(PS[:, 2 * (s % 2), q * HD:(q + 1) * HD],
                                         qs[0][:, (t + q) * P:(t + q + 1) * P],
                                         kk[:, g * HD:(g + 1) * HD], start=(n == 0), stop=(n == 1))
                        ins.then_inc(s_ready, 1)
                        return
                    ks = (k1[un],) if kind == "diff" else (k1[un], k2[un])
                    for c in range(0, nk, 4):
                        w = min(4, nk - c) * P
                        for n, kk in enumerate(ks):
                            ins = mm(PS[:, 2 * (s % 2) + c // 4, 0:w], qs[un][:, t * P:(t + 1) * P],
                                     kk[:, (k0 + c) * P:(k0 + c) * P + w],
                                     start=(n == 0), stop=(n == len(ks) - 1))
                    ins.then_inc(s_ready, 1)

                def transposes(s, i):
                    u, t, k0, nk = seg.steps[s]
                    pe_.wait_ge(sub_ready, seg.step(i, s))
                    for c in range(seg.chunks[s]):
                        pe_.wait_ge(p_ready, seg.chunk(i, s, c) + 1)
                        if u == "C":
                            apart(pe_)
                        bank = 4 + (sum(seg.chunks[:s]) + c) % 2
                        for q in range(4 if u == "C" else min(4, nk - 4 * c)):
                            w = HD if u == "C" else P
                            ins = tp(PS[0:w, bank, q * P:(q + 1) * P],
                                     sp[:, seg.buf(s), (4 * c + q) * w:(4 * c + q + 1) * w], ident)
                        ins.then_inc(t_ready, 1)

                def values(s, i):
                    u, t, k0, nk = seg.steps[s]
                    pe_.wait_ge(p_ready, seg.chunk(i, s + 1) + 2)
                    b = sum(e < s for e in seg.ends)
                    if s == 0 or s - 1 in seg.ends:
                        pe_.wait_ge(o_free, seg.batch(i, b) + 1)
                    bank = 6 + b % 2
                    if u == "C":
                        for q in range(4):
                            ins = mm(PS[:, bank, q * VW:(q + 1) * VW], pt[0:HD, s % 2, q * P:(q + 1) * P],
                                     vcm[:, g, :], start=True, stop=True)
                        ins.then_inc(pv_done, 1)
                        return
                    if kind == "nsa":
                        vh = V[:, g if u == "X" else 2 + g]
                    elif kind == "fox":
                        vh = V[:, bass.ds(2 * i + (4 + "XY".index(u)), 1)].rearrange("p o t d -> p (o t) d")
                    else:
                        vh = V[:, bass.ds(i + 8, 1)].rearrange("p o t d -> p (o t) d")
                    for q in range(nk):
                        ins = mm(PS[:, bank, (t % 4) * VW:(t % 4 + 1) * VW],
                                 pt[:, s % 2, q * P:(q + 1) * P], vh[:, k0 + q, :],
                                 start=(q == 0), stop=(q == nk - 1))
                    ins.then_inc(pv_done, 1)

                def work(v, i, last):
                    if v == 2:
                        pe_.wait_ge(mx_ready, seg.step(i, 0))
                    if v < seg.L or not last:
                        scores(v % seg.L, i + v // seg.L)
                    s = v - 2
                    if s >= 0 and (s < seg.L or not last):
                        transposes(s % seg.L, i + s // seg.L)
                    if v >= 3:
                        values(v - 3, i)

                seg.run(pe_, work)
            pe_.wait_ge(o_free, 2 + SEGS[3].batch(4, 0))

            def o_transposes(t, halves=(0, 1)):
                pe_.wait_ge(o_in[t % 2], 16 * (t // 2 + 1))
                for c in halves:
                    if c == 1:
                        pe_.wait_ge(o_norm, t + 1)
                    for q in range(4):
                        k = 4 * c + q
                        src = ot[:, t % 2, k * P:(k + 1) * P] if k < 6 else \
                            od[:, t, 2 * k - 12:2 * k - 10, :].rearrange("p h d -> p (h d)")
                        ins = tp(PS[:, c, q * P:(q + 1) * P], src, ident)
                    ins.then_inc(g_tr, 1)

            def h_transposes(t):
                for c in range(2):
                    pe_.wait_ge(h_xg, 2 * t + c + 1)
                    for q in range(4):
                        k = 4 * c + q
                        ins = tp(PS[:, 4 + c, q * P:(q + 1) * P], h2[:, t % 2, k * P:(k + 1) * P], ident)
                    ins.then_inc(h_tr, 1)

            def router(t):
                pe_.wait_ge(h_ev, 2 * t + 2)
                pe_.wait_ge(router_in, 32)
                if t:
                    pe_.wait_ge(h_lg, t)
                for k in range(KC):
                    ins = mm(PS[:, 6, 0:ROUT], h2T[:, k, :], wr[:, k, :], start=(k == 0), stop=(k == KC - 1))
                ins.then_inc(h_mm, 1)

            def project(t, h, ks):
                for k in ks:
                    for x, w in ((oth, woh), (oth, wol), (otl, woh)):
                        ins = mm(PS[:, 2 + h, :], x[:, t % 2, k, :], w[:, k, h * 512:(h + 1) * 512],
                                 start=(k == 0 and x is oth and w is woh), stop=(k == KC - 1 and x is otl))
                return ins

            o_transposes(0, (0,))
            pe_.wait_ge(wo_lo, 4)
            pe_.wait_ge(g_lo, 1)
            project(0, 0, range(4))
            o_transposes(0, (1,))
            project(0, 1, range(4))
            for t in range(NT):
                pe_.wait_ge(g_lo, 2 * t + 2)
                for h in range(2):
                    if h and t:
                        h_transposes(t - 1)
                    if t:
                        pe_.wait_ge(x2_done, 2 * (t - 1) + h + 1)
                    project(t, h, range(0 if t else 4, KC)).then_inc(g_mm, 1)
                if t + 1 < NT:
                    o_transposes(t + 1)
                if t:
                    router(t - 1)
            h_transposes(NT - 1)
            router(NT - 1)
            pe_.wait_ge(act_did, AC.of("onesr"))
            pe_.wait_ge(dve_did, DV.of("memb"))
            for t in range(NT):
                ins = mm(PS[:, 1, 0:NE], onesr[:], memb[:, t, :], start=(t == 0), stop=(t == NT - 1))
            PEV.did("cnt", ins)
            flat = lambda x: x.rearrange("p t e -> p (t e)")
            mm(PS[:, 0, 0:NT * NE], trisr[:], flat(memb[:]), start=True, stop=False)
            for s in range(1, NT):
                ins = mm(PS[:, 0, s * NE:NT * NE], onesr[:], flat(memb[:, 0:NT - s]), start=False, stop=(s == NT - 1))
            PEV.did("rank", ins)
            pe_.wait_ge(x2_done, 16)
            for k in range(2):
                pe_.wait_ge(dve_did, DV.of(f"in_row{k}"))
                for t in range(NT):
                    ins = mm(PS[:, 2, 0:TCOLS], in_row[:, k, t, :], in_tile[:, k, t, :],
                             start=(k == 0 and t == 0), stop=(k == 1 and t == NT - 1))
            PEV.did("idt", ins)
            pe_.wait_ge(dve_did, DV.of("ids"))

            def m_transposes(n, p, k):
                pe_.wait_ge(xg_in[p], k)
                for c in range(2):
                    for q in range(4):
                        kk = 4 * c + q
                        ins = tp(PS[:, c, q * P:(q + 1) * P], XG[:, p, kk * P:(kk + 1) * P], ident)
                ins.then_inc(m_tr, 1)

            def m_up(n, p, q, k):
                pe_.wait_ge(m_x0, n + 1)
                pe_.wait_ge(m_x1, n + 1)
                pe_.wait_ge(we_in[q], k)
                for c in range(KC):
                    ins = mm(PS[:, 2 + p, :], XT[:, p, c, :], wgu[q][:, c, :], start=(c == 0), stop=(c == KC - 1))
                ins.then_inc(m_gu, 1)

            def m_act_t(n, p):
                pe_.wait_ge(m_act, n + 1)
                for c in range(2):
                    ins = tp(PS[:, 4, c * P:(c + 1) * P], act2[:, p, c * P:(c + 1) * P], ident)
                ins.then_inc(m_ta, 1)

            def m_down(n, p, q):
                pe_.wait_ge(m_aT, n + 1)
                pe_.wait_ge(m_y0, n + 1)
                pe_.wait_ge(m_y1, n + 1)
                for h in range(2):
                    for c in range(2):
                        ins = mm(PS[:, 5 + h, :], aT[:, p, c, :], wdn[q][:, c, h * 512:(h + 1) * 512],
                                 start=(c == 0), stop=(c == 1))
                ins.then_inc(m_dn, 1)

            def m_slot(n, q, kw_, kx, before=True, after=True):
                p = q % 2
                m_up(n, p, q % 4, kw_)
                if before:
                    m_act_t(n - 1, 1 - p)
                if after:
                    m_transposes(n + 1, 1 - p, kx)
                if before:
                    m_down(n - 1, 1 - p, (q - 1) % 4)

            m_transposes(0, 0, 16)
            m_slot(0, 0, 32, 16, before=False)
            with pe_.Fori(0, 7) as i:
                for q in range(1, 5):
                    m_slot(4 * i + q, q, 32 * i + 32 * (1 + q // 4), 32 * i + 16 * ((q + 1) // 2 + 1))
            for q in range(1, 4):
                m_slot(28 + q, q, 32 * 8, 32 * 7 + 16 * ((q + 1) // 2 + 1), after=q < 3)
            m_act_t(31, 1)
            m_down(31, 1, 3)
            pe_.wait_ge(m_y0, NE + 1)
            pe_.wait_ge(m_y1, NE + 1)
            n_ovf = pe_.value_load(info[0:1, 0:1], min_val=0, max_val=MAX_OVF)
            with pe_.Fori(0, MAX_OVF) as j:
                with pe_.If(j < n_ovf):
                    pe_.wait_ge(ovf_x, 16 * j + 16)
                    for c in range(2):
                        for q in range(4):
                            kk = 4 * c + q
                            ins = tp(PS[:, c, q * P:(q + 1) * P], XG[:, 0, kk * P:(kk + 1) * P], ident)
                    ins.then_inc(ovf_pe, 1)
                    pe_.wait_ge(ovf_act, 4 * j + 1)
                    pe_.wait_ge(ovf_dve, 7 * j + 1)
                    pe_.wait_ge(ovf_w, 32 * j + 32)
                    for c in range(KC):
                        ins = mm(PS[:, 2, :], XT[:, 0, c, :], wgu[0][:, c, :], start=(c == 0), stop=(c == KC - 1))
                    ins.then_inc(ovf_pe, 1)
                    pe_.wait_ge(ovf_dve, 7 * j + 6)
                    for c in range(2):
                        ins = tp(PS[:, 4, c * P:(c + 1) * P], act2[:, 0, c * P:(c + 1) * P], ident)
                    ins.then_inc(ovf_pe, 1)
                    pe_.wait_ge(ovf_act, 4 * j + 3)
                    for h in range(2):
                        for c in range(2):
                            ins = mm(PS[:, 5 + h, :], aT[:, 0, c, :], wdn[0][:, c, h * 512:(h + 1) * 512],
                                     start=(c == 0), stop=(c == 1))
                    ins.then_inc(ovf_pe, 1)


_WIDTHS = (512, 128, 128, 128, 128, 128, 128, 24, 256, 256, 256, 4, 256, 256, 256)
_NAMES = ("q", "kc", "vc", "ks", "vs", "kw", "vw", "gate", "fq", "fk", "fv", "ff", "dq", "dk", "dv")


def slope(h, n):
    return 2.0 ** (-8.0 * (h + 1) / n)


def constants():
    c = np.zeros((P, CONSTS), np.float32)
    p = np.arange(P)[:, None]

    def put(name, v):
        s, e = COL[name]
        c[:, s:e] = np.broadcast_to(np.asarray(v, np.float32).reshape(-1, e - s) if np.ndim(v) else v, (P, e - s))

    put("ident", np.eye(P))
    d = p - np.arange(SEQ)[None] + (SEQ - P)
    put("dist", np.where(d >= 0, -d, NEG))
    d = p - np.arange(640)[None] + 512
    put("distw", np.where((d >= 0) & (d < 512), -d, NEG))
    d = (p[:, :, None] + P * np.arange(NT)[None, :, None]) - (16 * np.arange(64)[None, None] + 31)
    put("distc", np.where(d >= 0, -d, NEG).reshape(P, 512))
    m = np.arange(P)[None]
    put("tri", p <= m)
    put("tris", p < m)
    sc = np.ones((P, 16))
    for h in range(NSA_H):
        sc[HD * (h % 2):HD * (h % 2 + 1), G_QN + h // 2] = HD ** -0.5 / slope(h, NSA_H)
    sc[:, G_QF:G_KS] = HD ** -0.5
    for h in range(DIFF_H):
        sc[HD * (h % 2):HD * (h % 2 + 1), G_QD + h // 2] = 32 ** -0.5 / slope(h, DIFF_H)
    c[:, COL["scale"][0]:COL["scale"][1]] = sc
    put("slopes", [slope(h, NSA_H) for h in range(NSA_H)] + [slope(h, DIFF_H) for h in range(DIFF_H)])
    put("fi4", 4 - np.arange(4))
    put("fi32", NE - np.arange(NE))
    put("tok", p + P * np.arange(8)[None])
    put("iota", np.arange(P))
    put("thr", np.tile(CAP * np.arange(1, 8), NE))
    put("ecap", CAP * np.arange(NE))
    put("jj", np.arange(16))
    put("e31", CAP * (NE - 1 - np.arange(NE)))
    put("eps", EPS)
    put("cvalid", (p + P * np.arange(8)[None]) >= 31)
    return c


def layout(i):
    w = i["w_in"][0]
    at, cols = 0, {}
    for n, k in zip(_NAMES, _WIDTHS):
        cols[n] = w[:, at:at + k]
        at += k
    t = np.concatenate([cols[n] for n in ("kc", "vc", "q", "fq", "ks", "kw", "fk", "dq", "dk")], 1)
    wt = t.reshape(KC, P, 16, P).transpose(2, 1, 0, 3).reshape(16, P, SEQ)
    n0 = np.concatenate([cols["vs"], cols["vw"], cols["fv"][:, :P]], 1)
    n1 = np.concatenate([cols["fv"][:, P:], cols["dv"], cols["gate"], cols["ff"]], 1)
    kp = lambda x: x.reshape(-1, P, x.shape[-1]).transpose(1, 0, 2).reshape(P, -1)
    row = lambda x: np.broadcast_to(x.reshape(1, -1), (P, x.size))
    pe = [i[n][0].reshape(16, P).T for n in ("cmp_k_pe", "cmp_v_pe")]
    wo = i["w_out"][0].reshape(4, 2, P, D).transpose(0, 2, 1, 3).reshape(4, P, 2 * D)
    gu = np.concatenate([i["w_e_gate"][0], i["w_e_up"][0]], 2)
    return {
        "x": i["x"][0], "g_attn": row(i["norm_attn"]), "consts": constants(),
        "gbias": row(np.concatenate([i["b_gate"][0], i["b_fgt"][0]])),
        "rbias": row(np.concatenate([i["b_grp"][0], i["b_exp"][0]])),
        "subln": row(i["diff_subln"]), "lam": row(i["diff_lambda"]),
        "wn0": kp(n0), "wn1": kp(n1), "wt": wt,
        "w2k": kp(i["cmp_k_w2"][0]), "w2v": kp(i["cmp_v_w2"][0]), "pe": np.concatenate(pe, 1),
        "w1": np.stack([kp(i["cmp_k_w1"][0]), kp(i["cmp_v_w1"][0])]),
        "wo": wo, "wr": kp(np.concatenate([i["w_grp"][0], i["w_exp"][0]], 1)), "g_ffn": row(i["norm_ffn"]),
        "wgu": gu.reshape(NE, KC, P, 2 * DE).transpose(0, 2, 1, 3).reshape(NE, P, KC * 2 * DE),
        "wdn": i["w_e_down"][0].reshape(NE, 2, P, D).transpose(0, 2, 1, 3).reshape(NE, P, 2 * D),
        "g_fin": row(i["norm_final"]),
    }


def kernel(**inputs):
    import concourse.bacc as bacc
    from concourse.bass_utils import run_bass_kernel_spmd

    arrays = {k: np.ascontiguousarray(v) for k, v in layout({k: np.asarray(v) for k, v in inputs.items()}).items()}
    nc = bacc.Bacc("TRN2", target_bir_lowering=False, num_devices=1)
    a = {k: nc.dram_tensor("in_" + k, v.shape, mybir.dt.from_np(v.dtype), kind="ExternalInput").ap()
         for k, v in arrays.items()}
    out = nc.dram_tensor("out_0", (SEQ, D), mybir.dt.float32, kind="ExternalOutput").ap()
    program(nc, a, out)
    r = run_bass_kernel_spmd(nc, [{"in_" + k: v for k, v in arrays.items()}], core_ids=[0])
    return r.results[0]["out_0"].reshape(1, SEQ, D)
```
